# Optimizing a Trainium2 kernel written in Bass

```python
import jax, jax.numpy as jnp
from jax import lax
import numpy as np

D_MODEL = 1024
BATCH = 1
SEQ = 1024
DEPTH = 1

M_HEADS = 4
M_V_DIM = 128
M_QK_DIM = 64
M_CHUNK = 64
A_HEADS = 8
A_HEAD_DIM = 64
WINDOWS = (128, 512, 2048)
DILATIONS = (1, 4, 16)
ROT_DIM = A_HEAD_DIM // 4
ROPE_THETA = 500000.0
MIX_WIDTH = M_HEADS * M_V_DIM + A_HEADS * A_HEAD_DIM
IN_SPLITS = (M_HEADS * M_QK_DIM, M_HEADS * M_QK_DIM, M_HEADS * M_V_DIM, M_HEADS * M_V_DIM,
             4 * M_HEADS, A_HEADS * A_HEAD_DIM, A_HEADS * A_HEAD_DIM, A_HEADS * A_HEAD_DIM)
IN_COLS = sum(IN_SPLITS)
D_FF = 2816
N_MOD = 9
HALF_STEP = 0.5
EPS = 1e-6
NEG_INF = -1e30


def rms_norm(x, g):
    xf = x.astype(jnp.float32)
    y = xf * lax.rsqrt(jnp.mean(xf * xf, axis=-1, keepdims=True) + EPS)
    return (y * g.astype(jnp.float32)).astype(x.dtype)

def modulate(h, shift, scale):
    return h * (1.0 + scale) + shift

def swiglu(h, w_gu, w_down):
    g, u = jnp.split(h @ w_gu, 2, axis=-1)
    return (jax.nn.silu(g) * u) @ w_down

def partial_rope(t, pos):
    half = ROT_DIM // 2
    inv_freq = ROPE_THETA ** (-2.0 * jnp.arange(half, dtype=jnp.float32) / ROT_DIM)
    ang = pos.astype(jnp.float32)[:, None] * inv_freq[None, :]
    cos, sin = jnp.cos(ang), jnp.sin(ang)
    t1, t2 = t[..., :half], t[..., half:ROT_DIM]
    return jnp.concatenate([t1 * cos - t2 * sin, t2 * cos + t1 * sin, t[..., ROT_DIM:]], axis=-1)

def mlstm_scan(q, k, v, log_i, log_f):
    B, H, S, Dk = q.shape
    Dv = v.shape[-1]
    lc = min(M_CHUNK, S)
    nc = S // lc

    def chunks(t):
        return jnp.moveaxis(t.reshape((B, H, nc, lc) + t.shape[3:]), 2, 0)

    xs = (chunks(q), chunks(k), chunks(v), chunks(log_i), chunks(log_f))
    tril = jnp.tril(jnp.ones((lc, lc), dtype=bool))

    def step(carry, inp):
        C, n, m = carry
        q_c, k_c, v_c, li, lf = inp
        b = jnp.cumsum(lf, axis=-1)
        a_inter = b + m[..., None]
        d = jnp.where(tril, b[..., :, None] - b[..., None, :] + li[..., None, :], NEG_INF)
        m_t = jnp.maximum(a_inter, jnp.max(d, axis=-1))
        w_inter = jnp.exp(a_inter - m_t)
        s = jnp.exp(d - m_t[..., None]) * jnp.einsum('bhtd,bhsd->bhts', q_c, k_c)
        num = (w_inter[..., None] * jnp.einsum('bhvd,bhtd->bhtv', C, q_c)
               + jnp.einsum('bhts,bhsv->bhtv', s, v_c))
        den = w_inter * jnp.einsum('bhd,bhtd->bht', n, q_c) + jnp.sum(s, axis=-1)
        h = num / jnp.maximum(jnp.abs(den), jnp.exp(-m_t))[..., None]
        b_end = b[..., -1]
        g = b_end[..., None] - b + li
        m_new = jnp.maximum(b_end + m, jnp.max(g, axis=-1))
        decay = jnp.exp(b_end + m - m_new)
        wg = jnp.exp(g - m_new[..., None])
        C_new = decay[..., None, None] * C + jnp.einsum('bhs,bhsv,bhsd->bhvd', wg, v_c, k_c)
        n_new = decay[..., None] * n + jnp.einsum('bhs,bhsd->bhd', wg, k_c)
        return (C_new, n_new, m_new), h

    init = (jnp.zeros((B, H, Dv, Dk), jnp.float32), jnp.zeros((B, H, Dk), jnp.float32),
            jnp.full((B, H), NEG_INF, jnp.float32))
    _, hs = lax.scan(step, init, xs)
    return jnp.moveaxis(hs, 0, 2).reshape(B, H, S, Dv)

def bidirectional_mlstm(q, k, v, li_f, lf_f, li_b, lf_b):
    h_fwd = mlstm_scan(q, k, v, li_f, lf_f)
    flip = lambda t: jnp.flip(t, axis=2)
    h_bwd = flip(mlstm_scan(flip(q), flip(k), flip(v), flip(li_b), flip(lf_b)))
    return h_fwd + h_bwd

def dilated_band_attention(q, k, v, dilation, n_side):
    B, H, S, Dh = q.shape
    L = S // dilation

    def to_sub(t):
        return t.reshape(B, H, L, dilation, Dh).transpose(0, 1, 3, 2, 4)

    blk = n_side
    nb = -(-L // blk)
    lp = nb * blk
    qs = jnp.pad(to_sub(q), ((0, 0),) * 3 + ((0, lp - L), (0, 0)))
    kpad = ((0, 0),) * 3 + ((n_side, lp - L + n_side), (0, 0))
    ks = jnp.pad(to_sub(k), kpad)
    vs = jnp.pad(to_sub(v), kpad)
    qb = qs.reshape(B, H, dilation, nb, blk, Dh)

    def windows(t):
        tb = t.reshape(B, H, dilation, nb + 2, blk, Dh)
        return jnp.concatenate([tb[:, :, :, :-2], tb[:, :, :, 1:-1], tb[:, :, :, 2:]], axis=4)

    kw, vw = windows(ks), windows(vs)
    s = jnp.einsum('bhrnqe,bhrnke->bhrnqk', qb, kw)
    qi = jnp.arange(blk)[:, None]
    kk = jnp.arange(3 * blk)[None, :]
    band = jnp.abs(kk - n_side - qi) <= n_side
    key_idx = jnp.arange(nb)[:, None] * blk + kk - n_side
    in_range = (key_idx >= 0) & (key_idx < L)
    mask = band[None, :, :] & in_range[:, None, :]
    s = jnp.where(mask, s, NEG_INF)
    m = jnp.max(s, axis=-1, keepdims=True)
    p = jnp.exp(s - m)
    den = jnp.sum(p, axis=-1)
    o = jnp.einsum('bhrnqk,bhrnke->bhrnqe', p, vw) / den[..., None]
    lse = m[..., 0] + jnp.log(den)
    o = o.reshape(B, H, dilation, lp, Dh)[:, :, :, :L].transpose(0, 1, 3, 2, 4).reshape(B, H, S, Dh)
    lse = lse.reshape(B, H, dilation, lp)[..., :L].transpose(0, 1, 3, 2).reshape(B, H, S)
    return o, lse

def dilated_attention(q, k, v):
    outs, lses = [], []
    for w, d in zip(WINDOWS, DILATIONS):
        o, l = dilated_band_attention(q, k, v, d, w // (2 * d))
        outs.append(o)
        lses.append(l)
    wts = jax.nn.softmax(jnp.stack(lses), axis=0)
    return jnp.sum(wts[..., None] * jnp.stack(outs), axis=0)

def hybrid_mixer(h, w_in, gate_bias, g_q, g_k, g_mh, w_out):
    B, S, _ = h.shape
    proj = (h @ w_in).astype(jnp.float32)
    idx, acc = [], 0
    for n_cols in IN_SPLITS[:-1]:
        acc += n_cols
        idx.append(acc)
    mq, mk, mv, mo, mg, aq, ak, av = jnp.split(proj, idx, axis=-1)

    def heads(t, n):
        return t.reshape(B, S, n, -1).transpose(0, 2, 1, 3)

    gates = mg.reshape(B, S, 4, M_HEADS).transpose(2, 0, 3, 1) + gate_bias.astype(jnp.float32)[:, None, :, None]
    hm = bidirectional_mlstm(heads(mq, M_HEADS), heads(mk, M_HEADS) * (M_QK_DIM ** -0.5), heads(mv, M_HEADS),
                             gates[0], jax.nn.log_sigmoid(gates[1]), gates[2], jax.nn.log_sigmoid(gates[3]))
    hm = rms_norm(hm.transpose(0, 2, 1, 3), g_mh.reshape(M_HEADS, M_V_DIM))
    hm = (hm * jax.nn.sigmoid(mo.reshape(B, S, M_HEADS, M_V_DIM))).reshape(B, S, M_HEADS * M_V_DIM)

    pos = jnp.arange(S)
    qa = partial_rope(rms_norm(heads(aq, A_HEADS), g_q), pos) * (A_HEAD_DIM ** -0.5)
    ka = partial_rope(rms_norm(heads(ak, A_HEADS), g_k), pos)
    ha = dilated_attention(qa, ka, heads(av, A_HEADS))
    ha = ha.transpose(0, 2, 1, 3).reshape(B, S, A_HEADS * A_HEAD_DIM)

    return jnp.concatenate([hm, ha], axis=-1).astype(h.dtype) @ w_out

def first_inputs(seed: int = 0) -> dict:
    key = jax.random.key(seed)
    ks = jax.random.split(key, 20)
    f32 = jnp.float32

    def nrm(k, shape, scale):
        return jax.random.normal(k, shape, f32) * scale

    gate_bias = (nrm(ks[9], (DEPTH, 4, M_HEADS), 0.1)
                 + jnp.array([0.0, 1.0, 0.0, 1.0], f32)[None, :, None]
                 * jnp.linspace(3.0, 6.0, M_HEADS, dtype=f32)[None, None, :])
    return {
        'x': nrm(ks[0], (BATCH, SEQ, D_MODEL), 1.0),
        'c': nrm(ks[1], (BATCH, D_MODEL), 1.0),
        'w_ada': nrm(ks[2], (DEPTH, D_MODEL, N_MOD * D_MODEL), 0.5 * D_MODEL ** -0.5),
        'b_ada': nrm(ks[3], (DEPTH, N_MOD * D_MODEL), 0.02),
        'g_ffn1': 1.0 + nrm(ks[4], (DEPTH, D_MODEL), 0.02),
        'w_gu1': nrm(ks[5], (DEPTH, D_MODEL, 2 * D_FF), D_MODEL ** -0.5),
        'w_down1': nrm(ks[6], (DEPTH, D_FF, D_MODEL), D_FF ** -0.5),
        'g_mix': 1.0 + nrm(ks[7], (DEPTH, D_MODEL), 0.02),
        'w_in': nrm(ks[8], (DEPTH, D_MODEL, IN_COLS), D_MODEL ** -0.5),
        'gate_bias': gate_bias,
        'g_q': 1.0 + nrm(ks[10], (DEPTH, A_HEAD_DIM), 0.02),
        'g_k': 1.0 + nrm(ks[11], (DEPTH, A_HEAD_DIM), 0.02),
        'g_mh': 1.0 + nrm(ks[12], (DEPTH, M_HEADS * M_V_DIM), 0.02),
        'w_out': nrm(ks[13], (DEPTH, MIX_WIDTH, D_MODEL), MIX_WIDTH ** -0.5),
        'g_ffn2': 1.0 + nrm(ks[14], (DEPTH, D_MODEL), 0.02),
        'w_gu2': nrm(ks[15], (DEPTH, D_MODEL, 2 * D_FF), D_MODEL ** -0.5),
        'w_down2': nrm(ks[16], (DEPTH, D_FF, D_MODEL), D_FF ** -0.5),
        'g_final': 1.0 + nrm(ks[17], (DEPTH, D_MODEL), 0.02),
    }

def first_block(x, c, w_ada, b_ada, g_ffn1, w_gu1, w_down1, g_mix, w_in, gate_bias, g_q, g_k, g_mh,
              w_out, g_ffn2, w_gu2, w_down2, g_final):
    B, S, D = x.shape
    cs = jax.nn.silu(c)
    for l in range(DEPTH):
        mod = (cs @ w_ada[l] + b_ada[l]).reshape(B, N_MOD, D)[:, :, None, :]
        sh1, sc1, gt1, sh2, sc2, gt2, sh3, sc3, gt3 = [mod[:, i] for i in range(N_MOD)]
        h = modulate(rms_norm(x, g_ffn1[l]), sh1, sc1)
        x = x + HALF_STEP * gt1 * swiglu(h, w_gu1[l], w_down1[l])
        h = modulate(rms_norm(x, g_mix[l]), sh2, sc2)
        x = x + gt2 * hybrid_mixer(h, w_in[l], gate_bias[l], g_q[l], g_k[l], g_mh[l], w_out[l])
        h = modulate(rms_norm(x, g_ffn2[l]), sh3, sc3)
        x = x + HALF_STEP * gt3 * swiglu(h, w_gu2[l], w_down2[l])
        x = rms_norm(x, g_final[l])
    return x


DEPTH_2 = 2

HEAD_DIM = 64
ATTN_W = D_MODEL // 2
N_Q_HEADS = ATTN_W // HEAD_DIM
N_KV_HEADS = N_Q_HEADS // 4
GQA_GROUP = N_Q_HEADS // N_KV_HEADS
KV_W = N_KV_HEADS * HEAD_DIM
CONV_W = D_MODEL // 4
CONV_HEADS = CONV_W // HEAD_DIM
CONV_K = 3
FFT_W = D_MODEL // 4
FFT_GROUP_DIM = 64
FFT_GROUPS = FFT_W // FFT_GROUP_DIM
MIX_W = ATTN_W + CONV_W + FFT_W
IN_SIZES = (ATTN_W, KV_W, KV_W, ATTN_W, CONV_W, CONV_W, CONV_W, CONV_W, FFT_W, FFT_W)
IN_W = sum(IN_SIZES)
GRID_W = 64
ROPE_THETA_2 = 10000.0
ROPE_HALF = HEAD_DIM // 2
Q_BLOCK = 128
RMS_EPS = 1e-6
LN_EPS = 1e-5
DEEPNORM_ALPHA = (2 * DEPTH_2) ** 0.25
DEEPNORM_BETA = (8 * DEPTH_2) ** -0.25
ADA_SCALE = 0.1


def _layer_norm(x, eps):
    xf = x.astype(jnp.float32)
    mu = jnp.mean(xf, axis=-1, keepdims=True)
    xc = xf - mu
    var = jnp.mean(xc * xc, axis=-1, keepdims=True)
    return (xc * lax.rsqrt(var + eps)).astype(x.dtype)

def _rms_norm(x, gain):
    xf = x.astype(jnp.float32)
    y = xf * lax.rsqrt(jnp.mean(xf * xf, axis=-1, keepdims=True) + RMS_EPS)
    return (y * gain.astype(jnp.float32)).astype(x.dtype)

def _axial_angles(seq_len):
    rows = seq_len // GRID_W
    row_pos = jnp.repeat(jnp.arange(rows, dtype=jnp.float32), GRID_W)
    col_pos = jnp.tile(jnp.arange(GRID_W, dtype=jnp.float32), rows)
    inv_freq = 1.0 / (ROPE_THETA_2 ** (jnp.arange(0, ROPE_HALF, 2, dtype=jnp.float32) / ROPE_HALF))
    return row_pos[:, None] * inv_freq, col_pos[:, None] * inv_freq

def _rope_half(x, ang):
    cos = jnp.cos(ang)[:, None, :].astype(x.dtype)
    sin = jnp.sin(ang)[:, None, :].astype(x.dtype)
    x1, x2 = jnp.split(x, 2, axis=-1)
    return jnp.concatenate([x1 * cos - x2 * sin, x2 * cos + x1 * sin], axis=-1)

def _axial_rope(x, row_ang, col_ang):
    xr, xc = jnp.split(x, 2, axis=-1)
    return jnp.concatenate([_rope_half(xr, row_ang), _rope_half(xc, col_ang)], axis=-1)

def _attention(q, k, v):
    b, s = q.shape[0], q.shape[1]
    nb = s // Q_BLOCK
    scale = HEAD_DIM ** -0.5
    qg = q.reshape(b, nb, Q_BLOCK, N_KV_HEADS, GQA_GROUP, HEAD_DIM).transpose(1, 0, 2, 3, 4, 5)

    def block(qb):
        scores = jnp.einsum('bqkgd,bskd->bkgqs', qb, k,
                            preferred_element_type=jnp.float32) * scale
        p = jax.nn.softmax(scores, axis=-1).astype(v.dtype)
        return jnp.einsum('bkgqs,bskd->bqkgd', p, v)

    o = lax.map(block, qg)
    return o.transpose(1, 0, 2, 3, 4, 5).reshape(b, s, ATTN_W)

def _short_conv(u, w):
    s = u.shape[1]
    pad = CONV_K // 2
    up = jnp.pad(u, ((0, 0), (pad, pad), (0, 0)))
    return sum(up[:, j:j + s, :] * w[j] for j in range(CONV_K))

def _fourier(u, f_mix):
    b, s = u.shape[0], u.shape[1]
    ug = u.reshape(b, s, FFT_GROUPS, FFT_GROUP_DIM).astype(jnp.float32)
    f = jnp.fft.fft2(ug, axes=(1, 3), norm='ortho').real.astype(u.dtype)
    f = jnp.einsum('bsgc,gcd->bsgd', f, f_mix)
    return f.reshape(b, s, FFT_W)

def _split_indices():
    return np.cumsum(np.array(IN_SIZES))[:-1].tolist()

def second_inputs(seed: int = 0) -> dict:
    key = jax.random.key(seed)
    ks = jax.random.split(key, 12)
    f32 = jnp.float32
    x = jax.random.normal(ks[0], (BATCH, SEQ, D_MODEL), f32)
    c = jax.random.normal(ks[1], (BATCH, D_MODEL), f32)
    w_ada = jax.random.normal(ks[2], (DEPTH_2, D_MODEL, 3 * D_MODEL), f32) * (D_MODEL ** -0.5) * ADA_SCALE
    b_ada = jax.random.normal(ks[3], (DEPTH_2, 3 * D_MODEL), f32) * 0.01
    w_in = jax.random.normal(ks[4], (DEPTH_2, D_MODEL, IN_W), f32) * (D_MODEL ** -0.5)
    q_gain = 1.0 + 0.05 * jax.random.normal(ks[5], (DEPTH_2, HEAD_DIM), f32)
    k_gain = 1.0 + 0.05 * jax.random.normal(ks[6], (DEPTH_2, HEAD_DIM), f32)
    conv_w = jax.random.normal(ks[7], (DEPTH_2, CONV_K, CONV_W), f32) * (CONV_K ** -0.5)
    f_mix = jax.random.normal(ks[8], (DEPTH_2, FFT_GROUPS, FFT_GROUP_DIM, FFT_GROUP_DIM), f32) * (FFT_GROUP_DIM ** -0.5)
    w_out = jax.random.normal(ks[9], (DEPTH_2, MIX_W, D_MODEL), f32) * (MIX_W ** -0.5) * DEEPNORM_BETA
    ln_g = 1.0 + 0.05 * jax.random.normal(ks[10], (DEPTH_2, D_MODEL), f32)
    ln_b = 0.01 * jax.random.normal(ks[11], (DEPTH_2, D_MODEL), f32)
    return {"x": x, "c": c, "w_ada": w_ada, "b_ada": b_ada, "w_in": w_in,
            "q_gain": q_gain, "k_gain": k_gain, "conv_w": conv_w, "f_mix": f_mix,
            "w_out": w_out, "ln_g": ln_g, "ln_b": ln_b}

def second_block(x, c, w_ada, b_ada, w_in, q_gain, k_gain, conv_w, f_mix, w_out, ln_g, ln_b):
    b, s, _ = x.shape
    row_ang, col_ang = _axial_angles(s)
    split_idx = _split_indices()
    for l in range(DEPTH_2):
        mod = c @ w_ada[l] + b_ada[l]
        shift, scale, gate = jnp.split(mod, 3, axis=-1)
        h = _layer_norm(x, LN_EPS) * (1.0 + scale[:, None, :]) + shift[:, None, :]

        proj = h @ w_in[l]
        q, k, v, g_a, cu, cb, cc, g_c, fu, g_f = jnp.split(proj, split_idx, axis=-1)

        q = _axial_rope(_rms_norm(q.reshape(b, s, N_Q_HEADS, HEAD_DIM), q_gain[l]), row_ang, col_ang)
        k = _axial_rope(_rms_norm(k.reshape(b, s, N_KV_HEADS, HEAD_DIM), k_gain[l]), row_ang, col_ang)
        v = v.reshape(b, s, N_KV_HEADS, HEAD_DIM)
        y_attn = _attention(q, k, v) * jax.nn.silu(g_a)

        y_conv = cb * _short_conv(cc * cu, conv_w[l]) * jax.nn.silu(g_c)

        y_four = _fourier(fu, f_mix[l]) * jax.nn.silu(g_f)

        y = jnp.concatenate([y_attn, y_conv, y_four], axis=-1) @ w_out[l]

        x = _layer_norm(DEEPNORM_ALPHA * x + (1.0 + gate[:, None, :]) * y, LN_EPS) * ln_g[l] + ln_b[l]
    return x


def setup_inputs(seed=0):
    out = dict(first_inputs(seed))
    for name, value in second_inputs(seed + 1).items():
        if name != "x":
            out[name + "_2"] = value
    return out


def reference(
    x, c, w_ada, b_ada, g_ffn1, w_gu1, w_down1, g_mix, w_in, gate_bias, g_q, g_k, g_mh, w_out,
    g_ffn2, w_gu2, w_down2, g_final, c_2, w_ada_2, b_ada_2, w_in_2, q_gain_2, k_gain_2,
    conv_w_2, f_mix_2, w_out_2, ln_g_2, ln_b_2,
):
    x = first_block(
        x, c, w_ada, b_ada, g_ffn1, w_gu1, w_down1, g_mix, w_in, gate_bias, g_q, g_k, g_mh,
        w_out, g_ffn2, w_gu2, w_down2, g_final,
    )
    return second_block(
        x, c_2, w_ada_2, b_ada_2, w_in_2, q_gain_2, k_gain_2, conv_w_2, f_mix_2, w_out_2,
        ln_g_2, ln_b_2,
    )


_drawn_inputs = setup_inputs


def setup_inputs(seed=0):
    import zlib

    import numpy as np

    out = dict(_drawn_inputs(seed))
    spreads = {}
    factors = {'g_ffn1': 8.0,
     'g_mix': 7.952,
     'g_q': 8.0,
     'g_k': 8.0,
     'g_mh': 51.436,
     'g_ffn2': 8.0,
     'g_final': 2.763,
     'b_ada_2': 8.0,
     'q_gain_2': 8.0,
     'k_gain_2': 8.0,
     'ln_b_2': 3.898}
    for name, (base, spread) in spreads.items():
        noise = np.random.default_rng([zlib.crc32(name.encode()), seed]).standard_normal(out[name].shape)
        drawn = base * np.exp(spread * noise) if base else spread * noise
        out[name] = __import__('jax').numpy.asarray(drawn.astype(out[name].dtype))
    for name, factor in factors.items():
        out[name] = (out[name] * factor).astype(out[name].dtype)
    return out
```

```python
from contextlib import ExitStack

import numpy as np

import concourse.bass as bass
from concourse import mybir

F32 = mybir.dt.float32
F32R = mybir.dt.float32r
ALU = mybir.AluOpType
ACT = mybir.ActivationFunctionType
AX = mybir.AxisListType

P = 128
S = 1024
D = 1024
KT = D // P
ST = S // P
HALF = 512
EPS = 1e-6
LN_EPS = 1e-5
NEG = -1e30
FF_TILES = 22
FF_GROUPS = (5, 5, 4, 4, 4)
A_SLOTS = 6
RAW = 2
BLK = 2048
M_HEADS, M_QK, M_V = 4, 64, 128
A_HEADS, A_DIM = 8, 64
EXP_CAP = 88.0
ALPHA = 4.0 ** 0.25
N_ADA1, N_ADA2 = 9, 3

VEC = {}
_at = 0
for _name, _n in (("c", 8), ("b_ada", 72), ("g_ffn1", 8), ("g_mix", 8), ("g_ffn2", 8), ("g_final", 8),
                  ("g_mh", 4), ("g_q", 1), ("g_k", 1), ("c_2", 8), ("b_ada_2", 48), ("q_gain_2", 2),
                  ("k_gain_2", 2), ("conv_w", 12), ("ln_g", 16), ("ln_b", 16), ("gate_bias", 1)):
    VEC[_name] = (_at, _n)
    _at += _n
NVEC = _at
MATS = ("mean1024", "mean64", "mean128", "ones", "ident", "rot1", "rot2", "cosc", "sinc", "causal", "anti",
        "fm00", "fm01", "fm10", "fm11")
MAT = {n: i for i, n in enumerate(MATS)}


class Op:

    def __init__(self, fn, after, sem):
        self.fn, self.after, self.sem, self.counted, self.value = fn, after, sem, False, 0


class Loaded:

    def __init__(self, sem, value):
        self.sem, self.value = sem, value


class Load:

    def __init__(self, fn, after, sem):
        self.fn, self.after, self.sem = fn, after, sem


class Queues:

    def __init__(self, nc, ctx):
        self.nc, self.ctx = nc, ctx
        self.q = {n: [] for n in ("tensor", "vector", "scalar", "gpsimd", "sync")}
        self.last = {}
        self.held = {n: [] for n in self.q}
        self.dma_count = {}
        self.stage("start")

    def sem(self, name):
        return self.ctx.enter_context(self.nc.semaphore(name))

    def stage(self, name):
        self.sems = {n: self.sem(f"{name}_{n}") for n in ("tensor", "vector", "scalar")}

    def put(self, engine, fn, after):
        flat = [a for a in self.held[engine]]
        self.held[engine] = []
        stack = list(after)
        while stack:
            a = stack.pop()
            if a is None:
                continue
            if isinstance(a, (list, tuple)):
                stack.extend(a)
            else:
                flat.append(a)
        for a in flat:
            if isinstance(a, Op):
                a.counted = True
        op = Op(fn, flat, self.sems[engine])
        self.q[engine].append(op)
        self.last[engine] = op
        return op

    def T(self, fn, *after):
        return self.put("tensor", fn, after)

    def V(self, fn, *after):
        return self.put("vector", fn, after)

    def A(self, fn, *after):
        return self.put("scalar", fn, after)

    def dma(self, sem, out, in_, *after, queue="gpsimd"):
        flat = list(self.held[queue])
        self.held[queue] = []
        stack = list(after)
        while stack:
            a = stack.pop()
            if a is None:
                continue
            if isinstance(a, (list, tuple)):
                stack.extend(a)
            else:
                flat.append(a)
        for a in flat:
            if isinstance(a, Op):
                a.counted = True
        self.q[queue].append(Load(lambda e, out=out, in_=in_: e.dma_start(out, in_), flat, sem))
        n = self.dma_count.get(id(sem), 0) + 16
        self.dma_count[id(sem)] = n
        return Loaded(sem, n)

    def fence(self, *more):
        done = [self.last[e] for e in ("tensor", "vector", "scalar") if e in self.last]
        extra = [x for m in more for x in (m if isinstance(m, (list, tuple)) else [m])]
        for e in ("tensor", "vector", "scalar", "gpsimd"):
            self.held[e] = done + extra
        for op in done:
            op.counted = True

    def emit(self, block):
        counts = {}
        for ops in self.q.values():
            for op in ops:
                if isinstance(op, Op) and op.counted:
                    counts[id(op.sem)] = counts.get(id(op.sem), 0) + 1
                    op.value = counts[id(op.sem)]

        def run(name):
            def body(engine):
                seen = {}
                for op in self.q[name]:
                    need = {}
                    for a in op.after:
                        if a.value > max(seen.get(id(a.sem), 0), need.get(id(a.sem), (0, 0))[1]):
                            need[id(a.sem)] = (a.sem, a.value)
                    for key, (sem, value) in need.items():
                        engine.wait_ge(sem, value)
                        seen[key] = value
                    ins = op.fn(engine)
                    if isinstance(op, Load):
                        ins.then_inc(op.sem, 16)
                    elif op.counted:
                        ins.then_inc(op.sem, 1)
                if name == "sync":
                    engine.wait_ge(self.end.sem, self.end.value)
            return body

        block.tensor(run("tensor"))
        block.vector(run("vector"))
        block.scalar(run("scalar"))
        block.gpsimd(run("gpsimd"))
        block.sync(run("sync"))


class Pair:

    def __init__(self, tensor, i):
        self.full = tensor[:, 2 * i:2 * i + 2, :].rearrange("p a b -> p (a b)")
        self.half = [tensor[:, 2 * i + h, :] for h in range(2)]
        self.read = []


class Weights:

    def __init__(self, q, sb, plan, ada_step):
        self.q, self.plan, self.ada_step = q, plan, ada_step
        self.raw = [sb(f"w_raw{i}", [P, BLK], F32) for i in range(RAW)]
        self.hi = [sb(f"w_hi{i}", [P, BLK], F32R) for i in range(2)]
        self.lo = [sb(f"w_lo{i}", [P, BLK], F32R) for i in range(2)]
        self.sem = [q.sem(f"w_loaded{i}") for i in range(RAW)]
        self.raw_read = [[] for _ in range(RAW)]
        self.landed = {}
        self.last_use = [[], []]
        self.issued = self.taken = self.split = 0
        self.ready = []
        for _ in range(RAW):
            self.issue()

    def issue(self):
        n = self.issued
        if n >= len(self.plan):
            return
        _, src, shape, _ = self.plan[n]
        size = int(np.prod(shape))
        dst = self.raw[n % RAW][:, 0:size]
        if len(shape) == 2:
            dst = dst.rearrange("p (a b) -> p a b", a=shape[0])
        self.landed[n] = self.q.dma(self.sem[n % RAW], dst, src, self.raw_read[n % RAW], queue="sync")
        self.issued += 1

    def advance(self):
        n = self.taken
        kind, _, shape, tag = self.plan[n]
        size = int(np.prod(shape))
        raw = self.raw[n % RAW][:, 0:size]
        if kind == "ada":
            done = self.ada_step(raw, tag, self.landed[n])
        else:
            s = self.split % 2
            hi, lo = self.hi[s][:, 0:size], self.lo[s][:, 0:size]
            up = self.q.A(lambda e: e.activation(hi, raw, ACT.Identity), self.landed[n], self.last_use[s])
            done = self.q.V(lambda e: e.tensor_tensor(lo, raw, hi.bitcast(F32), ALU.subtract), up)
            self.ready.append((s, tag, hi, lo, done))
            self.split += 1
        self.raw_read[n % RAW] = [done]
        self.taken += 1
        self.issue()

    def get(self, tag):
        while not self.ready:
            self.advance()
        s, got, hi, lo, done = self.ready.pop(0)
        assert got == tag, (got, tag)
        while self.taken < len(self.plan) and not self.ready:
            self.advance()
        return s, hi, lo, done

    def used(self, s, op):
        self.last_use[s] = [op]


def build(nc, ins, out, stop=None):
    ctx = ExitStack()
    with ctx:
        q = Queues(nc, ctx)
        T, V, A = q.T, q.V, q.A

        def sb(name, shape, dt, scope=ctx):
            return scope.enter_context(nc.sbuf_tensor(name, shape, dt))

        psum = ctx.enter_context(nc.psum_tensor("psum", [P, 8, HALF], F32))
        pairs = [Pair(psum, i) for i in range(4)]
        turn = [0]

        def take():
            turn[0] += 1
            return pairs[(turn[0] - 1) % 4]

        x = sb("x", [P, KT, S], F32)
        vec = sb("vec", [P, NVEC], F32)
        mats = sb("mats", [P, 2 * P], F32)
        mod1 = sb("mod1", [P, N_ADA1 * KT], F32)
        mod2 = sb("mod2", [P, 2 * N_ADA2 * KT], F32)
        cs = sb("cs", [P, KT], F32)
        cols = sb("cols", [P, 64], F32)
        acc = sb("ada_acc", [P, D], F32)
        one = sb("one", [P, 1], F32)
        eps = sb("eps", [P, 2], F32)
        mean1024, ident = mats[:, 0:P], mats[:, P:2 * P]

        proj = nc.dram_tensor("proj_scratch", [24, P, S], F32).ap()
        avs = nc.dram_tensor("av_rows", [P, ST, 512], F32).ap()
        mvs = nc.dram_tensor("mv_rows", [P, ST, 512], F32).ap()
        mixd = nc.dram_tensor("mix_scratch", [KT, P, S], F32).ap()

        s_const, s_x = q.sem("const_loaded"), [q.sem(f"x_loaded{i}") for i in range(2)]
        vec_in = q.dma(s_const, vec[:], ins["vec"])
        q.dma(s_const, mats[:, 0:P], ins["mats"][MAT["mean1024"]], vec_in)
        consts = q.dma(s_const, mats[:, P:2 * P], ins["mats"][MAT["ident"]])
        x_in = []
        for i in range(2):
            x_in += [q.dma(s_x[i], x[:, 4 * i:4 * i + 4, :], ins["xT"][:, 4 * i:4 * i + 4, :])] * 4
        one_set = V(lambda e: e.memset(one[:], 1.0))
        V(lambda e: e.memset(eps[:, 0:1], EPS))
        eps_set = V(lambda e: e.memset(eps[:, 1:2], LN_EPS))

        def vc(name, i=0, n=1):
            return vec[:, VEC[name][0] + i:VEC[name][0] + i + n]

        cs_set = A(lambda e: e.activation(cs[:], vc("c", 0, 8), ACT.Silu), consts)
        mod_done = {}
        ada = {"free": [], "last": None, "due": []}

        def ada_step(raw, tag, landed):
            layer, i, kp = tag
            if kp == 0:
                ada_finish()
            for j in range(2):
                k = 2 * kp + j
                w = raw[:, j * D:(j + 1) * D]
                cv = cs[:, k:k + 1] if layer == 0 else vc("c_2", k)
                if k == 0:
                    ada["last"] = V(lambda e, w=w, cv=cv: e.tensor_scalar(acc[:], w, cv, None, ALU.mult),
                                    landed, cs_set, consts, ada["free"])
                else:
                    ada["last"] = V(lambda e, w=w, cv=cv: e.scalar_tensor_tensor(
                        out=acc[:], in0=w, scalar=cv, in1=acc[:], op0=ALU.mult, op1=ALU.add), landed, ada["last"])
            if kp == KT // 2 - 1:
                ada["due"].append((layer, i, ada["last"]))
                ada["free"] = None
            return ada["last"]

        def ada_finish():
            while ada["due"]:
                layer, i, done = ada["due"].pop(0)
                p = take()
                for j in range(KT):
                    mm = T(lambda e, j=j, p=p: e.matmul(p.full[:, j:j + 1], acc[:, j * P:(j + 1) * P], one[:],
                                                       start=True, stop=True), done, p.read, one_set)
                dst = mod1[:, i * KT:(i + 1) * KT] if layer == 0 else \
                    mod2[:, ((layer - 1) * N_ADA2 + i) * KT:((layer - 1) * N_ADA2 + i + 1) * KT]
                bias = vc("b_ada", i * KT, KT) if layer == 0 else vc("b_ada_2", ((layer - 1) * N_ADA2 + i) * KT, KT)
                d = V(lambda e, p=p, dst=dst, bias=bias: e.tensor_tensor(dst, p.full[:, 0:KT], bias, ALU.add), mm)
                p.read = [d]
                mod_done[(layer, i)] = d
                ada["free"] = [mm]

        plan = []
        ada_list = [(0, i, kp) for i in range(N_ADA1) for kp in range(4)] + \
                   [(l, i, kp) for l in (1, 2) for i in range(N_ADA2) for kp in range(4)]

        def plan_ada(n):
            for _ in range(min(n, len(ada_list))):
                l, i, kp = ada_list.pop(0)
                w = ins["w_ada"] if l == 0 else ins["w_ada_2"][l - 1]
                src = w[2 * kp * P:(2 * kp + 2) * P, i * D:(i + 1) * D].rearrange("(k p) n -> p k n", p=P)
                plan.append(("ada", src, (2, D), (l, i, kp)))

        def ffn_order():
            first, seq = 0, []
            starts = np.cumsum((0,) + FF_GROUPS)
            for g, n in enumerate(FF_GROUPS):
                fs = list(range(starts[g], starts[g + 1]))
                seq += [("gu", f) for f in (fs if g == 0 else fs[1:])]
                if g + 1 < len(FF_GROUPS):
                    seq.append(("gu", int(starts[g + 1])))
                seq.append(("down", g))
            return [(k, int(n)) for k, n in seq], starts

        def plan_ffn(n):
            seq, starts = ffn_order()
            for kind, i in seq:
                if kind == "gu":
                    plan.append(("w", ins[f"w_gu{n}"][i], (BLK,), ("gu", n, i)))
                    plan_ada(1)
                else:
                    for c in range(4):
                        src = ins[f"w_down{n}"][int(starts[i]):int(starts[i + 1]), :, c * 256:(c + 1) * 256]
                        plan.append(("w", src.rearrange("f p c -> p f c"), (FF_GROUPS[i], 256), ("down", n, i, c)))

        plan_ada(8)
        plan_ffn(1)
        for b in range(13):
            if b == 12:
                plan.append(("w", ins["w_in_gate"], (KT * P,), ("in1", b)))
            else:
                plan.append(("w", ins["w_in"][b], (BLK,), ("in1", b)))
            plan_ada(1)
        for c in range(4):
            plan.append(("w", ins["w_out"][:, :, c * 256:(c + 1) * 256].rearrange("f p c -> p f c"), (KT, 256), ("out1", c)))
        plan_ffn(2)
        plan_ada(99)
        for l in range(2):
            for b in range(11):
                plan.append(("w", ins["w_in_2"][l, b], (BLK,), ("in2", l, b)))
            for c in range(4):
                for t in range(2):
                    plan.append(("w", ins["dft"][t][:, :, c * 256:(c + 1) * 256].rearrange("f p c -> p f c"),
                                 (KT, 256), ("dft", l, c, t)))
            for c in range(4):
                plan.append(("w", ins["w_out_2"][l][:, :, c * 256:(c + 1) * 256].rearrange("f p c -> p f c"), (KT, 256),
                             ("out2", l, c)))
        W = Weights(q, sb, plan, ada_step)

        def get(tag):
            ada_finish()
            return W.get(tag)

        def gemm(blk, m, n, hi, lo, ready, width=256):
            s, whi, wlo, wdone = blk
            p = take()
            for k in range(n):
                for i, (a, b) in enumerate(((whi, hi), (whi, lo), (wlo, hi))):
                    for h in range(2):
                        mm = T(lambda e, a=a, b=b(k), k=k, h=h, i=i, p=p: e.matmul(
                            p.half[h], a[:, k * width + m * P:k * width + (m + 1) * P], b[:, h * HALF:(h + 1) * HALF],
                            start=(k == 0 and i == 0), stop=(k == n - 1 and i == 2)),
                            wdone, p.read if k == 0 and i == 0 else None, ready[k] if i < 2 else None)
            W.used(s, mm)
            return p, mm

        def gemm_rows(blk, hi, lo, tt0, ready):
            s, whi, wlo, wdone = blk
            p = take()
            for j in range(4):
                for k in range(KT):
                    for i, (a, b) in enumerate(((whi, hi), (whi, lo), (wlo, hi))):
                        mm = T(lambda e, a=a, b=b(k), k=k, j=j, i=i, p=p: e.matmul(
                            p.full[:, j * 256:(j + 1) * 256], b[:, (tt0 + j) * P:(tt0 + j + 1) * P],
                            a[:, k * 256:(k + 1) * 256], start=(k == 0 and i == 0), stop=(k == KT - 1 and i == 2)),
                            wdone, p.read if j == 0 else None, ready[k])
            W.used(s, mm)
            return p, mm

        def mean_over_features(mat, src, n, ready, free):
            p = take()
            for k in range(n):
                for h in range(2):
                    mm = T(lambda e, k=k, h=h, p=p: e.matmul(p.half[h], mat, src(k)[:, h * HALF:(h + 1) * HALF],
                                                            start=(k == 0), stop=(k == n - 1)),
                           ready(k), p.read if k == 0 else None)
                free(k, mm)
            return p, mm

        def rsqrt(var, epsc, r, u, after, free=None):
            l1 = A(lambda e: e.activation(r, var, ACT.Ln, bias=epsc), after, eps_set, free)
            l2 = A(lambda e: e.activation(r, r, ACT.Exp, scale=-0.5), l1)
            n1 = V(lambda e: e.scalar_tensor_tensor(out=u, in0=r, scalar=-0.5, in1=r, op0=ALU.mult, op1=ALU.mult), l2, free)
            n2 = V(lambda e: e.scalar_tensor_tensor(out=u, in0=var, scalar=epsc, in1=u, op0=ALU.add, op1=ALU.mult), n1)
            return V(lambda e: e.scalar_tensor_tensor(out=r, in0=u, scalar=1.5, in1=r, op0=ALU.add, op1=ALU.mult), n2), n2

        x_ready = [x_in[k] for k in range(KT)]

        def scale_cols(dst, g, sc, after):
            return V(lambda e: e.scalar_tensor_tensor(out=dst, in0=sc, scalar=1.0, in1=g, op0=ALU.add, op1=ALU.mult), after)

        def rms_stats(scope, name):
            sq = [sb(f"{name}_sq{i}", [P, S], F32, scope) for i in range(2)]
            r = sb(f"{name}_r", [P, S], F32, scope)
            u = sb(f"{name}_u", [P, S], F32, scope)
            sq_read = [None, None]
            sqd = {}

            def ready(k):
                sqd[k] = A(lambda e: e.activation(sq[k % 2][:], x[:, k, :], ACT.Square), x_ready[k], sq_read[k % 2])
                return sqd[k]

            def free(k, mm):
                sq_read[k % 2] = mm

            p, mm = mean_over_features(mean1024, lambda k: sq[k % 2], KT, lambda k: sqd[k] if k in sqd else ready(k), free)
            done, pr = rsqrt(p.full, eps[:, 0:1], r[:], u[:], mm)
            p.read = [pr]
            return r, done

        def split_shifted(t, sh, hi, lo, after):
            up = A(lambda e: e.activation(hi, t, ACT.Identity, bias=sh), after)
            dn = V(lambda e: e.scalar_tensor_tensor(out=lo, in0=t, scalar=sh, in1=hi.bitcast(F32), op0=ALU.add,
                                                    op1=ALU.subtract), up)
            return dn

        def modulated(name, h, g, ish, isc):
            while (0, ish) not in mod_done or (0, isc) not in mod_done:
                W.advance()
                ada_finish()
            with ExitStack() as scope:
                r, rd = rms_stats(scope, name)
                t = [sb(f"{name}_t{i}", [P, S], F32, scope) for i in range(2)]
                c0 = scale_cols(cols[:, 0:8], vc(g, 0, 8), mod1[:, isc * 8:isc * 8 + 8],
                                [mod_done[(0, isc)], mod_done[(0, ish)]])
                ready, free = [], [None, None]
                for k in range(KT):
                    td = V(lambda e, k=k: e.scalar_tensor_tensor(out=t[k % 2][:], in0=x[:, k, :], scalar=cols[:, k:k + 1],
                                                                 in1=r[:], op0=ALU.mult, op1=ALU.mult), rd, c0, free[k % 2])
                    d = split_shifted(t[k % 2][:], mod1[:, ish * 8 + k:ish * 8 + k + 1], h[0][:, k, :], h[1][:, k, :], td)
                    ready.append(d)
                    free[k % 2] = d
            return ready

        def ffn(n, igt):
            q.stage(f"ffn{n}")
            q.fence()
            with ExitStack() as hs:
                h = [sb(f"h{n}_hi", [P, KT, S], F32R, hs), sb(f"h{n}_lo", [P, KT, S], F32R, hs)]
                ready = modulated(f"nf{n}", h, f"g_ffn{n}", igt - 2, igt - 1)
                q.fence()
                ah = [sb(f"a{n}_hi{i}", [P, S], F32R, hs) for i in range(A_SLOTS)]
                al = [sb(f"a{n}_lo{i}", [P, S], F32R, hs) for i in range(A_SLOTS)]
                g = sb(f"gate{n}", [P, S], F32, hs)
                a_ready, a_free, g_free, gcols = {}, {}, [None], [None]
                seq, starts = ffn_order()
                for kind, i in seq:
                    if kind == "gu":
                        blk = get(("gu", n, i))
                        pg, m1 = gemm(blk, 0, KT, lambda k: h[0][:, k, :], lambda k: h[1][:, k, :], ready)
                        gd = A(lambda e, pg=pg: e.activation(g[:], pg.full, ACT.Silu), m1, g_free[0])
                        pg.read = [gd]
                        pu, m2 = gemm(blk, 1, KT, lambda k: h[0][:, k, :], lambda k: h[1][:, k, :], ready)
                        s = i % A_SLOTS
                        ad = V(lambda e, pu=pu: e.tensor_tensor(g[:], g[:], pu.full, ALU.mult), gd, m2)
                        pu.read = [ad]
                        up = A(lambda e, s=s: e.activation(ah[s][:], g[:], ACT.Identity), ad, a_free.get(i - A_SLOTS))
                        dn = V(lambda e, s=s: e.tensor_tensor(al[s][:], g[:], ah[s][:].bitcast(F32), ALU.subtract), up)
                        g_free[0] = dn
                        a_ready[i] = dn
                    else:
                        f0, nf = int(starts[i]), FF_GROUPS[i]
                        for c in range(4):
                            blk = get(("down", n, i, c))
                            if gcols[0] is None:
                                gcols[0] = V(lambda e: e.tensor_scalar(cols[:, 8:16], mod1[:, igt * 8:igt * 8 + 8], 0.5, None,
                                                                       ALU.mult), mod_done[(0, igt)])
                            for m in range(2):
                                d = 2 * c + m
                                p, mm = gemm(blk, m, nf, lambda k: ah[(f0 + k) % A_SLOTS], lambda k: al[(f0 + k) % A_SLOTS],
                                             [a_ready[f0 + k] for k in range(nf)])
                                x_ready[d] = V(lambda e, p=p, d=d: e.scalar_tensor_tensor(
                                    out=x[:, d, :], in0=p.full, scalar=cols[:, 8 + d:9 + d], in1=x[:, d, :],
                                    op0=ALU.mult, op1=ALU.add), mm, gcols[0], x_ready[d])
                                p.read = [x_ready[d]]
                        for f in range(f0, f0 + nf):
                            a_free[f] = mm

        spilled = {}

        class Store:

            def __init__(self, name, n, scope, width=S):
                self.t = [sb(f"{name}{i}", [P, width], F32, scope) for i in range(n)]
                self.s = [q.sem(f"{name}_stored{i}") for i in range(n)]
                self.free = [None] * n
                self.i, self.n = 0, n

            def next(self):
                i = self.i % self.n
                return self.t[i], self.free[i]

            def store(self, dst, key, *after):
                i = self.i % self.n
                self.i += 1
                self.free[i] = q.dma(self.s[i], dst, self.t[i][:], *after, queue="gpsimd")
                spilled[key] = self.free[i]

            def all(self):
                return [f for f in self.free if f is not None]

        def rope_heads(store, tmp, mats64, rot, cost, sint, gcol, key, dst, after0, p, mm, w):
            raw, sq, r, u, free = tmp
            a1 = A(lambda e: e.activation(sq, p.full, ACT.Square), mm, free)
            a2 = A(lambda e: e.activation(raw, p.full, ACT.Identity), mm, free)
            p.read = [a1, a2]
            yield
            p2 = take()
            for h in range(2):
                m2 = T(lambda e, h=h, p2=p2: e.matmul(p2.half[h], mats64, sq[:, h * HALF:(h + 1) * HALF], start=True,
                                                     stop=True), a1, p2.read, after0)
            rd, pr = rsqrt(p2.full, eps[:, 0:1], r, u, m2)
            p2.read = [pr]
            qn = V(lambda e: e.scalar_tensor_tensor(out=raw, in0=raw, scalar=gcol, in1=r, op0=ALU.mult, op1=ALU.mult),
                   rd, a2, after0)
            yield
            p3 = take()
            for h in range(2):
                m3 = T(lambda e, h=h, p3=p3: e.matmul(p3.half[h], rot, raw[:, h * HALF:(h + 1) * HALF], start=True,
                                                     stop=True), qn, p3.read)
            o, ofree = store.next()
            c1 = V(lambda e: e.tensor_tensor(o[:], raw, cost, ALU.mult), qn, ofree)
            c2 = V(lambda e: e.tensor_tensor(u, p3.full, sint, ALU.mult), m3, rd)
            p3.read = [c2]
            c3 = V(lambda e: e.tensor_tensor(o[:], o[:], u, ALU.add), c1, c2)
            tmp[4] = [c3, m3]
            store.store(dst, key, c3)
            yield

        def step(pending):
            for g in list(pending):
                try:
                    next(g)
                except StopIteration:
                    pending.remove(g)

        def attention(name, heads_of, mask, gate_key, mix0):
            q.stage(name)
            with ExitStack() as sc:
                maskt = None
                sem_m = q.sem(f"{name}_maskload")
                if mask is not None:
                    maskt = sb(f"{name}_mask", [P, 1920], F32, sc)
                    mask_in = q.dma(sem_m, maskt[:], mask)
                qt = [sb(f"{name}_q{i}", [P, S], F32, sc) for i in range(2)]
                kt = [sb(f"{name}_k{i}", [P, S], F32, sc) for i in range(2)]
                gt = [sb(f"{name}_g{i}", [P, S], F32, sc) for i in range(2)] if gate_key else None
                vt = sb(f"{name}_v", [P, ST, 512 if gate_key is None else P], F32, sc)
                pr = [sb(f"{name}_p{i}", [P, S], F32, sc) for i in range(2)]
                pt = [sb(f"{name}_pt{i}", [P, S], F32, sc) for i in range(2)]
                sm = [sb(f"{name}_sm{i}", [P, 4], F32, sc) for i in range(2)]
                st = Store(f"{name}_o", 2, sc)
                sem_q = [q.sem(f"{name}_qload{i}") for i in range(2)]
                sem_k = [q.sem(f"{name}_kload{i}") for i in range(2)]
                sem_g = [q.sem(f"{name}_gload{i}") for i in range(2)]
                sem_v = q.sem(f"{name}_vload")
                gq = gate_key is not None
                qf, kf, gf = [None, None], [None, None], [None, None]
                qin, kin, gin = {}, {}, {}

                def load(pp):
                    i = pp % 2
                    qin[pp] = q.dma(sem_q[i], qt[i][:], proj[pp], spilled[("proj", pp)], qf[i])
                    if gq:
                        kv = heads_of(2 * pp)
                        kin_ = q.dma(sem_k[i], kt[i][0:64, :], proj[4][kv * 64:kv * 64 + 64, :], spilled[("proj", 4)], kf[i])
                        kin[pp] = q.dma(sem_k[i], kt[i][64:128, :], proj[4][kv * 64:kv * 64 + 64, :], kin_)
                        gin[pp] = q.dma(sem_g[i], gt[i][:], proj[gate_key + pp], spilled[("proj", gate_key + pp)], gf[i])
                    else:
                        kin[pp] = q.dma(sem_k[i], kt[i][:], proj[4 + pp], spilled[("proj", 4 + pp)], kf[i])

                load(0)
                if gq:
                    v_in = None
                    vfm = pt[0]
                    vl = q.dma(sem_v, vfm[:], proj[5], spilled[("proj", 5)])
                    p = take()
                    for j in range(ST):
                        mm = T(lambda e, j=j, p=p: e.transpose(p.full[:, j * P:(j + 1) * P], vfm[:, j * P:(j + 1) * P],
                                                              ident), vl, p.read)
                    v_in = A(lambda e, p=p: e.activation(vt[:].rearrange("p a b -> p (a b)"), p.full, ACT.Identity), mm)
                    p.read = [v_in]
                else:
                    v_in = q.dma(sem_v, vt[:], avs, spilled[("avs", 0)], spilled[("avs", 1)])
                base = turn[0]
                ps_s, ps_t, ps_o = [take(), take()], take(), take()
                p_free, pt_free = [None, None], [None, None]
                n = A_HEADS * ST
                soft, turned, outs = {}, {}, {}

                def unit(u):
                    return u // 16, (u // 2) % 8, u % 2

                def scores(u):
                    pp, i, hh = unit(u)
                    if i == 4 and hh == 0 and pp < 3:
                        load(pp + 1)
                    p = ps_s[u % 2]
                    lo, b = 64 * hh, pp % 2
                    for h in range(2):
                        mm = T(lambda e, h=h: e.matmul(p.half[h], qt[b][lo:lo + 64, i * P:(i + 1) * P],
                                                      kt[b][lo:lo + 64, h * HALF:(h + 1) * HALF], start=True, stop=True),
                               qin[pp], kin[pp], p.read)
                    if i == 7 and hh == 1:
                        qf[b], kf[b] = mm, mm
                    s, m = pr[u % 2], sm[u % 2]
                    if mask is not None:
                        o = 896 - P * i
                        mx = V(lambda e: e.tensor_tensor(s[:], p.full, maskt[:, o:o + S], ALU.add), mm, mask_in,
                               p_free[u % 2])
                        p.read = [mx]
                        mx = V(lambda e: e.tensor_reduce(m[:, 0:1], s[:], AX.X, ALU.max), mx)
                        src = s[:]
                    else:
                        mx = V(lambda e: e.tensor_reduce(m[:, 0:1], p.full, AX.X, ALU.max), mm, p_free[u % 2])
                        src = p.full
                    mx = V(lambda e: e.tensor_scalar(m[:, 1:2], m[:, 0:1], -1.0, None, ALU.mult), mx)
                    ex = A(lambda e: e.activation(s[:], src, ACT.Exp, bias=m[:, 1:2], accum_out=m[:, 2:3]), mx,
                           p_free[u % 2])
                    if mask is None:
                        p.read = [ex]
                    rc = V(lambda e: e.reciprocal(m[:, 3:4], m[:, 2:3]), ex)
                    soft[u] = V(lambda e: e.tensor_scalar(s[:], s[:], m[:, 3:4], None, ALU.mult), rc)

                def turn_over(u):
                    s = pr[u % 2]
                    for j in range(ST):
                        mm = T(lambda e, j=j: e.transpose(ps_t.full[:, j * P:(j + 1) * P], s[:, j * P:(j + 1) * P], ident),
                               soft[u], ps_t.read)
                    p_free[u % 2] = mm
                    turned[u] = A(lambda e: e.activation(pt[u % 2][:], ps_t.full, ACT.Identity), mm, pt_free[u % 2])
                    ps_t.read = [turned[u]]

                def times_v(u):
                    pp, i, hh = unit(u)
                    kv = heads_of(2 * pp + hh)
                    o = ps_o.half[i // 4][64 * hh:64 * hh + 64, (i % 4) * P:(i % 4 + 1) * P]
                    for j in range(ST):
                        mm = T(lambda e, j=j: e.matmul(o, vt[:, j, kv * 64:kv * 64 + 64], pt[u % 2][:, j * P:(j + 1) * P],
                                                      start=(j == 0), stop=(j == ST - 1)), turned[u], v_in,
                               ps_o.read if i == 0 and hh == 0 else None,
                               ps_o.read2 if i == 4 and hh == 0 else None)
                    pt_free[u % 2] = mm
                    if hh == 1 and i % 4 == 3:
                        h = i // 4
                        t, fr = st.next()
                        c = slice(h * HALF, (h + 1) * HALF)
                        if gq:
                            d = V(lambda e: e.tensor_tensor(t[:, c], ps_o.half[h], gt[pp % 2][:, c], ALU.mult), mm, fr, gin[pp])
                            gf[pp % 2] = d
                        else:
                            d = V(lambda e: e.tensor_copy(t[:, c], ps_o.half[h]), mm, fr)
                        if h == 0:
                            ps_o.read = [d]
                        else:
                            ps_o.read2 = [d]
                            st.store(mixd[mix0 + pp], ("mix", mix0 + pp), d)

                ps_o.read2 = list(ps_o.read)
                if gq:
                    pt_free[0] = v_in
                for u in range(n + 2):
                    if u < n:
                        scores(u)
                    if 1 <= u <= n:
                        turn_over(u - 1)
                    if u >= 2:
                        times_v(u - 2)
                ps_o.read = ps_o.read + ps_o.read2
                return st.all()

        def load_mix(name, h):
            with ExitStack() as sc:
                t = [sb(f"{name}_t{i}", [P, S], F32, sc) for i in range(3)]
                sm = [q.sem(f"{name}_load{i}") for i in range(3)]
                free, ready = [None] * 3, []
                for k in range(KT):
                    ld = q.dma(sm[k % 3], t[k % 3][:], mixd[k], spilled[("mix", k)], free[k % 3])
                    up = A(lambda e, k=k: e.activation(h[0][:, k, :], t[k % 3][:], ACT.Identity), ld)
                    dn = V(lambda e, k=k: e.tensor_tensor(h[1][:, k, :], t[k % 3][:], h[0][:, k, :].bitcast(F32),
                                                          ALU.subtract), up)
                    free[k % 3] = dn
                    ready.append(dn)
            return ready

        def mixer1():
            q.stage("proj1")
            q.fence()
            with ExitStack() as hs:
                h = [sb("hm_hi", [P, KT, S], F32R, hs), sb("hm_lo", [P, KT, S], F32R, hs)]
                ready = modulated("nm", h, "g_mix", 3, 4)
                q.fence()
                hi, lo = (lambda k: h[0][:, k, :]), (lambda k: h[1][:, k, :])
                with ExitStack() as sc:
                    cst = sb("rope_cos", [P, S], F32, sc)
                    snt = sb("rope_sin", [P, S], F32, sc)
                    m2 = sb("rope_mats", [P, 2 * P], F32, sc)
                    s_t = q.sem("rope1_loaded")
                    t1 = q.dma(s_t, cst[:], ins["rope1"][0])
                    t2 = q.dma(s_t, snt[:], ins["rope1"][1])
                    t2 = q.dma(s_t, m2[:, 0:P], ins["mats"][MAT["mean64"]])
                    tables = q.dma(s_t, m2[:, P:2 * P], ins["mats"][MAT["rot1"]])
                    gq = V(lambda e: e.tensor_scalar(cols[:, 16:17], vc("g_q"), A_DIM ** -0.5, None, ALU.mult))
                    st = Store("p1_o", 2, sc)
                    tmps = []
                    for i in range(2):
                        tmps.append([sb(f"p1_{n}{i}", [P, S], F32, sc)[:] for n in ("raw", "sq", "r", "u")] + [None])
                    pending = []
                    nt = 0
                    for b in range(4):
                        blk = get(("in1", b))
                        for m in range(2):
                            p, mm = gemm(blk, m, KT, hi, lo, ready)
                            step(pending)
                            gc = cols[:, 16:17] if b < 2 else vc("g_k")
                            pending.append(rope_heads(st, tmps[nt % 2], m2[:, 0:P], m2[:, P:2 * P], cst[:], snt[:], gc,
                                                      ("proj", nt), proj[nt], [tables, gq], p, mm, nt))
                            next(pending[-1])
                            nt += 1
                    while pending:
                        step(pending)
                    done = st.all()
                q.fence(done)
                with ExitStack() as sc:
                    st = Store("p1b_o", 4, sc)
                    for b in range(4, 8):
                        blk = get(("in1", b))
                        for t0 in (0, 4):
                            p, mm = gemm_rows(blk, hi, lo, t0, ready)
                            t, fr = st.next()
                            d = A(lambda e, p=p, t=t: e.activation(t[:], p.full, ACT.Identity), mm, fr)
                            p.read = [d]
                            dst = (avs if b < 6 else mvs)[:, t0:t0 + 4, (b % 2) * 256:(b % 2 + 1) * 256]
                            st_t = t
                            i = st.i % st.n
                            st.i += 1
                            st.free[i] = q.dma(st.s[i], dst, t[:].rearrange("p (a b) -> p a b", a=4), d)
                            key = ("avs" if b < 6 else "mvs", b % 2)
                            spilled[key] = [spilled.get(key), st.free[i]]
                    for b in range(8, 13):
                        blk = get(("in1", b))
                        for m in range(2 if b < 12 else 1):
                            p, mm = gemm(blk, m, KT, hi, lo, ready, 256 if b < 12 else P)
                            t, fr = st.next()
                            if b == 9:
                                d = A(lambda e, p=p, t=t: e.activation(t[:], p.full, ACT.Identity, scale=M_QK ** -0.5), mm, fr)
                            elif b in (10, 11):
                                d = A(lambda e, p=p, t=t: e.activation(t[:], p.full, ACT.Sigmoid), mm, fr)
                            elif b == 12:
                                d = A(lambda e, p=p, t=t: e.activation(t[:], p.full, ACT.Identity, bias=vc("gate_bias")),
                                      mm, fr)
                            else:
                                d = A(lambda e, p=p, t=t: e.activation(t[:], p.full, ACT.Identity), mm, fr)
                            p.read = [d]
                            n = 8 + 2 * (b - 8) + m
                            st.store(proj[n], ("proj", n), d)
                    done = st.all()
            q.fence(done)
            done = mlstm()
            q.fence(done)
            done = attention("attn1", lambda h: h, ins["band"], None, 4)
            q.stage("out1")
            q.fence(done)
            with ExitStack() as hs:
                h = [sb("mix1_hi", [P, KT, S], F32R, hs), sb("mix1_lo", [P, KT, S], F32R, hs)]
                ready = load_mix("mix1", h)
                for c in range(4):
                    blk = get(("out1", c))
                    for m in range(2):
                        d = 2 * c + m
                        p, mm = gemm(blk, m, KT, lambda k: h[0][:, k, :], lambda k: h[1][:, k, :], ready)
                        x_ready[d] = V(lambda e, p=p, d=d: e.scalar_tensor_tensor(
                            out=x[:, d, :], in0=p.full, scalar=mod1[:, 5 * 8 + d:5 * 8 + d + 1], in1=x[:, d, :],
                            op0=ALU.mult, op1=ALU.add), mm, x_ready[d], mod_done[(0, 5)])
                        p.read = [x_ready[d]]

        def mlstm():
            q.stage("mlstm_rows")
            R = 36
            with ExitStack() as sc:
                colsA = sb("ml_colsA", [P, ST, P], F32, sc)
                colsB = sb("ml_colsB", [P, ST, P], F32, sc)
                nm = sb("ml_negM", [R, S], F32, sc)
                decB = sb("ml_decay", [P, 2, 2, ST], F32, sc)
                sel = sb("ml_sel", [R, 8 * P], F32, sc)
                mm_ = sb("ml_mats", [P, 3 * P], F32, sc)
                qk = sb("ml_qk", [P, 4, S], F32, sc)
                v1 = sb("ml_v", [P, ST, M_HEADS, M_V + 1], F32, sc)
                s_t = q.sem("ml_consts")
                ones, causal, anti = mm_[:, 0:P], mm_[:, P:2 * P], mm_[:, 2 * P:3 * P]
                q.dma(s_t, ones, ins["mats"][MAT["ones"]])
                q.dma(s_t, causal, ins["mats"][MAT["causal"]])
                q.dma(s_t, anti, ins["mats"][MAT["anti"]])
                tabs = q.dma(s_t, sel[:], ins["sel"])
                s_qk = q.sem("ml_qk_loaded")
                s_v = q.sem("ml_v_loaded")
                with ExitStack() as rs:
                    li = sb("ml_li", [R, S], F32, rs)
                    lf = sb("ml_lf", [R, S], F32, rs)
                    t1 = sb("ml_t1", [R, S], F32, rs)
                    t2 = sb("ml_t2", [R, S], F32, rs)
                    b = sb("ml_b", [R, S], F32, rs)
                    M = sb("ml_M", [R, S], F32, rs)
                    rst = sb("ml_reset", [R, S], F32, rs)
                    mrow = sb("ml_m", [R, 16], F32, rs)
                    dec = sb("ml_dec", [R, ST], F32, rs)
                    dex = sb("ml_decx", [R, R, ST], F32, rs)
                    QA = sb("ml_QA", [P, S], F32, rs)
                    QB = sb("ml_QB", [P, S], F32, rs)
                    s_g = q.sem("ml_gates_loaded")
                    gate = proj[16]
                    q.dma(s_g, li[0:32, :], gate[0:32, :], spilled[("proj", 16)])
                    q.dma(s_g, t1[32:36, :], gate[32:36, :])
                    q.dma(s_g, lf[0:32, :], gate[64:96, :])
                    q.dma(s_g, t2[32:36, :], gate[96:100, :])
                    g_in = q.dma(s_g, rst[:], ins["reset"])
                    for i in range(4):
                        qk_in = q.dma(s_qk, qk[:, i, :], proj[8 + i], spilled[("proj", 8 + i)])
                    for c in range(ST):
                        v_in = q.dma(s_v, v1[:, c, :, 0:M_V], mvs[:, c, :].rearrange("p (h v) -> p h v", h=M_HEADS),
                                     spilled[("mvs", 0)], spilled[("mvs", 1)])
                    v_one = V(lambda e: e.memset(v1[:, :, :, M_V:M_V + 1], 1.0))
                    V(lambda e: e.memset(QA[:], 0.0))
                    q0 = V(lambda e: e.memset(QB[:], 0.0))
                    r1 = V(lambda e: e.tensor_copy(li[32:36, :], t1[32:36, ::-1]), g_in)
                    r2 = V(lambda e: e.tensor_copy(lf[32:36, :], t2[32:36, ::-1]), g_in)
                    a1 = A(lambda e: e.activation(t1[:], lf[:], ACT.Abs), r2, r1)
                    a2 = A(lambda e: e.activation(t1[:], t1[:], ACT.Exp, scale=-1.0), a1)
                    a3 = A(lambda e: e.activation(t1[:], t1[:], ACT.Ln, bias=one[0:R, 0:1]), a2, one_set)
                    f1 = V(lambda e: e.scalar_tensor_tensor(out=lf[:], in0=lf[:], scalar=0.0, in1=t1[:], op0=ALU.min,
                                                            op1=ALU.subtract), a3)
                    b1 = V(lambda e: e.tensor_tensor_scan(b[:], rst[:], lf[:], 0.0, ALU.mult, ALU.add), f1)
                    s1 = V(lambda e: e.tensor_tensor(li[:], li[:], b[:], ALU.subtract), b1)
                    m0 = V(lambda e: e.memset(mrow[:, 0:1], NEG))
                    prev = [s1, m0]
                    for c in range(ST):
                        sl = slice(c * P, (c + 1) * P)
                        sc1 = V(lambda e, sl=sl, c=c: e.tensor_tensor_scan(M[:, sl], li[:, sl], li[:, sl],
                                                                         mrow[:, c:c + 1], ALU.max, ALU.max), prev)
                        prev = [V(lambda e, c=c: e.tensor_tensor(mrow[:, c + 1:c + 2], b[:, c * P + P - 1:c * P + P],
                                                                 M[:, c * P + P - 1:c * P + P], ALU.add), sc1)]
                    b3 = b[:].rearrange("p (c t) -> p c t", c=ST)
                    a3d = li[:].rearrange("p (c t) -> p c t", c=ST)
                    M3 = M[:].rearrange("p (c t) -> p c t", c=ST)
                    T1 = t1[:].rearrange("p (c t) -> p c t", c=ST)
                    T2 = t2[:].rearrange("p (c t) -> p c t", c=ST)
                    LF3 = lf[:].rearrange("p (c t) -> p c t", c=ST)
                    mp = mrow[:, 0:ST].unsqueeze(2).to_broadcast([R, ST, P])
                    me = M3[:, :, P - 1:P].to_broadcast([R, ST, P])
                    w1 = V(lambda e: e.tensor_tensor(T1, mp, M3, ALU.subtract), prev)
                    w2 = V(lambda e: e.tensor_tensor(LF3, a3d, me, ALU.subtract), prev)
                    w3 = V(lambda e: e.tensor_tensor(t2[:], b[:], M[:], ALU.add), prev)
                    w4 = V(lambda e: e.tensor_scalar(t2[:], t2[:], -1.0, EXP_CAP, ALU.mult, ALU.min), w3)
                    w5 = V(lambda e: e.tensor_tensor(dec[:].unsqueeze(2), mrow[:, 0:ST].unsqueeze(2), M3[:, :, P - 1:P],
                                                     ALU.subtract), prev)
                    e5 = A(lambda e: e.activation(dec[:], dec[:], ACT.Exp), w5)
                    outs = []
                    for r0, r1_, rv in ((0, 32, 1), (32, 36, -1)):
                        s_ = slice(r0, r1_)
                        o_ = slice(64 + r0, 64 + r1_)

                        def dirn(t, rows, rv=rv):
                            return t[rows, :] if rv == 1 else t[rows, ::-1]
                        outs.append(A(lambda e, s_=s_, o_=o_, d=dirn: e.activation(d(QA, o_), t1[s_, :], ACT.Exp), w1, q0))
                        outs.append(A(lambda e, s_=s_, o_=o_, d=dirn: e.activation(d(QB, o_), lf[s_, :], ACT.Exp), w2, q0))
                        outs.append(A(lambda e, s_=s_, d=dirn: e.activation(d(QB, s_), t2[s_, :], ACT.Exp), w4, q0))
                        outs.append(V(lambda e, s_=s_, d=dirn: e.tensor_copy(d(QA, s_), li[s_, :]), q0, prev))
                        outs.append(V(lambda e, s_=s_, d=dirn: e.tensor_scalar(d(nm, s_), M[s_, :], -1.0, None, ALU.mult),
                                      prev))
                    colr = []
                    for src, dst in ((QA, colsA), (QB, colsB)):
                        p = take()
                        for c in range(ST):
                            mm = T(lambda e, c=c, p=p, src=src: e.transpose(p.full[:, c * P:(c + 1) * P],
                                                                          src[:, c * P:(c + 1) * P], ident), outs, p.read)
                        d = A(lambda e, p=p, dst=dst: e.activation(dst[:].rearrange("p a b -> p (a b)"), p.full,
                                                                  ACT.Identity), mm)
                        p.read = [d]
                        colr.append(d)
                    dx = V(lambda e: e.tensor_tensor(dex[:], ident[0:R, 0:R].unsqueeze(2).to_broadcast([R, R, ST]),
                                                     dec[:].unsqueeze(1).to_broadcast([R, R, ST]), ALU.mult), e5)
                    p = take()
                    mm = T(lambda e, p=p: e.matmul(p.full[:, 0:R * ST], ones[0:R, :], dex[:].rearrange("p a b -> p (a b)"),
                                                   start=True, stop=True), dx, tabs, p.read)
                    dd = []
                    for h in range(M_HEADS):
                        for dr in range(2):
                            row = 32 * dr + h
                            hp = slice(64 * (h % 2), 64 * (h % 2) + 64)
                            dd.append(V(lambda e, h=h, dr=dr, row=row, hp=hp, p=p: e.tensor_copy(
                                decB[hp, h // 2, dr, :], p.full[hp, row * ST:(row + 1) * ST]), mm))
                    p.read = [dd[-1]]
                q.fence()
                q.stage("mlstm")
                ktok = sb("ml_ktok", [P, ST, 256], F32, sc)
                E = [[sb(f"ml_E{i}{d}", [P, ST, P], F32, sc) for d in range(2)] for i in range(2)]
                kw = [sb(f"ml_kw{i}", [P, ST, M_QK], F32, sc) for i in range(2)]
                C = sb("ml_C", [P, 2, ST, M_V + 1], F32, sc)
                hs = sb("ml_hs", [P, ST, 512], F32, sc)
                num = sb("ml_num", [P, 4, M_V + 1], F32, sc)
                dn = sb("ml_den", [P, 16], F32, sc)
                kt_done = []
                for hp in range(2):
                    p = take()
                    for c in range(ST):
                        mm = T(lambda e, c=c, p=p, hp=hp: e.transpose(p.full[:, c * P:(c + 1) * P],
                                                                    qk[:, 2 + hp, c * P:(c + 1) * P], ident), qk_in, p.read)
                    d = A(lambda e, p=p, hp=hp: e.activation(ktok[:, :, hp * P:(hp + 1) * P],
                                                             p.full.rearrange("p (c k) -> p c k", c=ST), ACT.Identity), mm)
                    p.read = [d]
                    kt_done.append(d)
                zC = V(lambda e: e.memset(C[:, :, 0, :], 0.0))
                e_free = [[None, None], [None, None]]
                kw_free = [None, None]
                c_free = [None, None]
                num_free, hs_last = None, {}
                def head(h):
                    nonlocal num_free
                    i, pr_, lo = h % 2, h // 2, 64 * (h % 2)
                    part = slice(lo, lo + 64)
                    ed = []
                    for dr in range(2):
                        row = 32 * dr + h
                        p = take()
                        hd = dr * 4 + h
                        for hf in range(2):
                            mm = T(lambda e, p=p, hf=hf, hd=hd: e.matmul(p.half[hf], sel[:, hd * P:(hd + 1) * P],
                                                                       nm[:, hf * HALF:(hf + 1) * HALF], start=True,
                                                                       stop=True), p.read)
                        Et = E[i][dr]
                        x1 = V(lambda e, p=p, Et=Et, row=row: e.tensor_tensor(
                            Et[:], p.full.rearrange("p (c t) -> p c t", c=ST),
                            colsA[:, :, row:row + 1].to_broadcast([P, ST, P]), ALU.add), mm, colr, e_free[i][dr])
                        p.read = [x1]
                        mk = causal if dr == 0 else anti
                        x2 = V(lambda e, Et=Et, mk=mk: e.tensor_tensor(
                            Et[:], Et[:], mk.unsqueeze(1).to_broadcast([P, ST, P]), ALU.add), x1)
                        ed.append(A(lambda e, Et=Et: e.activation(Et[:], Et[:], ACT.Exp), x2))
                    p = take()
                    for c in range(ST):
                        mm = T(lambda e, p=p, c=c: e.matmul(p.full[:, c * P:(c + 1) * P],
                                                            qk[part, 2 + pr_, c * P:(c + 1) * P],
                                                            qk[part, pr_, c * P:(c + 1) * P], start=True, stop=True),
                               p.read, qk_in)
                    st_ = []
                    for dr in range(2):
                        Et = E[i][dr]
                        st_.append(V(lambda e, p=p, Et=Et: e.tensor_tensor(
                            Et[:], Et[:], p.full.rearrange("p (c t) -> p c t", c=ST), ALU.mult), ed[dr], mm))
                    p.read = [st_[1]]
                    cd = []
                    for dr in range(2):
                        row = 32 * dr + h
                        kwt = kw[dr]
                        kd = V(lambda e, kwt=kwt, row=row, h=h: e.tensor_tensor(
                            kwt[:], ktok[:, :, h * 64:(h + 1) * 64],
                            colsB[:, :, 64 + row:64 + row + 1].to_broadcast([P, ST, M_QK]), ALU.mult), kt_done, kw_free[dr],
                            colr)
                        last = zC
                        for j0 in (0, 4):
                            p = take()
                            for j in range(j0, min(j0 + 4, ST - 1)):
                                c = j if dr == 0 else ST - 1 - j
                                mm = T(lambda e, p=p, j=j, c=c, kwt=kwt: e.matmul(
                                    p.full[part, (j % 4) * 256:(j % 4) * 256 + M_V + 1], kwt[:, c, :], v1[:, c, h, :],
                                    start=True, stop=True), kd, v_in, v_one, p.read)
                            kw_free[dr] = mm
                            for j in range(j0, min(j0 + 4, ST - 1)):
                                last = V(lambda e, p=p, j=j, dr=dr: e.scalar_tensor_tensor(
                                    out=C[part, dr, j + 1, :], in0=C[part, dr, j, :],
                                    scalar=decB[part, pr_, dr, j:j + 1],
                                    in1=p.full[part, (j % 4) * 256:(j % 4) * 256 + M_V + 1],
                                    op0=ALU.mult, op1=ALU.add), mm, last, c_free[h % 2])
                            p.read = [last]
                        cd.append(last)
                    for dr in range(2):
                        row = 32 * dr + h
                        for c0 in (0, 4):
                            pl = take()
                            for c in range(c0, c0 + 4):
                                ml = T(lambda e, pl=pl, c=c, dr=dr: e.matmul(
                                    pl.full[:, (c % 4) * 256:(c % 4) * 256 + M_V + 1], E[i][dr][:, c, :], v1[:, c, h, :],
                                    start=True, stop=True), st_[dr], pl.read)
                            pi = take()
                            for c in range(c0, c0 + 4):
                                j = c if dr == 0 else ST - 1 - c
                                mi = T(lambda e, pi=pi, c=c, dr=dr, j=j: e.matmul(
                                    pi.full[:, (c % 4) * 256:(c % 4) * 256 + M_V + 1], qk[part, pr_, c * P:(c + 1) * P],
                                    C[part, dr, j, :], start=True, stop=True), cd[dr], pi.read)
                            pi3 = pi.full.rearrange("p (c v) -> p c v", c=4)[:, :, 0:M_V + 1]
                            pl3 = pl.full.rearrange("p (c v) -> p c v", c=4)[:, :, 0:M_V + 1]
                            n1 = V(lambda e, pi3=pi3, c0=c0, row=row: e.tensor_tensor(
                                num[:], pi3, colsA[:, c0:c0 + 4, 64 + row:64 + row + 1].to_broadcast([P, 4, M_V + 1]),
                                ALU.mult), mi, num_free)
                            pi.read = [n1]
                            n2 = V(lambda e, pl3=pl3: e.tensor_tensor(num[:], num[:], pl3, ALU.add), n1, ml)
                            pl.read = [n2]
                            n3 = A(lambda e: e.activation(dn[:, 0:4].unsqueeze(2), num[:, :, M_V:M_V + 1], ACT.Abs), n2)
                            n4 = V(lambda e, c0=c0, row=row: e.tensor_tensor(
                                dn[:, 4:8].unsqueeze(2), dn[:, 0:4].unsqueeze(2), colsB[:, c0:c0 + 4, row:row + 1],
                                ALU.max), n3)
                            n5 = V(lambda e: e.reciprocal(dn[:, 8:12], dn[:, 4:8]), n4)
                            rb = dn[:, 8:12].unsqueeze(2).to_broadcast([P, 4, M_V])
                            dst = hs[:, c0:c0 + 4, h * M_V:(h + 1) * M_V]
                            if dr == 0:
                                n6 = V(lambda e, dst=dst, rb=rb: e.tensor_tensor(dst, num[:, :, 0:M_V], rb, ALU.mult), n5)
                            else:
                                n5 = V(lambda e, rb=rb: e.tensor_tensor(num[:, :, 0:M_V], num[:, :, 0:M_V], rb, ALU.mult), n5)
                                n6 = V(lambda e, dst=dst: e.tensor_tensor(dst, dst, num[:, :, 0:M_V], ALU.add), n5)
                            num_free = n6
                            hs_last[(h, c0)] = n6
                        e_free[i][dr] = ml
                    c_free[h % 2] = mi
                for h in range(M_HEADS):
                    head(h)
                q.fence()
                sq = E[0][0][:].rearrange("p a b -> p (a b)")
                ss = dn
                st = Store("ml_o", 2, sc)
                mo = [E[1][0][:].rearrange("p a b -> p (a b)"), E[1][1][:].rearrange("p a b -> p (a b)")]
                s_mo = [q.sem(f"ml_mo_loaded{i}") for i in range(2)]
                ss = sb("ml_ss", [P, 3, ST * M_HEADS], F32, sc)
                for c in range(ST):
                    sqt = sq[:, 0:HALF] if c % 2 == 0 else sq[:, HALF:S]
                    s1 = A(lambda e, c=c, sqt=sqt: e.activation(sqt, hs[:, c, :], ACT.Square),
                           [s2] if c >= 2 else None)
                    if c >= 1:
                        s2_prev = s2
                    s2 = V(lambda e, c=c, sqt=sqt: e.tensor_reduce(
                        ss[:, 0, c * M_HEADS:(c + 1) * M_HEADS], sqt.rearrange("p (h v) -> p h v", h=M_HEADS), AX.X,
                        ALU.add), s1)
                s3 = V(lambda e: e.tensor_scalar(ss[:, 0, :], ss[:, 0, :], 1.0 / M_V, None, ALU.mult), s2)
                rd, _ = rsqrt(ss[:, 0, :], eps[:, 0:1], ss[:, 1, :], ss[:, 2, :], s3)
                hn = []
                for c in range(ST):
                    hv = hs[:, c, :].rearrange("p (h v) -> p h v", h=M_HEADS)
                    hn.append(V(lambda e, c=c, hv=hv: e.tensor_tensor(
                        hv, hv, ss[:, 1, c * M_HEADS:(c + 1) * M_HEADS].unsqueeze(2).to_broadcast([P, M_HEADS, M_V]),
                        ALU.mult), rd))
                mo_free = [None, None]
                for h in range(M_HEADS):
                    ld = q.dma(s_mo[h % 2], mo[h % 2], proj[12 + h], spilled[("proj", 12 + h)], mo_free[h % 2])
                    p = take()
                    for c in range(ST):
                        mm = T(lambda e, p=p, c=c, h=h: e.transpose(p.full[:, c * P:(c + 1) * P],
                                                                   hs[:, c, h * M_V:(h + 1) * M_V], ident), hn[c], p.read)
                    t, fr = st.next()
                    d = V(lambda e, p=p, t=t, h=h: e.scalar_tensor_tensor(out=t[:], in0=p.full, scalar=vc("g_mh", h),
                                                                        in1=mo[h % 2], op0=ALU.mult, op1=ALU.mult),
                          mm, ld, fr)
                    p.read = [d]
                    mo_free[h % 2] = d
                    st.store(mixd[h], ("mix", h), d)
                return st.all()

        def layer_norm(name, write, last=False):
            with ExitStack() as sc:
                xc = sb(f"{name}_xc", [P, KT, S], F32, sc)
                sq = [sb(f"{name}_sq{i}", [P, S], F32, sc) for i in range(2)]
                r = sb(f"{name}_r", [P, S], F32, sc)
                u = sb(f"{name}_u", [P, S], F32, sc)
                p, mm = mean_over_features(mean1024, lambda k: x[:, k, :], KT, lambda k: x_ready[k], lambda k, m: None)
                xd = [V(lambda e, k=k, p=p: e.tensor_tensor(xc[:, k, :], x[:, k, :], p.full, ALU.subtract), mm, x_ready[k])
                      for k in range(KT)]
                p.read = [xd[-1]]
                sf, sqd = [None, None], {}

                def ready(k):
                    if k not in sqd:
                        sqd[k] = A(lambda e: e.activation(sq[k % 2][:], xc[:, k, :], ACT.Square), xd[k], sf[k % 2])
                    return sqd[k]

                def free(k, m):
                    sf[k % 2] = m

                p, mm = mean_over_features(mean1024, lambda k: sq[k % 2], KT, ready, free)
                rd, pr_ = rsqrt(p.full, eps[:, 1:2], r[:], u[:], mm)
                p.read = [pr_]
                return [write(k, xc[:, k, :], r[:], rd) for k in range(KT)]

        def block2(l):
            q.stage(f"proj2_{l}")
            q.fence()
            mo = l * N_ADA2 * KT
            c1 = V(lambda e: e.tensor_scalar(cols[:, 24:32], mod2[:, mo + 8:mo + 16], 1.0, None, ALU.add),
                   [mod_done[(l + 1, i)] for i in range(3)])
            c2 = V(lambda e: e.tensor_scalar(cols[:, 32:40], mod2[:, mo + 16:mo + 24], 1.0, None, ALU.add))
            c3 = V(lambda e: e.tensor_scalar(cols[:, 16:17], vc("q_gain_2", l), A_DIM ** -0.5, None, ALU.mult))
            with ExitStack() as hs:
                h = [sb(f"h2{l}_hi", [P, KT, S], F32R, hs), sb(f"h2{l}_lo", [P, KT, S], F32R, hs)]

                def write(k, xc, r, rd):
                    td = V(lambda e: e.scalar_tensor_tensor(out=xc, in0=xc, scalar=cols[:, 24 + k:25 + k], in1=r,
                                                            op0=ALU.mult, op1=ALU.mult), rd, c1)
                    return split_shifted(xc, mod2[:, mo + k:mo + k + 1], h[0][:, k, :], h[1][:, k, :], td)

                ready = layer_norm(f"ln{l}", write)
                q.fence()
                hi, lo = (lambda k: h[0][:, k, :]), (lambda k: h[1][:, k, :])
                with ExitStack() as sc:
                    cst = sb(f"r2cos{l}", [P, S], F32, sc)
                    snt = sb(f"r2sin{l}", [P, S], F32, sc)
                    m2 = sb(f"r2mats{l}", [P, 2 * P], F32, sc)
                    s_t = q.sem(f"rope2_loaded{l}")
                    q.dma(s_t, cst[:], ins["rope2"][0])
                    q.dma(s_t, snt[:], ins["rope2"][1])
                    q.dma(s_t, m2[:, 0:P], ins["mats"][MAT["mean64"]])
                    tables = q.dma(s_t, m2[:, P:2 * P], ins["mats"][MAT["rot2"]])
                    st = Store(f"p2{l}_o", 2, sc)
                    tmps = [[sb(f"p2{l}_{n}{i}", [P, S], F32, sc)[:] for n in ("raw", "sq", "r", "u")] + [None]
                            for i in range(2)]
                    pending = []
                    for b in range(3):
                        blk = get(("in2", l, b))
                        for m in range(2):
                            nt = 2 * b + m
                            p, mm = gemm(blk, m, KT, hi, lo, ready)
                            step(pending)
                            if nt < 5:
                                gc = cols[:, 16:17] if nt < 4 else vc("k_gain_2", l)
                                pending.append(rope_heads(st, tmps[nt % 2], m2[:, 0:P], m2[:, P:2 * P], cst[:], snt[:], gc,
                                                          ("proj", nt), proj[nt], [tables, c3], p, mm, nt))
                                next(pending[-1])
                            else:
                                while pending:
                                    step(pending)
                                t, fr = st.next()
                                d = A(lambda e, p=p, t=t: e.activation(t[:], p.full, ACT.Identity), mm, fr)
                                p.read = [d]
                                st.store(proj[5], ("proj", 5), d)
                    done = st.all()
                q.fence(done)
                with ExitStack() as sc:
                    st = Store(f"p2b{l}_o", 4, sc)
                    cu = sb(f"cu{l}", [P, S], F32, sc)
                    uu = sb(f"cuu{l}", [P, S], F32, sc)
                    ac = sb(f"cac{l}", [P, S], F32, sc)
                    conv_free = None
                    for b in range(3, 11):
                        blk = get(("in2", l, b))
                        for m in range(2):
                            nt = 2 * b + m
                            p, mm = gemm(blk, m, KT, hi, lo, ready)
                            if nt < 14:
                                t, fr = st.next()
                                fn = ACT.Identity if nt < 8 else ACT.Silu
                                d = A(lambda e, p=p, t=t, fn=fn: e.activation(t[:], p.full, fn), mm, fr)
                                p.read = [d]
                                st.store(proj[nt], ("proj", nt), d)
                                continue
                            what, tile = (nt - 14) % 4, (nt - 14) // 4

                            def w(j, tile=tile):
                                return vc("conv_w", (l * 3 + j) * 2 + tile)
                            if what == 0:
                                v0 = A(lambda e, p=p: e.activation(cu[:], p.full, ACT.Identity), mm, conv_free)
                                p.read = [v0]
                            elif what == 1:
                                v1_ = V(lambda e, p=p: e.tensor_tensor(uu[:], cu[:], p.full, ALU.mult), v0, mm)
                                p.read = [v1_]
                                v2 = V(lambda e, w=w: e.tensor_scalar(ac[:], uu[:], w(1), None, ALU.mult), v1_)
                                v3 = V(lambda e, w=w: e.scalar_tensor_tensor(out=ac[:, 1:S], in0=uu[:, 0:S - 1], scalar=w(0),
                                                                             in1=ac[:, 1:S], op0=ALU.mult, op1=ALU.add), v2)
                                v4 = V(lambda e, w=w: e.scalar_tensor_tensor(out=ac[:, 0:S - 1], in0=uu[:, 1:S], scalar=w(2),
                                                                             in1=ac[:, 0:S - 1], op0=ALU.mult, op1=ALU.add),
                                       v3)
                            elif what == 2:
                                v5 = V(lambda e, p=p: e.tensor_tensor(ac[:], ac[:], p.full, ALU.mult), v4, mm)
                                p.read = [v5]
                            else:
                                v6 = A(lambda e, p=p: e.activation(cu[:], p.full, ACT.Silu), mm, v1_)
                                p.read = [v6]
                                t, fr = st.next()
                                conv_free = V(lambda e, t=t: e.tensor_tensor(t[:], ac[:], cu[:], ALU.mult), v5, v6, fr)
                                st.store(mixd[4 + tile], ("mix", 4 + tile), conv_free)
                    done = st.all()
            q.fence(done)
            done = attention(f"attn2_{l}", lambda hq: hq // 4, None, 10, 0)
            q.fence(done)
            done = fourier(l)
            q.stage(f"out2_{l}")
            q.fence(done)
            with ExitStack() as hs:
                h = [sb(f"mix2{l}_hi", [P, KT, S], F32R, hs), sb(f"mix2{l}_lo", [P, KT, S], F32R, hs)]
                xa = [V(lambda e, k=k: e.tensor_scalar(x[:, k, :], x[:, k, :], ALPHA, None, ALU.mult)) for k in range(KT)]
                ready = load_mix(f"mix2{l}", h)
                for c in range(4):
                    blk = get(("out2", l, c))
                    for m in range(2):
                        d = 2 * c + m
                        p, mm = gemm(blk, m, KT, lambda k: h[0][:, k, :], lambda k: h[1][:, k, :], ready)
                        x_ready[d] = V(lambda e, p=p, d=d: e.scalar_tensor_tensor(
                            out=x[:, d, :], in0=p.full, scalar=cols[:, 32 + d:33 + d], in1=x[:, d, :],
                            op0=ALU.mult, op1=ALU.add), mm, xa[d], c2)
                        p.read = [x_ready[d]]
            q.fence()

            def write(k, xc, r, rd):
                td = V(lambda e: e.tensor_tensor(xc, xc, r, ALU.mult), rd)
                x_ready[k] = V(lambda e: e.tensor_scalar(x[:, k, :], xc, vc("ln_g", l * 8 + k), vc("ln_b", l * 8 + k),
                                                         ALU.mult, ALU.add), td)
                return x_ready[k]
            layer_norm(f"lno{l}", write)

        def fourier(l):
            q.stage(f"fourier{l}")
            with ExitStack() as sc:
                cm = sb(f"fo{l}_mats", [P, 4 * P], F32, sc)
                ab = sb(f"fo{l}_ab", [P, 2, 2 * P], F32, sc)
                fu = sb(f"fo{l}_u", [P, 2, S], F32, sc)
                gf = sb(f"fo{l}_g", [P, 2, S], F32, sc)
                uh = sb(f"fo{l}_uhi", [P, 2, ST, 256], F32R, sc)
                ul = sb(f"fo{l}_ulo", [P, 2, ST, 256], F32R, sc)
                t = [sb(f"fo{l}_t{i}", [P, S], F32, sc) for i in range(2)]
                o = sb(f"fo{l}_out", [P, 2, S], F32, sc)
                s_c, s_u, s_g = q.sem(f"fo{l}_consts"), q.sem(f"fo{l}_uload"), q.sem(f"fo{l}_gload")
                for j, n in enumerate(("cosc", "sinc", f"fm{l}0", f"fm{l}1")):
                    cin = q.dma(s_c, cm[:, j * P:(j + 1) * P], ins["mats"][MAT[n]])
                for j in range(2):
                    u_in = q.dma(s_u, fu[:, j, :], proj[6 + j], spilled[("proj", 6 + j)])
                    g_in = q.dma(s_g, gf[:, j, :], proj[8 + j], spilled[("proj", 8 + j)])
                p = take()
                for g in range(2):
                    for j in range(2):
                        mm = T(lambda e, g=g, j=j, p=p: e.matmul(p.half[g][:, j * P:(j + 1) * P], cm[:, j * P:(j + 1) * P],
                                                                cm[:, (2 + g) * P:(3 + g) * P], start=True, stop=True),
                               cin, p.read)
                abd = A(lambda e, p=p: e.activation(ab[:], p.full.rearrange("p (g c) -> p g c", g=2)[:, :, 0:256],
                                                    ACT.Identity), mm)
                p.read = [abd]
                ud = []
                tf = [None, None]
                for g in range(2):
                    for t0 in (0, 4):
                        p = take()
                        for j in range(4):
                            mm = T(lambda e, g=g, j=j, p=p, t0=t0: e.matmul(
                                p.full[:, j * 256:(j + 1) * 256], fu[:, g, (t0 + j) * P:(t0 + j + 1) * P], ab[:, g, :],
                                start=True, stop=True), abd, u_in, p.read)
                        hi = uh[:, g, t0:t0 + 4, :].rearrange("p a b -> p (a b)")
                        lo = ul[:, g, t0:t0 + 4, :].rearrange("p a b -> p (a b)")
                        up = A(lambda e, p=p, hi=hi: e.activation(hi, p.full, ACT.Identity), mm)
                        dn = V(lambda e, p=p, hi=hi, lo=lo: e.tensor_tensor(lo, p.full, hi.bitcast(F32), ALU.subtract), up)
                        p.read = [dn]
                        ud.append(dn)
                for c in range(4):
                    p = None
                    for tb in range(2):
                        s, whi, wlo, wdone = get(("dft", l, c, tb))
                        if p is None:
                            p = take()
                        for g in range(2):
                            for k in range(ST):
                                for i, (a, b) in enumerate(((whi, uh), (whi, ul), (wlo, uh))):
                                    mm = T(lambda e, a=a, b=b, k=k, g=g, tb=tb, i=i, p=p: e.matmul(
                                        p.half[g][:, 0:256], b[:, g, k, tb * P:(tb + 1) * P], a[:, k * 256:(k + 1) * 256],
                                        start=(tb == 0 and k == 0 and i == 0), stop=(tb == 1 and k == ST - 1 and i == 2)),
                                        wdone, ud, p.read if tb == 0 else None)
                        W.used(s, mm)
                    res = p.full.rearrange("p (g c) -> p g c", g=2)[:, :, 0:256]
                    d = V(lambda e, res=res, c=c: e.tensor_tensor(o[:, :, c * 256:(c + 1) * 256], res,
                                                                  gf[:, :, c * 256:(c + 1) * 256], ALU.mult), mm, g_in)
                    p.read = [d]
                s_o = q.sem(f"fo{l}_stored")
                a1 = q.dma(s_o, mixd[6], o[:, 0, :], d)
                a2 = q.dma(s_o, mixd[7], o[:, 1, :])
                spilled[("mix", 6)] = a2
                spilled[("mix", 7)] = a2
                return [a2]

        def finish():
            s_out = q.sem("out_stored")
            for k in range(KT):
                fin = q.dma(s_out, out[:, k, :], x[:, k, :], x_ready[k], queue="sync")
            return fin

        def final_norm():
            q.stage("final1")
            q.fence()
            with ExitStack() as sc:
                r, rd = rms_stats(sc, "fin")
                for k in range(KT):
                    x_ready[k] = V(lambda e, k=k: e.scalar_tensor_tensor(out=x[:, k, :], in0=x[:, k, :],
                                                                        scalar=vc("g_final", k), in1=r[:], op0=ALU.mult,
                                                                        op1=ALU.mult), rd)

        stages = [("ffn1", lambda: ffn(1, 2)), ("mixer1", mixer1), ("ffn2", lambda: ffn(2, 8)), ("final", final_norm),
                  ("b0", lambda: block2(0)), ("b1", lambda: block2(1))]
        for name, run in stages:
            run()
            if name == "ffn2":
                while W.taken < len(plan) and plan[W.taken][0] == "ada":
                    W.advance()
                    ada_finish()
            if name == stop:
                break
        q.end = finish()
        q.emit(ctx.enter_context(nc.Block()))



def tiles(w, width=256, cols=None):
    if cols is not None:
        w = np.concatenate([w, np.zeros((w.shape[0], 1), w.dtype)], 1)[:, cols]
    k, n = w.shape
    return np.ascontiguousarray(w.reshape(k // P, P, n // width, width).transpose(2, 1, 0, 3)
                                .reshape(n // width, P, -1))


def shape_constants():
    f = np.float32
    m = {}
    m["mean1024"] = np.full((P, P), 1 / 1024, f)
    blk = np.kron(np.eye(2), np.ones((64, 64)))
    m["mean64"] = (blk / 64).astype(f)
    m["mean128"] = np.full((P, P), 1 / 128, f)
    m["ones"] = np.ones((P, P), f)
    m["ident"] = np.eye(P, dtype=f)
    r1 = np.zeros((64, 64), f)
    for d in range(8):
        r1[d + 8, d] = -1.0
        r1[d, d + 8] = 1.0
    m["rot1"] = np.kron(np.eye(2), r1).astype(f)
    r2 = np.zeros((64, 64), f)
    for h in (0, 32):
        for d in range(16):
            r2[h + d + 16, h + d] = -1.0
            r2[h + d, h + d + 16] = 1.0
    m["rot2"] = np.kron(np.eye(2), r2).astype(f)
    ang = 2 * np.pi * np.outer(np.arange(64), np.arange(64)) / 64
    m["cosc"] = np.kron(np.eye(2), np.cos(ang)).astype(f)
    m["sinc"] = np.kron(np.eye(2), np.sin(ang)).astype(f)
    i = np.arange(P)
    m["causal"] = np.where(i[:, None] <= i[None, :], 0.0, NEG).astype(f)
    m["anti"] = np.where(i[:, None] >= i[None, :], 0.0, NEG).astype(f)
    t = 2 * np.pi * (np.outer(np.arange(S), np.arange(S)) % S) / S
    dft = np.stack([np.cos(t) / 256, -np.sin(t) / 256]).astype(f).reshape(2, KT, P, S)
    inv1 = (f(500000.0) ** (f(-2.0) * np.arange(8, dtype=f) / f(16))).astype(f)
    a1 = (np.arange(S, dtype=f)[:, None] * inv1[None, :]).astype(f)
    c1, s1 = np.ones((64, S), f), np.zeros((64, S), f)
    for d in range(16):
        c1[d], s1[d] = np.cos(a1[:, d % 8]), np.sin(a1[:, d % 8])
    inv2 = (f(1.0) / (f(10000.0) ** (np.arange(0, 32, 2, dtype=f) / f(32)))).astype(f)
    row = np.repeat(np.arange(S // 64, dtype=f), 64)[:, None] * inv2
    col = np.tile(np.arange(64, dtype=f), S // 64)[:, None] * inv2
    c2, s2 = np.zeros((64, S), f), np.zeros((64, S), f)
    for d in range(64):
        a = (row if d < 32 else col)[:, d % 16]
        c2[d], s2[d] = np.cos(a), np.sin(a)
    rope1 = np.stack([np.tile(c1, (2, 1)), np.tile(s1, (2, 1))])
    rope2 = np.stack([np.tile(c2, (2, 1)), np.tile(s2, (2, 1))])
    j = np.abs(np.arange(1920)[None, :] - 896 - np.arange(P)[:, None])
    count = (j <= 64).astype(int) + ((j % 4 == 0) & (j <= 256)) + (j % 16 == 0)
    band = np.where(count > 0, np.log(np.maximum(count, 1)), NEG).astype(f)
    sel = np.zeros((36, 8, P), f)
    for d in range(2):
        for h in range(4):
            sel[32 * d + h, d * 4 + h] = 1.0
    reset = np.ones((36, S), f)
    reset[:, ::P] = 0.0
    return m, dft, rope1, rope2, band, sel.reshape(36, -1), reset


def layouts(i):
    a = {k: np.asarray(v) for k, v in i.items()}
    m, dft, rope1, rope2, band, sel, reset = shape_constants()
    for l in range(2):
        for g in range(2):
            z = np.zeros((P, P), np.float32)
            z[0:64, 0:64] = a["f_mix_2"][l, 2 * g]
            z[64:, 64:] = a["f_mix_2"][l, 2 * g + 1]
            m[f"fm{l}{g}"] = z
    vec = np.zeros((P, NVEC), np.float32)

    def put(name, v):
        o, n = VEC[name]
        vec[:, o:o + n] = v

    def colsof(v):
        return v.reshape(-1, P).T

    put("c", colsof(a["c"]))
    put("b_ada", colsof(a["b_ada"]))
    for n in ("g_ffn1", "g_mix", "g_ffn2", "g_final", "g_mh"):
        put(n, colsof(a[n]))
    put("g_q", np.tile(a["g_q"][0], 2)[:, None])
    put("g_k", np.tile(a["g_k"][0], 2)[:, None])
    put("c_2", colsof(a["c_2"]))
    put("b_ada_2", colsof(a["b_ada_2"]))
    put("q_gain_2", np.tile(a["q_gain_2"], (1, 2)).T)
    put("k_gain_2", np.tile(a["k_gain_2"], (1, 2)).T)
    put("conv_w", a["conv_w_2"].reshape(-1, P).T)
    put("ln_g", colsof(a["ln_g_2"]))
    put("ln_b", colsof(a["ln_b_2"]))
    gb = a["gate_bias"][0]
    o = VEC["gate_bias"][0]
    for r0, g in ((0, 0), (32, 2), (64, 1), (96, 3)):
        vec[r0:r0 + 4, o] = gb[g]

    w = a["w_in"][0]
    R = np.arange
    mq, mk, mv, mo, mg = R(0, 256), R(256, 512), R(512, 1024), R(1024, 1536), R(1536, 1552)
    aq, ak, av = R(1552, 2064), R(2064, 2576), R(2576, 3088)
    gate_cols = np.full(P, -1)
    for r0, g in ((0, 0), (32, 2), (64, 1), (96, 3)):
        gate_cols[r0:r0 + 4] = mg[4 * g:4 * g + 4]
    sizes = (512, 128, 128, 512, 256, 256, 256, 256, 256, 256)
    st = np.cumsum((0,) + sizes)
    Q, K, V_, GA, CU, CB, CC, GC, FU, GF = (R(st[n], st[n + 1]) for n in range(10))
    h = [slice(0, P), slice(P, 256)]
    order2 = np.concatenate([Q, K, V_, FU, GF, GA] + [x_[s_] for s_ in h for x_ in (CU, CC, CB, GC)])
    gu = []
    for n in (1, 2):
        g = a[f"w_gu{n}"][0].reshape(KT, P, 2, FF_TILES, P).transpose(3, 1, 0, 2, 4)
        gu.append(np.ascontiguousarray(g).reshape(FF_TILES, P, BLK))
    return {"in_" + n: v for n, v in {
        "xT": np.ascontiguousarray(a["x"][0].T.reshape(KT, P, S).transpose(1, 0, 2)),
        "vec": vec, "mats": np.stack([m[n] for n in MATS]), "dft": dft, "rope1": rope1, "rope2": rope2,
        "band": band, "sel": sel, "reset": reset,
        "w_ada": a["w_ada"][0], "w_ada_2": a["w_ada_2"],
        "w_gu1": gu[0], "w_gu2": gu[1],
        "w_down1": a["w_down1"][0].reshape(FF_TILES, P, D), "w_down2": a["w_down2"][0].reshape(FF_TILES, P, D),
        "w_in": tiles(w, cols=np.concatenate([aq, ak, av, mv, mq, mk, mo])),
        "w_in_gate": tiles(w, P, gate_cols)[0],
        "w_out": a["w_out"][0].reshape(KT, P, D),
        "w_in_2": np.stack([tiles(a["w_in_2"][l], cols=order2) for l in range(2)]),
        "w_out_2": a["w_out_2"].reshape(2, KT, P, D),
    }.items()}


def program(nc, arrays, stop=None):
    ins = {}
    for n, v in arrays.items():
        ins[n[3:]] = nc.dram_tensor(n, list(v.shape), mybir.dt.from_np(v.dtype), kind="ExternalInput").ap()
    out = nc.dram_tensor("out", [P, KT, S], F32, kind="ExternalOutput").ap()
    build(nc, ins, out, stop)


def kernel(**inputs):
    import concourse.bacc as bacc
    from concourse.bass_utils import run_bass_kernel_spmd

    arrays = layouts(inputs)
    nc = bacc.Bacc("TRN2", target_bir_lowering=False, num_devices=1)
    program(nc, arrays)
    res = run_bass_kernel_spmd(nc, [arrays], core_ids=[0])
    y = np.asarray(res.results[0]["out"])
    return np.ascontiguousarray(y.transpose(1, 0, 2).reshape(D, S).T)[None]
```

```python
from contextlib import ExitStack

import numpy as np

import concourse.bass as bass
from concourse import mybir

F32 = mybir.dt.float32
F32R = mybir.dt.float32r
ALU = mybir.AluOpType
ACT = mybir.ActivationFunctionType
AX = mybir.AxisListType

P = 128
S = 1024
D = 1024
KT = D // P
ST = S // P
HALF = 512
EPS = 1e-6
LN_EPS = 1e-5
NEG = -1e30
FF_TILES = 22
FF_GROUPS = (5, 5, 4, 4, 4)
A_SLOTS = 6
RAW = 2
BLK = 2048
M_HEADS, M_QK, M_V = 4, 64, 128
A_HEADS, A_DIM = 8, 64
EXP_CAP = 88.0
ALPHA = 4.0 ** 0.25
N_ADA1, N_ADA2 = 9, 3

VEC = {}
_at = 0
for _name, _n in (("c", 8), ("b_ada", 72), ("g_ffn1", 8), ("g_mix", 8), ("g_ffn2", 8), ("g_final", 8),
                  ("g_mh", 4), ("g_q", 1), ("g_k", 1), ("c_2", 8), ("b_ada_2", 48), ("q_gain_2", 2),
                  ("k_gain_2", 2), ("conv_w", 12), ("ln_g", 16), ("ln_b", 16), ("gate_bias", 1)):
    VEC[_name] = (_at, _n)
    _at += _n
NVEC = _at
MATS = ("mean1024", "mean64", "mean128", "ones", "ident", "rot1", "rot2", "cosc", "sinc", "causal", "anti",
        "fm00", "fm01", "fm10", "fm11")
MAT = {n: i for i, n in enumerate(MATS)}


class Op:

    def __init__(self, fn, after, sem):
        self.fn, self.after, self.sem, self.counted, self.value = fn, after, sem, False, 0


class Loaded:

    def __init__(self, sem, value):
        self.sem, self.value = sem, value


class Load:

    def __init__(self, fn, after, sem):
        self.fn, self.after, self.sem = fn, after, sem


class Queues:

    def __init__(self, nc, ctx):
        self.nc, self.ctx = nc, ctx
        self.q = {n: [] for n in ("tensor", "vector", "scalar", "gpsimd", "sync")}
        self.last = {}
        self.held = {n: [] for n in self.q}
        self.dma_count = {}
        self.stage("start")

    def sem(self, name):
        return self.ctx.enter_context(self.nc.semaphore(name))

    def stage(self, name):
        self.sems = {n: self.sem(f"{name}_{n}") for n in ("tensor", "vector", "scalar")}

    def put(self, engine, fn, after):
        flat = [a for a in self.held[engine]]
        self.held[engine] = []
        stack = list(after)
        while stack:
            a = stack.pop()
            if a is None:
                continue
            if isinstance(a, (list, tuple)):
                stack.extend(a)
            else:
                flat.append(a)
        for a in flat:
            if isinstance(a, Op):
                a.counted = True
        op = Op(fn, flat, self.sems[engine])
        self.q[engine].append(op)
        self.last[engine] = op
        return op

    def T(self, fn, *after):
        return self.put("tensor", fn, after)

    def V(self, fn, *after):
        return self.put("vector", fn, after)

    def A(self, fn, *after):
        return self.put("scalar", fn, after)

    def dma(self, sem, out, in_, *after, queue="gpsimd"):
        flat = list(self.held[queue])
        self.held[queue] = []
        stack = list(after)
        while stack:
            a = stack.pop()
            if a is None:
                continue
            if isinstance(a, (list, tuple)):
                stack.extend(a)
            else:
                flat.append(a)
        for a in flat:
            if isinstance(a, Op):
                a.counted = True
        self.q[queue].append(Load(lambda e, out=out, in_=in_: e.dma_start(out, in_), flat, sem))
        n = self.dma_count.get(id(sem), 0) + 16
        self.dma_count[id(sem)] = n
        return Loaded(sem, n)

    def fence(self, *more):
        done = [self.last[e] for e in ("tensor", "vector", "scalar") if e in self.last]
        extra = [x for m in more for x in (m if isinstance(m, (list, tuple)) else [m])]
        for e in ("vector", "scalar", "gpsimd"):
            self.held[e] = self.held[e] + done + extra
        for op in done:
            op.counted = True

    def emit(self, block):
        counts = {}
        for ops in self.q.values():
            for op in ops:
                if isinstance(op, Op) and op.counted:
                    counts[id(op.sem)] = counts.get(id(op.sem), 0) + 1
                    op.value = counts[id(op.sem)]

        def run(name):
            def body(engine):
                seen = {}
                for op in self.q[name]:
                    need = {}
                    for a in op.after:
                        if a.value > max(seen.get(id(a.sem), 0), need.get(id(a.sem), (0, 0))[1]):
                            need[id(a.sem)] = (a.sem, a.value)
                    for key, (sem, value) in need.items():
                        engine.wait_ge(sem, value)
                        seen[key] = value
                    ins = op.fn(engine)
                    if isinstance(op, Load):
                        ins.then_inc(op.sem, 16)
                    elif op.counted:
                        ins.then_inc(op.sem, 1)
                if name == "sync":
                    engine.wait_ge(self.end.sem, self.end.value)
            return body

        block.tensor(run("tensor"))
        block.vector(run("vector"))
        block.scalar(run("scalar"))
        block.gpsimd(run("gpsimd"))
        block.sync(run("sync"))


class Pair:

    def __init__(self, tensor, i):
        self.full = tensor[:, 2 * i:2 * i + 2, :].rearrange("p a b -> p (a b)")
        self.half = [tensor[:, 2 * i + h, :] for h in range(2)]
        self.read = []
        self.kept = False


class Weights:

    def __init__(self, q, sb, plan, ada_step):
        self.q, self.plan, self.ada_step = q, plan, ada_step
        self.raw = [sb(f"w_raw{i}", [P, BLK], F32) for i in range(RAW)]
        self.hi = [sb(f"w_hi{i}", [P, BLK], F32R) for i in range(2)]
        self.lo = [sb(f"w_lo{i}", [P, BLK], F32R) for i in range(2)]
        self.sem = [q.sem(f"w_loaded{i}") for i in range(RAW)]
        self.raw_read = [[] for _ in range(RAW)]
        self.landed = {}
        self.last_use = [[], []]
        self.issued = self.taken = self.split = 0
        self.ready = []
        for _ in range(RAW):
            self.issue()

    def issue(self):
        n = self.issued
        if n >= len(self.plan):
            return
        _, src, shape, _ = self.plan[n]
        size = int(np.prod(shape))
        dst = self.raw[n % RAW][:, 0:size]
        if len(shape) == 2:
            dst = dst.rearrange("p (a b) -> p a b", a=shape[0])
        self.landed[n] = self.q.dma(self.sem[n % RAW], dst, src, self.raw_read[n % RAW], queue="sync")
        self.issued += 1

    def advance(self):
        n = self.taken
        kind, _, shape, tag = self.plan[n]
        size = int(np.prod(shape))
        raw = self.raw[n % RAW][:, 0:size]
        if kind == "ada":
            done = self.ada_step(raw, tag, self.landed[n])
        else:
            s = self.split % 2
            hi, lo = self.hi[s][:, 0:size], self.lo[s][:, 0:size]
            up = self.q.A(lambda e: e.activation(hi, raw, ACT.Identity), self.landed[n], self.last_use[s])
            done = self.q.V(lambda e: e.tensor_tensor(lo, raw, hi.bitcast(F32), ALU.subtract), up)
            self.ready.append((s, tag, hi, lo, done))
            self.split += 1
        self.raw_read[n % RAW] = [done]
        self.taken += 1
        self.issue()

    def get(self, tag):
        while not self.ready:
            self.advance()
        s, got, hi, lo, done = self.ready.pop(0)
        assert got == tag, (got, tag)
        while self.taken < len(self.plan) and not self.ready:
            self.advance()
        return s, hi, lo, done

    def prepare(self):
        while not self.ready:
            self.advance()

    def used(self, s, op):
        self.last_use[s] = [op]


def build(nc, ins, out, stop=None):
    ctx = ExitStack()
    with ctx:
        q = Queues(nc, ctx)
        T, V, A = q.T, q.V, q.A

        def sb(name, shape, dt, scope=ctx):
            return scope.enter_context(nc.sbuf_tensor(name, shape, dt))

        psum = ctx.enter_context(nc.psum_tensor("psum", [P, 8, HALF], F32))
        pairs = [Pair(psum, i) for i in range(4)]
        turn = [0]

        def take():
            while pairs[turn[0] % 4].kept:
                turn[0] += 1
            turn[0] += 1
            return pairs[(turn[0] - 1) % 4]

        x = sb("x", [P, KT, S], F32)
        vec = sb("vec", [P, NVEC], F32)
        mats = sb("mats", [P, 2 * P], F32)
        mod1 = sb("mod1", [P, N_ADA1 * KT], F32)
        mod2 = sb("mod2", [P, 2 * N_ADA2 * KT], F32)
        cs = sb("cs", [P, KT], F32)
        cols = sb("cols", [P, 64], F32)
        acc = sb("ada_acc", [P, D], F32)
        one = sb("one", [P, 1], F32)
        eps = sb("eps", [P, 2], F32)
        sqh = [sb(f"sq{h}", [P, HALF], F32) for h in range(2)]
        mean1024, ident = mats[:, 0:P], mats[:, P:2 * P]

        proj = nc.dram_tensor("proj_scratch", [24, P, S], F32).ap()
        qk_hi = nc.dram_tensor("qk_hi_scratch", [8, P, S], F32R).ap()
        qk_lo = nc.dram_tensor("qk_lo_scratch", [8, P, S], F32R).ap()
        vsp = nc.dram_tensor("v_split_scratch", [A_HEADS, P, ST, P], F32R).ap()
        mvs = nc.dram_tensor("mv_rows", [P, ST, 512], F32).ap()
        mixd = nc.dram_tensor("mix_scratch", [KT, P, S], F32).ap()

        s_const, s_x = q.sem("const_loaded"), [q.sem(f"x_loaded{i}") for i in range(2)]
        vec_in = q.dma(s_const, vec[:], ins["vec"])
        q.dma(s_const, mats[:, 0:P], ins["mats"][MAT["mean1024"]], vec_in)
        consts = q.dma(s_const, mats[:, P:2 * P], ins["mats"][MAT["ident"]])
        x_in = []
        for i in range(2):
            x_in += [q.dma(s_x[i], x[:, 4 * i:4 * i + 4, :], ins["xT"][:, 4 * i:4 * i + 4, :])] * 4
        one_set = V(lambda e: e.memset(one[:], 1.0))
        V(lambda e: e.memset(eps[:, 0:1], EPS))
        eps_set = V(lambda e: e.memset(eps[:, 1:2], LN_EPS))

        def vc(name, i=0, n=1):
            return vec[:, VEC[name][0] + i:VEC[name][0] + i + n]

        cs_set = A(lambda e: e.activation(cs[:], vc("c", 0, 8), ACT.Silu), consts)
        mod_done = {}
        ada = {"free": [], "last": None, "due": []}

        def ada_step(raw, tag, landed):
            layer, i, kp = tag
            if kp == 0:
                ada_finish()
            for j in range(2):
                k = 2 * kp + j
                w = raw[:, j * D:(j + 1) * D]
                cv = cs[:, k:k + 1] if layer == 0 else vc("c_2", k)
                if k == 0:
                    ada["last"] = V(lambda e, w=w, cv=cv: e.tensor_scalar(acc[:], w, cv, None, ALU.mult),
                                    landed, cs_set, consts, ada["free"])
                else:
                    ada["last"] = V(lambda e, w=w, cv=cv: e.scalar_tensor_tensor(
                        out=acc[:], in0=w, scalar=cv, in1=acc[:], op0=ALU.mult, op1=ALU.add), landed, ada["last"])
            if kp == KT // 2 - 1:
                ada["due"].append((layer, i, ada["last"]))
                ada["free"] = None
            return ada["last"]

        def ada_finish():
            while ada["due"]:
                layer, i, done = ada["due"].pop(0)
                p = take()
                for j in range(KT):
                    mm = T(lambda e, j=j, p=p: e.transpose(p.full[:, j * P:(j + 1) * P], acc[:, j * P:(j + 1) * P],
                                                          ident), done, p.read, consts)
                dst = mod1[:, i * KT:(i + 1) * KT] if layer == 0 else \
                    mod2[:, ((layer - 1) * N_ADA2 + i) * KT:((layer - 1) * N_ADA2 + i + 1) * KT]
                bias = vc("b_ada", i * KT, KT) if layer == 0 else vc("b_ada_2", ((layer - 1) * N_ADA2 + i) * KT, KT)
                d = V(lambda e, p=p, dst=dst: e.tensor_reduce(dst, p.full.rearrange("p (j k) -> p j k", j=KT), AX.X,
                                                              ALU.add), mm)
                p.read = [d]
                d = V(lambda e, dst=dst, bias=bias: e.tensor_tensor(dst, dst, bias, ALU.add), d)
                mod_done[(layer, i)] = d
                ada["free"] = [mm]

        plan = []
        ada_list = [(0, i, kp) for i in range(N_ADA1) for kp in range(4)] + \
                   [(l, i, kp) for l in (1, 2) for i in range(N_ADA2) for kp in range(4)]

        def plan_ada(n):
            for _ in range(min(n, len(ada_list))):
                l, i, kp = ada_list.pop(0)
                w = ins["w_ada"] if l == 0 else ins["w_ada_2"][l - 1]
                src = w[2 * kp * P:(2 * kp + 2) * P, i * D:(i + 1) * D].rearrange("(k p) n -> p k n", p=P)
                plan.append(("ada", src, (2, D), (l, i, kp)))

        def ffn_order():
            first, seq = 0, []
            starts = np.cumsum((0,) + FF_GROUPS)
            for g, n in enumerate(FF_GROUPS):
                fs = list(range(starts[g], starts[g + 1]))
                seq += [("gu", f) for f in (fs if g == 0 else fs[1:])]
                if g + 1 < len(FF_GROUPS):
                    seq.append(("gu", int(starts[g + 1])))
                seq.append(("down", g))
            return [(k, int(n)) for k, n in seq], starts

        def plan_ffn(n):
            seq, starts = ffn_order()
            for kind, i in seq:
                if kind == "gu":
                    plan.append(("w", ins[f"w_gu{n}"][i], (BLK,), ("gu", n, i)))
                    plan_ada(1)
                else:
                    for c in range(4):
                        src = ins[f"w_down{n}"][int(starts[i]):int(starts[i + 1]), :, c * 256:(c + 1) * 256]
                        plan.append(("w", src.rearrange("f p c -> p f c"), (FF_GROUPS[i], 256), ("down", n, i, c)))

        plan_ada(8)
        plan_ffn(1)
        for b in range(13):
            if b == 12:
                plan.append(("w", ins["w_in_gate"], (KT * P,), ("in1", b)))
            else:
                plan.append(("w", ins["w_in"][b], (BLK,), ("in1", b)))
            plan_ada(1)
        for c in range(4):
            plan.append(("w", ins["w_out"][:, :, c * 256:(c + 1) * 256].rearrange("f p c -> p f c"), (KT, 256), ("out1", c)))
        plan_ffn(2)
        plan_ada(99)
        for l in range(2):
            for b in range(11):
                plan.append(("w", ins["w_in_2"][l, b], (BLK,), ("in2", l, b)))
            for c in range(4):
                for t in range(2):
                    plan.append(("w", ins["dft"][t][:, :, c * 256:(c + 1) * 256].rearrange("f p c -> p f c"),
                                 (KT, 256), ("dft", l, c, t)))
            for c in range(4):
                plan.append(("w", ins["w_out_2"][l][:, :, c * 256:(c + 1) * 256].rearrange("f p c -> p f c"), (KT, 256),
                             ("out2", l, c)))
        W = Weights(q, sb, plan, ada_step)

        def get(tag):
            ada_finish()
            return W.get(tag)

        def gemm(blk, m, n, hi, lo, ready, width=256, order=None):
            s, whi, wlo, wdone = blk
            p = take()
            order = order or list(range(n))
            for h in range(2):
                for k in order:
                    for i, (a, b) in enumerate(((whi, hi), (whi, lo), (wlo, hi))):
                        mm = T(lambda e, a=a, b=b(k), k=k, h=h, i=i, p=p: e.matmul(
                            p.half[h], a[:, k * width + m * P:k * width + (m + 1) * P], b[:, h * HALF:(h + 1) * HALF],
                            start=(k == order[0] and i == 0), stop=(k == order[-1] and i == 2)),
                            wdone, p.read if k == order[0] and i == 0 else None,
                            ready[k][h] if isinstance(ready[k], tuple) else ready[k])
            W.used(s, mm)
            return p, mm

        def gemm_pair(blk, hi, lo, ready):
            s, whi, wlo, wdone = blk
            ps = [take(), take()]
            mms = {}
            for h in range(2):
                for m in range(2):
                    for k in range(KT):
                        for i, (a, b) in enumerate(((whi, hi), (whi, lo), (wlo, hi))):
                            mms[m] = T(lambda e, a=a, b=b(k), k=k, h=h, m=m, i=i: e.matmul(
                                ps[m].half[h], a[:, k * 256 + m * P:k * 256 + (m + 1) * P], b[:, h * HALF:(h + 1) * HALF],
                                start=(k == 0 and i == 0), stop=(k == KT - 1 and i == 2)),
                                wdone, ps[m].read if k == 0 and i == 0 else None, ready[k][h])
            W.used(s, mms[1])
            return [(ps[m], mms[m]) for m in range(2)]

        def gemm_rows(blk, hi, lo, tt0, ready):
            s, whi, wlo, wdone = blk
            p = take()
            for j in range(4):
                for k in range(KT):
                    for i, (a, b) in enumerate(((whi, hi), (whi, lo), (wlo, hi))):
                        mm = T(lambda e, a=a, b=b(k), k=k, j=j, i=i, p=p: e.matmul(
                            p.full[:, j * 256:(j + 1) * 256], b[:, (tt0 + j) * P:(tt0 + j + 1) * P],
                            a[:, k * 256:(k + 1) * 256], start=(k == 0 and i == 0), stop=(k == KT - 1 and i == 2)),
                            wdone, p.read if j == 0 else None, list(ready[k]))
            W.used(s, mm)
            return p, mm

        stat = {"pair": None, "free": [None, None], "sq": {}}

        def stat_open():
            stat["pair"] = take()
            stat["pair"].kept = True

        def stat_square(d):
            for h in range(2):
                stat["sq"][(d, h)] = A(lambda e, h=h: e.activation(sqh[h][:], x[:, d, h * HALF:(h + 1) * HALF], ACT.Square),
                                       x_ready[d], stat["free"][h])

        def stat_mean(d, squares=True):
            p = stat["pair"]
            for h in range(2):
                src = sqh[h][:] if squares else x[:, d, h * HALF:(h + 1) * HALF]
                mm = T(lambda e, h=h, src=src: e.matmul(p.half[h], mean1024, src, start=(d == 0), stop=(d == KT - 1)),
                       stat["sq"][(d, h)] if squares else x_ready[d], p.read if d == 0 else None, consts)
                if squares:
                    stat["free"][h] = mm
                stat[("sum", h)] = mm

        def stat_all(squares):
            stat_open()
            for d in range(KT):
                if squares:
                    stat_square(d)
                stat_mean(d, squares)

        def rsqrt_guess(var, epsc, r, after, free=None):
            l1 = A(lambda e: e.activation(r, var, ACT.Ln, bias=epsc), after, eps_set, free)
            return A(lambda e: e.activation(r, r, ACT.Exp, scale=-0.5), l1)

        def rsqrt_newton(var, epsc, r, u, guess, free=None):
            n1 = V(lambda e: e.scalar_tensor_tensor(out=u, in0=r, scalar=-0.5, in1=r, op0=ALU.mult, op1=ALU.mult),
                   guess, free)
            n2 = V(lambda e: e.scalar_tensor_tensor(out=u, in0=var, scalar=epsc, in1=u, op0=ALU.add, op1=ALU.mult), n1)
            return V(lambda e: e.scalar_tensor_tensor(out=r, in0=u, scalar=1.5, in1=r, op0=ALU.add, op1=ALU.mult), n2), n2

        def rsqrt(var, epsc, r, u, after, free=None):
            return rsqrt_newton(var, epsc, r, u, rsqrt_guess(var, epsc, r, after, free), free)

        x_ready = [x_in[k] for k in range(KT)]

        def scale_cols(dst, g, sc, after):
            return V(lambda e: e.scalar_tensor_tensor(out=dst, in0=sc, scalar=1.0, in1=g, op0=ALU.add, op1=ALU.mult), after)

        def halves(p, name, epsc, scope, write):
            r = [sb(f"{name}_r{h}", [P, HALF], F32, scope)[:] for h in range(2)]
            u = sb(f"{name}_u", [P, HALF], F32, scope)[:]
            g = [rsqrt_guess(p.half[h], epsc, r[h], stat[("sum", h)]) for h in range(2)]
            done, p.read = [], []
            for h in range(2):
                rd, pr = rsqrt_newton(p.half[h], epsc, r[h], u, g[h], done)
                p.read.append(pr)
                done = [rd]
                write(h, r[h], rd)
            p.kept = False

        def split_shifted(t, sh, hi, lo, after):
            up = A(lambda e: e.activation(hi, t, ACT.Identity, bias=sh), after)
            return lambda: V(lambda e: e.scalar_tensor_tensor(out=lo, in0=t, scalar=sh, in1=hi.bitcast(F32), op0=ALU.add,
                                                              op1=ALU.subtract), up)

        def modulated(name, h_, g, ish, isc):
            with ExitStack() as scope:
                t = [sb(f"{name}_t{i}", [P, HALF], F32, scope) for i in range(4)]
                ready, free = {}, [None] * 4

                def write(h, r, rd):
                    if h == 0:
                        while (0, ish) not in mod_done or (0, isc) not in mod_done:
                            W.advance()
                            ada_finish()
                        stat["cols"] = scale_cols(cols[:, 0:8], vc(g, 0, 8), mod1[:, isc * 8:isc * 8 + 8],
                                                  [mod_done[(0, isc)], mod_done[(0, ish)]])
                    c = slice(h * HALF, (h + 1) * HALF)
                    low = {}

                    def finish_tile(k):
                        ready[(k, h)] = free[(h * KT + k) % 4] = low[k]()

                    for k in range(KT):
                        i = (h * KT + k) % 4
                        td = V(lambda e, k=k, i=i: e.scalar_tensor_tensor(
                            out=t[i][:], in0=x[:, k, c], scalar=cols[:, k:k + 1], in1=r, op0=ALU.mult, op1=ALU.mult),
                            rd, stat["cols"], free[i])
                        low[k] = split_shifted(t[i][:], mod1[:, ish * 8 + k:ish * 8 + k + 1], h_[0][:, k, c],
                                               h_[1][:, k, c], td)
                        if k >= 2:
                            finish_tile(k - 2)
                    finish_tile(KT - 2)
                    finish_tile(KT - 1)

                halves(stat["pair"], name, eps[:, 0:1], scope, write)
            return [(ready[(k, 0)], ready[(k, 1)]) for k in range(KT)]

        def ffn(n, igt):
            q.stage(f"ffn{n}")
            q.fence()
            if n == 1:
                stat_all(True)
                while (0, igt - 1) not in mod_done:
                    W.advance()
                    ada_finish()
                W.prepare()
            with ExitStack() as hs:
                h = [sb(f"h{n}_hi", [P, KT, S], F32R, hs), sb(f"h{n}_lo", [P, KT, S], F32R, hs)]
                ready = modulated(f"nf{n}", h, f"g_ffn{n}", igt - 2, igt - 1)
                q.fence()
                ah = [sb(f"a{n}_hi{i}", [P, S], F32R, hs) for i in range(A_SLOTS)]
                al = [sb(f"a{n}_lo{i}", [P, S], F32R, hs) for i in range(A_SLOTS)]
                g = sb(f"gate{n}", [P, S], F32, hs)
                a_ready, a_free, g_free, gcols = {}, {}, [None], [None]
                seq, starts = ffn_order()
                for kind, i in seq:
                    if kind == "gu":
                        blk = get(("gu", n, i))
                        hi, lo = (lambda k: h[0][:, k, :]), (lambda k: h[1][:, k, :])
                        both = gemm_pair(blk, hi, lo, ready) if i == 0 else None
                        pg, m1 = both[0] if both else gemm(blk, 0, KT, hi, lo, ready)
                        gd = A(lambda e, pg=pg: e.activation(g[:], pg.full, ACT.Silu), m1, g_free[0])
                        pg.read = [gd]
                        pu, m2 = both[1] if both else gemm(blk, 1, KT, hi, lo, ready)
                        s = i % A_SLOTS
                        ad = V(lambda e, pu=pu: e.tensor_tensor(g[:], g[:], pu.full, ALU.mult), gd, m2)
                        pu.read = [ad]
                        up = A(lambda e, s=s: e.activation(ah[s][:], g[:], ACT.Identity), ad, a_free.get(i - A_SLOTS))
                        dn = V(lambda e, s=s: e.tensor_tensor(al[s][:], g[:], ah[s][:].bitcast(F32), ALU.subtract), up)
                        g_free[0] = dn
                        a_ready[i] = dn
                    else:
                        f0, nf = int(starts[i]), FF_GROUPS[i]
                        for c in range(4):
                            blk = get(("down", n, i, c))
                            if gcols[0] is None:
                                gcols[0] = V(lambda e: e.tensor_scalar(cols[:, 8:16], mod1[:, igt * 8:igt * 8 + 8], 0.5, None,
                                                                       ALU.mult), mod_done[(0, igt)])
                            last = i == len(FF_GROUPS) - 1
                            if last and c == 0:
                                stat_open()
                            for m in range(2):
                                d = 2 * c + m
                                p, mm = gemm(blk, m, nf, lambda k: ah[(f0 + k) % A_SLOTS], lambda k: al[(f0 + k) % A_SLOTS],
                                             [a_ready[f0 + k] for k in range(nf)])
                                x_ready[d] = V(lambda e, p=p, d=d: e.scalar_tensor_tensor(
                                    out=x[:, d, :], in0=p.full, scalar=cols[:, 8 + d:9 + d], in1=x[:, d, :],
                                    op0=ALU.mult, op1=ALU.add), mm, gcols[0], x_ready[d])
                                p.read = [x_ready[d]]
                                if last:
                                    if d:
                                        stat_mean(d - 1)
                                    stat_square(d)
                        if last:
                            stat_mean(KT - 1)
                        for f in range(f0, f0 + nf):
                            a_free[f] = mm

        spilled = {}

        class Store:

            def __init__(self, name, n, scope, dt=F32):
                self.t = [sb(f"{name}{i}", [P, S], dt, scope) for i in range(n)]
                self.s = [q.sem(f"{name}_stored{i}") for i in range(n)]
                self.free = [None] * n
                self.i, self.n = 0, n

            def next(self):
                i = self.i % self.n
                return self.t[i], self.free[i]

            def store(self, dst, key, *after, view=None):
                i = self.i % self.n
                self.i += 1
                for to, of in (view(self.t[i]) if view else [(dst, self.t[i][:])]):
                    self.free[i] = q.dma(self.s[i], to, of, *after)
                spilled.setdefault(key, []).append(self.free[i])

            def all(self):
                return [f for f in self.free if f is not None]

        def split_out(src, his, los, to_hi, to_lo, key, after, view=None):
            th, fh = his.next()
            tl, fl = los.next()
            up = A(lambda e: e.activation(th[:], src, ACT.Identity), after, fh)
            dn = V(lambda e: e.tensor_tensor(tl[:], src, th[:].bitcast(F32), ALU.subtract), up, fl)
            his.store(to_hi, key, dn, view=view and (lambda t: view(t, 0)))
            los.store(to_lo, key, dn, view=view and (lambda t: view(t, 1)))
            return dn

        def rope_heads(his, los, tmp, mats64, rot, cost, sint, gcol, nt, tables, p, mm):
            raw, sq, u, free = tmp
            a1 = A(lambda e: e.activation(sq, p.full, ACT.Square), mm, free)
            a2 = A(lambda e: e.activation(raw, p.full, ACT.Identity), mm, free)
            p.read = [a1, a2]
            yield
            p2 = take()
            for h in range(2):
                m2 = T(lambda e, h=h, p2=p2: e.matmul(p2.half[h], mats64, sq[:, h * HALF:(h + 1) * HALF], start=True,
                                                     stop=True), a1, p2.read, tables)
            rd, pr = rsqrt(p2.full, eps[:, 0:1], sq, u, m2)
            p2.read = [pr]
            qn = V(lambda e: e.scalar_tensor_tensor(out=raw, in0=raw, scalar=gcol, in1=sq, op0=ALU.mult, op1=ALU.mult),
                   rd, a2, tables)
            yield
            p3 = take()
            for h in range(2):
                m3 = T(lambda e, h=h, p3=p3: e.matmul(p3.half[h], rot, raw[:, h * HALF:(h + 1) * HALF], start=True,
                                                     stop=True), qn, p3.read)
            c2 = V(lambda e: e.tensor_tensor(u, p3.full, sint, ALU.mult), m3, rd)
            p3.read = [c2]
            c1 = V(lambda e: e.tensor_tensor(raw, raw, cost, ALU.mult), m3)
            c3 = V(lambda e: e.tensor_tensor(raw, raw, u, ALU.add), c1, c2)
            tmp[3] = split_out(raw, his, los, qk_hi[nt], qk_lo[nt], ("qk", nt), c3)
            yield

        def step(pending):
            for g in list(pending):
                try:
                    next(g)
                except StopIteration:
                    pending.remove(g)

        def attention(name, kv_of, kv_tile, mask, gate_tile, mixh):
            q.stage(name)
            with ExitStack() as sc:
                qs = [sb(f"{name}_q{i}", [P, S], F32R, sc) for i in range(2)]
                kh = [sb(f"{name}_kh{i}", [P, S], F32R, sc) for i in range(2)]
                kl = [sb(f"{name}_kl{i}", [P, S], F32R, sc) for i in range(2)]
                vs = [sb(f"{name}_v{i}", [P, ST, P], F32R, sc) for i in range(2)]
                nu = [sb(f"{name}_num{i}", [P, S], F32, sc) for i in range(2)]
                th = [sb(f"{name}_th{i}", [P, ST, 256], F32R, sc) for i in range(2)]
                tl = [sb(f"{name}_tl{i}", [P, ST, 256], F32R, sc) for i in range(2)]
                sm = [sb(f"{name}_sm{i}", [P, 4], F32, sc) for i in range(2)]
                dg = [sqh[1][:, (i + 1) * P:(i + 2) * P] for i in range(3)]
                og = sb(f"{name}_o", [P, S], F32, sc)
                onest = sqh[1][:, 0:P]
                tm = [sqh[0][0:64, i * 256:(i + 1) * 256] for i in range(2)]
                s_q = [q.sem(f"{name}_qload{i}") for i in range(2)]
                s_k = [q.sem(f"{name}_kload{i}") for i in range(2)]
                s_v = [q.sem(f"{name}_vload{i}") for i in range(2)]
                s_c = q.sem(f"{name}_constload")
                q_free, k_free = [None, None], [None, None]
                qin, kin, vin = {}, {}, {}
                kv_list = []
                for hd in range(A_HEADS):
                    if kv_of(hd) not in kv_list:
                        kv_list.append(kv_of(hd))

                def load_q(hd):
                    i, r = hd % 2, slice(64 * (hd % 2), 64 * (hd % 2) + 64)
                    got = spilled[("qk", hd // 2)]
                    q.dma(s_q[i], qs[i][0:64, :], qk_hi[hd // 2][r, :], got, q_free[i])
                    qin[hd] = q.dma(s_q[i], qs[i][64:128, :], qk_lo[hd // 2][r, :])

                def load_kv(kv):
                    i, r, t = kv % 2, slice(64 * (kv % 2), 64 * (kv % 2) + 64), kv_tile + kv // 2
                    got = spilled[("qk", t)]
                    for d, src in ((kh, qk_hi), (kl, qk_lo)):
                        for o in (0, 64):
                            kin[kv] = q.dma(s_k[i], d[i][o:o + 64, :], src[t][r, :], got, k_free[i])
                    vin[kv] = q.dma(s_v[i], vs[i][:], vsp[kv], spilled[("v", kv)], k_free[i])

                load_q(0)
                load_kv(kv_list[0])
                if mask is not None:
                    maskt = sb(f"{name}_mask", [P, 1920], F32, sc)
                    q.dma(s_c, maskt[:], mask)
                else:
                    gt = [sb(f"{name}_g{i}", [P, S], F32, sc) for i in range(1)]
                    s_g = q.sem(f"{name}_gload")
                    g_free = None
                c_in = q.dma(s_c, onest, ins["mats"][MAT["ones"]])
                load_q(1)
                if len(kv_list) > 1:
                    load_kv(kv_list[1])
                ps_s, ps_t, ps_o = [take(), take()], take(), take()
                ps_o_read = [list(ps_o.read), list(ps_o.read)]
                nu_free, t_free, tm_free, og_free = [None, None], [None, None], [None, None], None
                n = A_HEADS * ST
                soft, parts, o_done, sdone, maxed, turned, dgd, vdone = {}, {}, {}, {}, {}, {}, {}, {}
                dg_free, ps_t_read = [None] * 3, [list(ps_t.read), list(ps_t.read)]

                def unit(u):
                    return u // ST, u % ST

                def score_products(u):
                    hd, i = unit(u)
                    kv = kv_of(hd)
                    b, c = hd % 2, kv % 2
                    p = ps_s[u % 2]
                    for h in range(2):
                        for a, k_ in enumerate((kh, kl)):
                            mm = T(lambda e, h=h, a=a, k_=k_: e.matmul(
                                p.half[h], qs[b][:, i * P:(i + 1) * P], k_[c][:, h * HALF:(h + 1) * HALF],
                                start=(a == 0), stop=(a == 1)), qin[hd], kin[kv], p.read)
                    if i == ST - 1:
                        q_free[b] = mm
                        if hd + 2 < A_HEADS:
                            load_q(hd + 2)
                    sdone[u] = mm

                def maximum(u):
                    p, s, m, mm, i = ps_s[u % 2], nu[u % 2], sm[u % 2], sdone[u], u % ST
                    if mask is not None:
                        o = 896 - P * i
                        mx = V(lambda e: e.tensor_tensor_reduce(
                            out=s[:], in0=p.full, in1=maskt[:, o:o + S], scale=1.0, scalar=-3e38, op0=ALU.add,
                            op1=ALU.max, accum_out=m[:, 0:1]), mm, c_in, nu_free[u % 2])
                        p.read = [mx]
                        mx = V(lambda e: e.tensor_scalar(m[:, 1:2], m[:, 0:1], -1.0, None, ALU.mult), mx)
                        src = s[:]
                    else:
                        mx = V(lambda e: e.tensor_reduce(m[:, 1:2], p.full, AX.X, ALU.max, negate=True), mm,
                               nu_free[u % 2])
                        src = p.full
                    maxed[u] = (mx, src)

                def numerators(u):
                    p, s, m, (mx, src) = ps_s[u % 2], nu[u % 2], sm[u % 2], maxed[u]
                    ex = A(lambda e: e.activation(s[:], src, ACT.Exp, bias=m[:, 1:2], accum_out=m[:, 2:3]), mx,
                           nu_free[u % 2])
                    if mask is None:
                        p.read = [ex]
                    soft[u] = ex

                def reciprocal_sum(u):
                    m = sm[u % 2]
                    rc = V(lambda e: e.reciprocal(m[:, 3:4], m[:, 2:3]), soft[u])
                    dgd[u] = A(lambda e: e.activation(dg[u % 3], ident, ACT.Copy, scale=m[:, 3:4]), rc, dg_free[u % 3])

                def turn_over(u):
                    s, w = nu[u % 2], u // 2
                    c = slice((u % 2) * P, (u % 2) * P + P)
                    fr = t_free[w % 2] if u % 2 == 0 else None
                    for h in range(2):
                        for j in range(4):
                            mm = T(lambda e, h=h, j=j: e.transpose(
                                ps_t.half[h][:, j * P:(j + 1) * P], s[:, (4 * h + j) * P:(4 * h + j + 1) * P], ident),
                                soft[u], ps_t_read[h])
                        t3 = ps_t.half[h].rearrange("p (j q) -> p j q", j=4)
                        hi, lo = th[w % 2][:, 4 * h:4 * h + 4, c], tl[w % 2][:, 4 * h:4 * h + 4, c]
                        up = A(lambda e, t3=t3, hi=hi: e.activation(hi, t3, ACT.Identity), mm, fr)
                        turned[(u, h)] = (up, t3, hi, lo, fr)
                    nu_free[u % 2] = mm

                def low_parts(u):
                    for h in range(2):
                        up, t3, hi, lo, fr = turned[(u, h)]
                        dn = V(lambda e, t3=t3, hi=hi, lo=lo: e.tensor_tensor(lo, t3, hi.bitcast(F32), ALU.subtract), up, fr)
                        ps_t_read[h] = [dn]
                    parts[u] = dn

                def spread_sum(u):
                    bank = ps_o.half[(u // 2) % 2]
                    dg_free[u % 3] = T(lambda e: e.matmul(
                        bank[:, 256 + (u % 2) * P:256 + (u % 2 + 1) * P], onest, dg[u % 3], start=True, stop=True),
                        dgd[u], c_in, ps_o_read[(u // 2) % 2])

                def times_v(w, part):
                    nonlocal g_in
                    hd, i = unit(2 * w)
                    kv, pp, hh = kv_of(hd), hd // 2, hd % 2
                    if gate_tile is not None and hh == 0 and i == 0 and part == 0:
                        g_in = q.dma(s_g, gt[0][:], proj[gate_tile + pp], spilled[("proj", gate_tile + pp)], og_free)
                    bank = ps_o.half[w % 2]
                    for j in range(ST):
                        mm = T(lambda e, j=j: e.matmul(
                            bank[:, 0:256], vs[kv % 2][:, j, :], (th, tl)[part][w % 2][:, j, :],
                            start=(part == 0 and j == 0), stop=(part == 1 and j == ST - 1)), parts[2 * w + 1], vin[kv])
                    if part == 0:
                        return
                    t_free[w % 2] = mm
                    vdone[w] = mm
                    if i + 2 >= ST and (hd + 1 == A_HEADS or kv_of(hd + 1) != kv):
                        k_free[kv % 2] = mm
                        at = kv_list.index(kv)
                        if at + 2 < len(kv_list):
                            load_kv(kv_list[at + 2])

                def results(w):
                    nonlocal og_free
                    hd, i = unit(2 * w)
                    pp, hh = hd // 2, hd % 2
                    bank = ps_o.half[w % 2]
                    t = tm[w % 2]
                    a1 = A(lambda e: e.activation(t, bank[64:128, 0:256], ACT.Identity), vdone[w], tm_free[w % 2])
                    v1 = V(lambda e: e.tensor_tensor(t, bank[0:64, 0:256], t, ALU.add), a1)
                    o = og[64 * hh:64 * hh + 64, i * P:(i + 2) * P]
                    v2 = V(lambda e: e.tensor_tensor(o, t, bank[0:64, 256:512], ALU.mult), v1,
                           og_free if hh == 0 and i == 0 else None)
                    tm_free[w % 2] = v2
                    ps_o_read[w % 2] = [v2]
                    if hh == 1 and i + 2 >= ST:
                        if gate_tile is not None:
                            v2 = V(lambda e: e.tensor_tensor(og[:], og[:], gt[0][:], ALU.mult), v2, g_in)
                        up = A(lambda e: e.activation(mixh[0][:, pp, :], og[:], ACT.Identity), v2)
                        og_free = V(lambda e: e.tensor_tensor(mixh[1][:, pp, :], og[:], mixh[0][:, pp, :].bitcast(F32),
                                                              ALU.subtract), up)
                        o_done[pp] = og_free

                g_in = None
                for u in range(n + 4):
                    if u < n:
                        score_products(u)
                        maximum(u)
                    if u >= 5 and u % 2 == 1:
                        results((u - 5) // 2)
                    if 1 <= u <= n:
                        turn_over(u - 1)
                    if u < n:
                        numerators(u)
                    if 1 <= u <= n:
                        low_parts(u - 1)
                        reciprocal_sum(u - 1)
                    if u >= 3 and u % 2 == 1 and u < n + 3:
                        spread_sum(u - 3)
                        spread_sum(u - 2)
                        times_v((u - 3) // 2, 0)
                    if u >= 4 and u % 2 == 0:
                        times_v((u - 4) // 2, 1)
                ps_o.read = ps_o_read[0] + ps_o_read[1]
                ps_t.read = ps_t_read[0] + ps_t_read[1]
                return [o_done[pp] for pp in range(4)]

        def load_mix(name, h, first):
            with ExitStack() as sc:
                t = [sb(f"{name}_t{i}", [P, S], F32, sc) for i in range(3)]
                sm = [q.sem(f"{name}_load{i}") for i in range(3)]
                free, ready = [None] * 3, []
                for k in range(4):
                    ld = q.dma(sm[k % 3], t[k % 3][:], mixd[first + k], spilled[("mix", first + k)], free[k % 3])
                    up = A(lambda e, k=k: e.activation(h[0][:, k, :], t[k % 3][:], ACT.Identity), ld)
                    dn = V(lambda e, k=k: e.tensor_tensor(h[1][:, k, :], t[k % 3][:], h[0][:, k, :].bitcast(F32),
                                                          ALU.subtract), up)
                    free[k % 3] = dn
                    ready.append(dn)
            return ready

        def mixer1():
            q.stage("proj1")
            q.fence()
            with ExitStack() as hs:
                h = [sb("hm_hi", [P, KT, S], F32R, hs), sb("hm_lo", [P, KT, S], F32R, hs)]
                ready = modulated("nm", h, "g_mix", 3, 4)
                q.fence()
                hi, lo = (lambda k: h[0][:, k, :]), (lambda k: h[1][:, k, :])
                with ExitStack() as sc:
                    cst = sb("rope_cos", [P, S], F32, sc)
                    snt = sb("rope_sin", [P, S], F32, sc)
                    m2 = sb("rope_mats", [P, 2 * P], F32, sc)
                    s_t = q.sem("rope1_loaded")
                    t1 = q.dma(s_t, cst[:], ins["rope1"][0])
                    t2 = q.dma(s_t, snt[:], ins["rope1"][1])
                    t2 = q.dma(s_t, m2[:, 0:P], ins["mats"][MAT["mean64"]])
                    tables = q.dma(s_t, m2[:, P:2 * P], ins["mats"][MAT["rot1"]])
                    gq = V(lambda e: e.tensor_scalar(cols[:, 16:17], vc("g_q"), A_DIM ** -0.5, None, ALU.mult))
                    his, los = Store("p1_hi", 2, sc, F32R), Store("p1_lo", 2, sc, F32R)
                    tmps = []
                    for i in range(2):
                        tmps.append([sb(f"p1_{n}{i}", [P, S], F32, sc)[:] for n in ("raw", "sq", "u")] + [None])
                    pending = []
                    nt = 0
                    for b in range(4):
                        blk = get(("in1", b))
                        both = gemm_pair(blk, hi, lo, ready) if b == 0 else None
                        for m in range(2):
                            p, mm = both[m] if both else gemm(blk, m, KT, hi, lo, ready)
                            step(pending)
                            gc = cols[:, 16:17] if b < 2 else vc("g_k")
                            pending.append(rope_heads(his, los, tmps[nt % 2], m2[:, 0:P], m2[:, P:2 * P], cst[:], snt[:],
                                                      gc, nt, [tables, gq], p, mm))
                            next(pending[-1])
                            nt += 1
                    while pending:
                        step(pending)
                    done = his.all() + los.all()
                q.fence(done)
                with ExitStack() as sc:
                    st = Store("p1b_o", 4, sc)
                    his, los = Store("p1b_hi", 2, sc, F32R), Store("p1b_lo", 2, sc, F32R)
                    for b in range(4, 8):
                        blk = get(("in1", b))
                        for t0 in (0, 4):
                            p, mm = gemm_rows(blk, hi, lo, t0, ready)
                            if b < 6:
                                def view(t, part, b=b, t0=t0):
                                    t4 = t[:].rearrange("p (a h d) -> p a h d", a=4, h=4)
                                    return [(vsp[4 * (b % 2) + hd][:, t0:t0 + 4, 64 * part:64 * part + 64], t4[:, :, hd, :])
                                            for hd in range(4)]
                                p.read = [split_out(p.full, his, los, None, None, ("vrows", b % 2), mm, view=view)]
                                continue
                            t, fr = st.next()
                            d = A(lambda e, p=p, t=t: e.activation(t[:], p.full, ACT.Identity), mm, fr)
                            p.read = [d]
                            st.store(None, ("mvs", b % 2), d, view=lambda t, t0=t0, b=b: [
                                (mvs[:, t0:t0 + 4, (b % 2) * 256:(b % 2 + 1) * 256], t[:].rearrange("p (a b) -> p a b", a=4))])
                    for hd in range(A_HEADS):
                        spilled[("v", hd)] = spilled[("vrows", hd // 4)]
                    for b in range(8, 13):
                        blk = get(("in1", b))
                        for m in range(2 if b < 12 else 1):
                            p, mm = gemm(blk, m, KT, hi, lo, ready, 256 if b < 12 else P)
                            t, fr = st.next()
                            if b == 9:
                                d = A(lambda e, p=p, t=t: e.activation(t[:], p.full, ACT.Identity, scale=M_QK ** -0.5), mm, fr)
                            elif b in (10, 11):
                                d = A(lambda e, p=p, t=t: e.activation(t[:], p.full, ACT.Sigmoid), mm, fr)
                            elif b == 12:
                                d = A(lambda e, p=p, t=t: e.activation(t[:], p.full, ACT.Identity, bias=vc("gate_bias")),
                                      mm, fr)
                            else:
                                d = A(lambda e, p=p, t=t: e.activation(t[:], p.full, ACT.Identity), mm, fr)
                            p.read = [d]
                            n = 8 + 2 * (b - 8) + m
                            st.store(proj[n], ("proj", n), d)
                    done = st.all() + his.all() + los.all()
            q.fence(done)
            done = mlstm()
            q.fence(done)
            with ExitStack() as ma:
                mixa = [sb("mix1a_hi", [P, 4, S], F32R, ma), sb("mix1a_lo", [P, 4, S], F32R, ma)]
                ra = attention("attn1", lambda h: h, 4, ins["band"], None, mixa)
                q.stage("out1")
                q.fence()
                mixb = [sb("mix1b_hi", [P, 4, S], F32R, ma), sb("mix1b_lo", [P, 4, S], F32R, ma)]
                rb = load_mix("mix1", mixb, 0)
                stat_open()
                for c in range(4):
                    blk = get(("out1", c))
                    for m in range(2):
                        d = 2 * c + m
                        p, mm = gemm(blk, m, KT, lambda k: (mixb if k < 4 else mixa)[0][:, k % 4, :],
                                     lambda k: (mixb if k < 4 else mixa)[1][:, k % 4, :], rb + ra,
                                     order=[4, 5, 6, 7, 0, 1, 2, 3])
                        x_ready[d] = V(lambda e, p=p, d=d: e.scalar_tensor_tensor(
                            out=x[:, d, :], in0=p.full, scalar=mod1[:, 5 * 8 + d:5 * 8 + d + 1], in1=x[:, d, :],
                            op0=ALU.mult, op1=ALU.add), mm, x_ready[d], mod_done[(0, 5)])
                        p.read = [x_ready[d]]
                        if d:
                            stat_mean(d - 1)
                        stat_square(d)
                stat_mean(KT - 1)

        def mlstm():
            q.stage("mlstm_rows")
            R = 36
            with ExitStack() as sc:
                colsA = sb("ml_colsA", [P, ST, P], F32, sc)
                colsB = sb("ml_colsB", [P, ST, P], F32, sc)
                nm = sb("ml_negM", [R, S], F32, sc)
                decB = sb("ml_decay", [P, 2, 2, ST], F32, sc)
                sel = sb("ml_sel", [R, 8 * P], F32, sc)
                mm_ = sb("ml_mats", [P, 3 * P], F32, sc)
                qk = sb("ml_qk", [P, 4, S], F32, sc)
                v1 = sb("ml_v", [P, ST, M_HEADS, M_V + 1], F32, sc)
                s_t = q.sem("ml_consts")
                ones, causal, anti = mm_[:, 0:P], mm_[:, P:2 * P], mm_[:, 2 * P:3 * P]
                q.dma(s_t, ones, ins["mats"][MAT["ones"]])
                q.dma(s_t, causal, ins["mats"][MAT["causal"]])
                q.dma(s_t, anti, ins["mats"][MAT["anti"]])
                tabs = q.dma(s_t, sel[:], ins["sel"])
                s_qk = q.sem("ml_qk_loaded")
                s_v = q.sem("ml_v_loaded")
                with ExitStack() as rs:
                    li = sb("ml_li", [R, S], F32, rs)
                    lf = sb("ml_lf", [R, S], F32, rs)
                    t1 = sb("ml_t1", [R, S], F32, rs)
                    t2 = sb("ml_t2", [R, S], F32, rs)
                    b = sb("ml_b", [R, S], F32, rs)
                    M = sb("ml_M", [R, S], F32, rs)
                    rst = sb("ml_reset", [R, S], F32, rs)
                    mrow = sb("ml_m", [R, 16], F32, rs)
                    dec = sb("ml_dec", [R, ST], F32, rs)
                    dex = sb("ml_decx", [R, R, ST], F32, rs)
                    QA = sb("ml_QA", [P, S], F32, rs)
                    QB = sb("ml_QB", [P, S], F32, rs)
                    s_g = q.sem("ml_gates_loaded")
                    gate = proj[16]
                    q.dma(s_g, li[0:32, :], gate[0:32, :], spilled[("proj", 16)])
                    q.dma(s_g, t1[32:36, :], gate[32:36, :])
                    q.dma(s_g, lf[0:32, :], gate[64:96, :])
                    q.dma(s_g, t2[32:36, :], gate[96:100, :])
                    g_in = q.dma(s_g, rst[:], ins["reset"])
                    for i in range(4):
                        qk_in = q.dma(s_qk, qk[:, i, :], proj[8 + i], spilled[("proj", 8 + i)])
                    for c in range(ST):
                        v_in = q.dma(s_v, v1[:, c, :, 0:M_V], mvs[:, c, :].rearrange("p (h v) -> p h v", h=M_HEADS),
                                     spilled[("mvs", 0)], spilled[("mvs", 1)])
                    v_one = V(lambda e: e.memset(v1[:, :, :, M_V:M_V + 1], 1.0))
                    V(lambda e: e.memset(QA[:], 0.0))
                    q0 = V(lambda e: e.memset(QB[:], 0.0))
                    r1 = V(lambda e: e.tensor_copy(li[32:36, :], t1[32:36, ::-1]), g_in)
                    r2 = V(lambda e: e.tensor_copy(lf[32:36, :], t2[32:36, ::-1]), g_in)
                    a1 = A(lambda e: e.activation(t1[:], lf[:], ACT.Abs), r2, r1)
                    a2 = A(lambda e: e.activation(t1[:], t1[:], ACT.Exp, scale=-1.0), a1)
                    a3 = A(lambda e: e.activation(t1[:], t1[:], ACT.Ln, bias=one[0:R, 0:1]), a2, one_set)
                    f1 = V(lambda e: e.scalar_tensor_tensor(out=lf[:], in0=lf[:], scalar=0.0, in1=t1[:], op0=ALU.min,
                                                            op1=ALU.subtract), a3)
                    b1 = V(lambda e: e.tensor_tensor_scan(b[:], rst[:], lf[:], 0.0, ALU.mult, ALU.add), f1)
                    s1 = V(lambda e: e.tensor_tensor(li[:], li[:], b[:], ALU.subtract), b1)
                    m0 = V(lambda e: e.memset(mrow[:, 0:1], NEG))
                    prev = [s1, m0]
                    for c in range(ST):
                        sl = slice(c * P, (c + 1) * P)
                        sc1 = V(lambda e, sl=sl, c=c: e.tensor_tensor_scan(M[:, sl], li[:, sl], li[:, sl],
                                                                         mrow[:, c:c + 1], ALU.max, ALU.max), prev)
                        prev = [V(lambda e, c=c: e.tensor_tensor(mrow[:, c + 1:c + 2], b[:, c * P + P - 1:c * P + P],
                                                                 M[:, c * P + P - 1:c * P + P], ALU.add), sc1)]
                    b3 = b[:].rearrange("p (c t) -> p c t", c=ST)
                    a3d = li[:].rearrange("p (c t) -> p c t", c=ST)
                    M3 = M[:].rearrange("p (c t) -> p c t", c=ST)
                    T1 = t1[:].rearrange("p (c t) -> p c t", c=ST)
                    T2 = t2[:].rearrange("p (c t) -> p c t", c=ST)
                    LF3 = lf[:].rearrange("p (c t) -> p c t", c=ST)
                    mp = mrow[:, 0:ST].unsqueeze(2).to_broadcast([R, ST, P])
                    me = M3[:, :, P - 1:P].to_broadcast([R, ST, P])
                    w1 = V(lambda e: e.tensor_tensor(T1, mp, M3, ALU.subtract), prev)
                    w2 = V(lambda e: e.tensor_tensor(LF3, a3d, me, ALU.subtract), prev)
                    w3 = V(lambda e: e.tensor_tensor(t2[:], b[:], M[:], ALU.add), prev)
                    w4 = V(lambda e: e.tensor_scalar(t2[:], t2[:], -1.0, EXP_CAP, ALU.mult, ALU.min), w3)
                    w5 = V(lambda e: e.tensor_tensor(dec[:].unsqueeze(2), mrow[:, 0:ST].unsqueeze(2), M3[:, :, P - 1:P],
                                                     ALU.subtract), prev)
                    e5 = A(lambda e: e.activation(dec[:], dec[:], ACT.Exp), w5)
                    outs = []
                    for r0, r1_, rv in ((0, 32, 1), (32, 36, -1)):
                        s_ = slice(r0, r1_)
                        o_ = slice(64 + r0, 64 + r1_)

                        def dirn(t, rows, rv=rv):
                            return t[rows, :] if rv == 1 else t[rows, ::-1]
                        outs.append(A(lambda e, s_=s_, o_=o_, d=dirn: e.activation(d(QA, o_), t1[s_, :], ACT.Exp), w1, q0))
                        outs.append(A(lambda e, s_=s_, o_=o_, d=dirn: e.activation(d(QB, o_), lf[s_, :], ACT.Exp), w2, q0))
                        outs.append(A(lambda e, s_=s_, d=dirn: e.activation(d(QB, s_), t2[s_, :], ACT.Exp), w4, q0))
                        outs.append(V(lambda e, s_=s_, d=dirn: e.tensor_copy(d(QA, s_), li[s_, :]), q0, prev))
                        outs.append(V(lambda e, s_=s_, d=dirn: e.tensor_scalar(d(nm, s_), M[s_, :], -1.0, None, ALU.mult),
                                      prev))
                    colr = []
                    for src, dst in ((QA, colsA), (QB, colsB)):
                        p = take()
                        for c in range(ST):
                            mm = T(lambda e, c=c, p=p, src=src: e.transpose(p.full[:, c * P:(c + 1) * P],
                                                                          src[:, c * P:(c + 1) * P], ident), outs, p.read)
                        d = A(lambda e, p=p, dst=dst: e.activation(dst[:].rearrange("p a b -> p (a b)"), p.full,
                                                                  ACT.Identity), mm)
                        p.read = [d]
                        colr.append(d)
                    dx = V(lambda e: e.tensor_tensor(dex[:], ident[0:R, 0:R].unsqueeze(2).to_broadcast([R, R, ST]),
                                                     dec[:].unsqueeze(1).to_broadcast([R, R, ST]), ALU.mult), e5)
                    p = take()
                    mm = T(lambda e, p=p: e.matmul(p.full[:, 0:R * ST], ones[0:R, :], dex[:].rearrange("p a b -> p (a b)"),
                                                   start=True, stop=True), dx, tabs, p.read)
                    dd = []
                    for h in range(M_HEADS):
                        for dr in range(2):
                            row = 32 * dr + h
                            hp = slice(64 * (h % 2), 64 * (h % 2) + 64)
                            dd.append(V(lambda e, h=h, dr=dr, row=row, hp=hp, p=p: e.tensor_copy(
                                decB[hp, h // 2, dr, :], p.full[hp, row * ST:(row + 1) * ST]), mm))
                    p.read = [dd[-1]]
                q.fence()
                q.stage("mlstm")
                ktok = sb("ml_ktok", [P, ST, 256], F32, sc)
                E = [[sb(f"ml_E{i}{d}", [P, ST, P], F32, sc) for d in range(2)] for i in range(2)]
                kw = [sb(f"ml_kw{i}", [P, ST, M_QK], F32, sc) for i in range(2)]
                C = sb("ml_C", [P, 2, ST, M_V + 1], F32, sc)
                hs = sb("ml_hs", [P, ST, 512], F32, sc)
                num = sb("ml_num", [P, 4, M_V + 1], F32, sc)
                dn = sb("ml_den", [P, 16], F32, sc)
                kt_done = []
                for hp in range(2):
                    p = take()
                    for c in range(ST):
                        mm = T(lambda e, c=c, p=p, hp=hp: e.transpose(p.full[:, c * P:(c + 1) * P],
                                                                    qk[:, 2 + hp, c * P:(c + 1) * P], ident), qk_in, p.read)
                    d = A(lambda e, p=p, hp=hp: e.activation(ktok[:, :, hp * P:(hp + 1) * P],
                                                             p.full.rearrange("p (c k) -> p c k", c=ST), ACT.Identity), mm)
                    p.read = [d]
                    kt_done.append(d)
                zC = V(lambda e: e.memset(C[:, :, 0, :], 0.0))
                e_free = [[None, None], [None, None]]
                kw_free = [None, None]
                c_free = [None, None]
                num_free, hs_last = None, {}
                def head(h):
                    nonlocal num_free
                    i, pr_, lo = h % 2, h // 2, 64 * (h % 2)
                    part = slice(lo, lo + 64)
                    ed = []
                    for dr in range(2):
                        row = 32 * dr + h
                        p = take()
                        hd = dr * 4 + h
                        for hf in range(2):
                            mm = T(lambda e, p=p, hf=hf, hd=hd: e.matmul(p.half[hf], sel[:, hd * P:(hd + 1) * P],
                                                                       nm[:, hf * HALF:(hf + 1) * HALF], start=True,
                                                                       stop=True), p.read)
                        Et = E[i][dr]
                        x1 = V(lambda e, p=p, Et=Et, row=row: e.tensor_tensor(
                            Et[:], p.full.rearrange("p (c t) -> p c t", c=ST),
                            colsA[:, :, row:row + 1].to_broadcast([P, ST, P]), ALU.add), mm, colr, e_free[i][dr])
                        p.read = [x1]
                        mk = causal if dr == 0 else anti
                        x2 = V(lambda e, Et=Et, mk=mk: e.tensor_tensor(
                            Et[:], Et[:], mk.unsqueeze(1).to_broadcast([P, ST, P]), ALU.add), x1)
                        ed.append(A(lambda e, Et=Et: e.activation(Et[:], Et[:], ACT.Exp), x2))
                    p = take()
                    for c in range(ST):
                        mm = T(lambda e, p=p, c=c: e.matmul(p.full[:, c * P:(c + 1) * P],
                                                            qk[part, 2 + pr_, c * P:(c + 1) * P],
                                                            qk[part, pr_, c * P:(c + 1) * P], start=True, stop=True),
                               p.read, qk_in)
                    st_ = []
                    for dr in range(2):
                        Et = E[i][dr]
                        st_.append(V(lambda e, p=p, Et=Et: e.tensor_tensor(
                            Et[:], Et[:], p.full.rearrange("p (c t) -> p c t", c=ST), ALU.mult), ed[dr], mm))
                    p.read = [st_[1]]
                    cd = []
                    for dr in range(2):
                        row = 32 * dr + h
                        kwt = kw[dr]
                        kd = V(lambda e, kwt=kwt, row=row, h=h: e.tensor_tensor(
                            kwt[:], ktok[:, :, h * 64:(h + 1) * 64],
                            colsB[:, :, 64 + row:64 + row + 1].to_broadcast([P, ST, M_QK]), ALU.mult), kt_done, kw_free[dr],
                            colr)
                        last = zC
                        for j0 in (0, 4):
                            p = take()
                            for j in range(j0, min(j0 + 4, ST - 1)):
                                c = j if dr == 0 else ST - 1 - j
                                mm = T(lambda e, p=p, j=j, c=c, kwt=kwt: e.matmul(
                                    p.full[part, (j % 4) * 256:(j % 4) * 256 + M_V + 1], kwt[:, c, :], v1[:, c, h, :],
                                    start=True, stop=True), kd, v_in, v_one, p.read)
                            kw_free[dr] = mm
                            for j in range(j0, min(j0 + 4, ST - 1)):
                                last = V(lambda e, p=p, j=j, dr=dr: e.scalar_tensor_tensor(
                                    out=C[part, dr, j + 1, :], in0=C[part, dr, j, :],
                                    scalar=decB[part, pr_, dr, j:j + 1],
                                    in1=p.full[part, (j % 4) * 256:(j % 4) * 256 + M_V + 1],
                                    op0=ALU.mult, op1=ALU.add), mm, last, c_free[h % 2])
                            p.read = [last]
                        cd.append(last)
                    for dr in range(2):
                        row = 32 * dr + h
                        for c0 in (0, 4):
                            pl = take()
                            for c in range(c0, c0 + 4):
                                ml = T(lambda e, pl=pl, c=c, dr=dr: e.matmul(
                                    pl.full[:, (c % 4) * 256:(c % 4) * 256 + M_V + 1], E[i][dr][:, c, :], v1[:, c, h, :],
                                    start=True, stop=True), st_[dr], pl.read)
                            pi = take()
                            for c in range(c0, c0 + 4):
                                j = c if dr == 0 else ST - 1 - c
                                mi = T(lambda e, pi=pi, c=c, dr=dr, j=j: e.matmul(
                                    pi.full[:, (c % 4) * 256:(c % 4) * 256 + M_V + 1], qk[part, pr_, c * P:(c + 1) * P],
                                    C[part, dr, j, :], start=True, stop=True), cd[dr], pi.read)
                            pi3 = pi.full.rearrange("p (c v) -> p c v", c=4)[:, :, 0:M_V + 1]
                            pl3 = pl.full.rearrange("p (c v) -> p c v", c=4)[:, :, 0:M_V + 1]
                            n1 = V(lambda e, pi3=pi3, c0=c0, row=row: e.tensor_tensor(
                                num[:], pi3, colsA[:, c0:c0 + 4, 64 + row:64 + row + 1].to_broadcast([P, 4, M_V + 1]),
                                ALU.mult), mi, num_free)
                            pi.read = [n1]
                            n2 = V(lambda e, pl3=pl3: e.tensor_tensor(num[:], num[:], pl3, ALU.add), n1, ml)
                            pl.read = [n2]
                            n3 = A(lambda e: e.activation(dn[:, 0:4].unsqueeze(2), num[:, :, M_V:M_V + 1], ACT.Abs), n2)
                            n4 = V(lambda e, c0=c0, row=row: e.tensor_tensor(
                                dn[:, 4:8].unsqueeze(2), dn[:, 0:4].unsqueeze(2), colsB[:, c0:c0 + 4, row:row + 1],
                                ALU.max), n3)
                            n5 = V(lambda e: e.reciprocal(dn[:, 8:12], dn[:, 4:8]), n4)
                            rb = dn[:, 8:12].unsqueeze(2).to_broadcast([P, 4, M_V])
                            dst = hs[:, c0:c0 + 4, h * M_V:(h + 1) * M_V]
                            if dr == 0:
                                n6 = V(lambda e, dst=dst, rb=rb: e.tensor_tensor(dst, num[:, :, 0:M_V], rb, ALU.mult), n5)
                            else:
                                n5 = V(lambda e, rb=rb: e.tensor_tensor(num[:, :, 0:M_V], num[:, :, 0:M_V], rb, ALU.mult), n5)
                                n6 = V(lambda e, dst=dst: e.tensor_tensor(dst, dst, num[:, :, 0:M_V], ALU.add), n5)
                            num_free = n6
                            hs_last[(h, c0)] = n6
                        e_free[i][dr] = ml
                    c_free[h % 2] = mi
                for h in range(M_HEADS):
                    head(h)
                q.fence()
                sq = E[0][0][:].rearrange("p a b -> p (a b)")
                ss = dn
                st = Store("ml_o", 2, sc)
                mo = [E[1][0][:].rearrange("p a b -> p (a b)"), E[1][1][:].rearrange("p a b -> p (a b)")]
                s_mo = [q.sem(f"ml_mo_loaded{i}") for i in range(2)]
                ss = sb("ml_ss", [P, 3, ST * M_HEADS], F32, sc)
                for c in range(ST):
                    sqt = sq[:, 0:HALF] if c % 2 == 0 else sq[:, HALF:S]
                    s1 = A(lambda e, c=c, sqt=sqt: e.activation(sqt, hs[:, c, :], ACT.Square),
                           [s2] if c >= 2 else None)
                    if c >= 1:
                        s2_prev = s2
                    s2 = V(lambda e, c=c, sqt=sqt: e.tensor_reduce(
                        ss[:, 0, c * M_HEADS:(c + 1) * M_HEADS], sqt.rearrange("p (h v) -> p h v", h=M_HEADS), AX.X,
                        ALU.add), s1)
                s3 = V(lambda e: e.tensor_scalar(ss[:, 0, :], ss[:, 0, :], 1.0 / M_V, None, ALU.mult), s2)
                rd, _ = rsqrt(ss[:, 0, :], eps[:, 0:1], ss[:, 1, :], ss[:, 2, :], s3)
                hn = []
                for c in range(ST):
                    hv = hs[:, c, :].rearrange("p (h v) -> p h v", h=M_HEADS)
                    hn.append(V(lambda e, c=c, hv=hv: e.tensor_tensor(
                        hv, hv, ss[:, 1, c * M_HEADS:(c + 1) * M_HEADS].unsqueeze(2).to_broadcast([P, M_HEADS, M_V]),
                        ALU.mult), rd))
                mo_free = [None, None]
                for h in range(M_HEADS):
                    ld = q.dma(s_mo[h % 2], mo[h % 2], proj[12 + h], spilled[("proj", 12 + h)], mo_free[h % 2])
                    p = take()
                    for c in range(ST):
                        mm = T(lambda e, p=p, c=c, h=h: e.transpose(p.full[:, c * P:(c + 1) * P],
                                                                   hs[:, c, h * M_V:(h + 1) * M_V], ident), hn[c], p.read)
                    t, fr = st.next()
                    d = V(lambda e, p=p, t=t, h=h: e.scalar_tensor_tensor(out=t[:], in0=p.full, scalar=vc("g_mh", h),
                                                                        in1=mo[h % 2], op0=ALU.mult, op1=ALU.mult),
                          mm, ld, fr)
                    p.read = [d]
                    mo_free[h % 2] = d
                    st.store(mixd[h], ("mix", h), d)
                return st.all()

        def layer_norm(name, write):
            with ExitStack() as sc:
                xc = sb(f"{name}_xc", [P, KT, S], F32, sc)
                sq = [sb(f"{name}_sq{i}", [P, HALF], F32, sc) for i in range(4)]
                pm = stat["pair"]
                pm.kept = False
                pv = take()
                sf, n, pm.read = [None] * 4, 0, []
                mean_done = [stat[("sum", 0)], stat[("sum", 1)]]
                for h in range(2):
                    c = slice(h * HALF, (h + 1) * HALF)
                    for k in range(KT):
                        xd = V(lambda e, k=k, h=h, c=c: e.tensor_tensor(xc[:, k, c], x[:, k, c], pm.half[h], ALU.subtract),
                               mean_done[h], x_ready[k])
                        i = n % 4
                        n += 1
                        sd = A(lambda e, k=k, i=i, c=c: e.activation(sq[i][:], xc[:, k, c], ACT.Square), xd, sf[i])
                        sf[i] = T(lambda e, k=k, h=h, i=i: e.matmul(pv.half[h], mean1024, sq[i][:], start=(k == 0),
                                                                   stop=(k == KT - 1)), sd, pv.read)
                    pm.read.append(xd)
                    stat[("sum", h)] = sf[i]

                def put(h, r, rd):
                    c = slice(h * HALF, (h + 1) * HALF)
                    later = []
                    for k in range(KT):
                        later.append(write(k, h, c, xc[:, k, c], r, rd))
                        if len(later) > 2:
                            later.pop(0)()
                    for f in later:
                        f()

                halves(pv, name, eps[:, 1:2], sc, put)

        def block2(l):
            q.stage(f"proj2_{l}")
            q.fence()
            mo = l * N_ADA2 * KT
            c1 = V(lambda e: e.tensor_scalar(cols[:, 24:32], mod2[:, mo + 8:mo + 16], 1.0, None, ALU.add),
                   [mod_done[(l + 1, i)] for i in range(3)])
            c2 = V(lambda e: e.tensor_scalar(cols[:, 32:40], mod2[:, mo + 16:mo + 24], 1.0, None, ALU.add))
            c3 = V(lambda e: e.tensor_scalar(cols[:, 16:17], vc("q_gain_2", l), A_DIM ** -0.5, None, ALU.mult))
            with ExitStack() as hs:
                h = [sb(f"h2{l}_hi", [P, KT, S], F32R, hs), sb(f"h2{l}_lo", [P, KT, S], F32R, hs)]

                rr = {}

                def write(k, hf, c, xc, r, rd):
                    td = V(lambda e: e.scalar_tensor_tensor(out=xc, in0=xc, scalar=cols[:, 24 + k:25 + k], in1=r,
                                                            op0=ALU.mult, op1=ALU.mult), rd, c1)
                    low = split_shifted(xc, mod2[:, mo + k:mo + k + 1], h[0][:, k, c], h[1][:, k, c], td)

                    def last_step():
                        rr[(k, hf)] = low()
                    return last_step

                layer_norm(f"ln{l}", write)
                ready = [(rr[(k, 0)], rr[(k, 1)]) for k in range(KT)]
                q.fence()
                hi, lo = (lambda k: h[0][:, k, :]), (lambda k: h[1][:, k, :])
                with ExitStack() as sc:
                    cst = sb(f"r2cos{l}", [P, S], F32, sc)
                    snt = sb(f"r2sin{l}", [P, S], F32, sc)
                    m2 = sb(f"r2mats{l}", [P, 2 * P], F32, sc)
                    s_t = q.sem(f"rope2_loaded{l}")
                    q.dma(s_t, cst[:], ins["rope2"][0])
                    q.dma(s_t, snt[:], ins["rope2"][1])
                    q.dma(s_t, m2[:, 0:P], ins["mats"][MAT["mean64"]])
                    tables = q.dma(s_t, m2[:, P:2 * P], ins["mats"][MAT["rot2"]])
                    his, los = Store(f"p2{l}_hi", 2, sc, F32R), Store(f"p2{l}_lo", 2, sc, F32R)
                    tmps = [[sb(f"p2{l}_{n}{i}", [P, S], F32, sc)[:] for n in ("raw", "sq", "u")] + [None]
                            for i in range(2)]
                    pending = []
                    for b in range(3):
                        blk = get(("in2", l, b))
                        both = gemm_pair(blk, hi, lo, ready) if b == 0 else None
                        for m in range(2):
                            nt = 2 * b + m
                            p, mm = both[m] if both else gemm(blk, m, KT, hi, lo, ready)
                            step(pending)
                            if nt < 5:
                                gc = cols[:, 16:17] if nt < 4 else vc("k_gain_2", l)
                                pending.append(rope_heads(his, los, tmps[nt % 2], m2[:, 0:P], m2[:, P:2 * P], cst[:], snt[:],
                                                          gc, nt, [tables, c3], p, mm))
                                next(pending[-1])
                            else:
                                while pending:
                                    step(pending)
                                raw = tmps[nt % 2][0]
                                d = A(lambda e, p=p, raw=raw: e.activation(raw, p.full, ACT.Identity), mm, tmps[nt % 2][3])
                                p.read = [d]
                                pv = take()
                                for j in range(ST):
                                    mt = T(lambda e, j=j, pv=pv, raw=raw: e.transpose(
                                        pv.full[:, j * P:(j + 1) * P], raw[:, j * P:(j + 1) * P], ident), d, pv.read)

                                def view(t, part):
                                    t4 = t[:].rearrange("p (a h d) -> p a h d", a=ST, h=2)
                                    return [(vsp[hd][:, :, 64 * part:64 * part + 64], t4[:, :, hd, :]) for hd in range(2)]
                                pv.read = [split_out(pv.full, his, los, None, None, ("v2", l), mt, view=view)]
                    done = his.all() + los.all()
                    spilled[("v", 0)] = spilled[("v", 1)] = spilled[("v2", l)]
                q.fence(done)
                with ExitStack() as sc:
                    st = Store(f"p2b{l}_o", 4, sc)
                    cu = sb(f"cu{l}", [P, S], F32, sc)
                    uu = sb(f"cuu{l}", [P, S], F32, sc)
                    ac = sb(f"cac{l}", [P, S], F32, sc)
                    conv_free = None
                    for b in range(3, 11):
                        blk = get(("in2", l, b))
                        for m in range(2):
                            nt = 2 * b + m
                            p, mm = gemm(blk, m, KT, hi, lo, ready)
                            if nt < 14:
                                t, fr = st.next()
                                fn = ACT.Identity if nt < 8 else ACT.Silu
                                d = A(lambda e, p=p, t=t, fn=fn: e.activation(t[:], p.full, fn), mm, fr)
                                p.read = [d]
                                st.store(proj[nt], ("proj", nt), d)
                                continue
                            what, tile = (nt - 14) % 4, (nt - 14) // 4

                            def w(j, tile=tile):
                                return vc("conv_w", (l * 3 + j) * 2 + tile)
                            if what == 0:
                                v0 = A(lambda e, p=p: e.activation(cu[:], p.full, ACT.Identity), mm, conv_free)
                                p.read = [v0]
                            elif what == 1:
                                v1_ = V(lambda e, p=p: e.tensor_tensor(uu[:], cu[:], p.full, ALU.mult), v0, mm)
                                p.read = [v1_]
                                v2 = V(lambda e, w=w: e.tensor_scalar(ac[:], uu[:], w(1), None, ALU.mult), v1_)
                                v3 = V(lambda e, w=w: e.scalar_tensor_tensor(out=ac[:, 1:S], in0=uu[:, 0:S - 1], scalar=w(0),
                                                                             in1=ac[:, 1:S], op0=ALU.mult, op1=ALU.add), v2)
                                v4 = V(lambda e, w=w: e.scalar_tensor_tensor(out=ac[:, 0:S - 1], in0=uu[:, 1:S], scalar=w(2),
                                                                             in1=ac[:, 0:S - 1], op0=ALU.mult, op1=ALU.add),
                                       v3)
                            elif what == 2:
                                v5 = V(lambda e, p=p: e.tensor_tensor(ac[:], ac[:], p.full, ALU.mult), v4, mm)
                                p.read = [v5]
                            else:
                                v6 = A(lambda e, p=p: e.activation(cu[:], p.full, ACT.Silu), mm, v1_)
                                p.read = [v6]
                                t, fr = st.next()
                                conv_free = V(lambda e, t=t: e.tensor_tensor(t[:], ac[:], cu[:], ALU.mult), v5, v6, fr)
                                st.store(mixd[4 + tile], ("mix", 4 + tile), conv_free)
                    done = st.all()
            q.fence(done)
            done = fourier(l)
            q.fence(done)
            with ExitStack() as ma:
                mixa = [sb(f"mix2a{l}_hi", [P, 4, S], F32R, ma), sb(f"mix2a{l}_lo", [P, 4, S], F32R, ma)]
                ra = attention(f"attn2_{l}", lambda hq: hq // 4, 4, None, 10, mixa)
                q.stage(f"out2_{l}")
                q.fence()
                mixb = [sb(f"mix2b{l}_hi", [P, 4, S], F32R, ma), sb(f"mix2b{l}_lo", [P, 4, S], F32R, ma)]
                rb = load_mix(f"mix2{l}", mixb, 4)
                stat_open()
                xa = [V(lambda e, k=k: e.tensor_scalar(x[:, k, :], x[:, k, :], ALPHA, None, ALU.mult)) for k in range(KT)]
                for c in range(4):
                    blk = get(("out2", l, c))
                    for m in range(2):
                        d = 2 * c + m
                        p, mm = gemm(blk, m, KT, lambda k: (mixa if k < 4 else mixb)[0][:, k % 4, :],
                                     lambda k: (mixa if k < 4 else mixb)[1][:, k % 4, :], ra + rb)
                        x_ready[d] = V(lambda e, p=p, d=d: e.scalar_tensor_tensor(
                            out=x[:, d, :], in0=p.full, scalar=cols[:, 32 + d:33 + d], in1=x[:, d, :],
                            op0=ALU.mult, op1=ALU.add), mm, xa[d], c2)
                        p.read = [x_ready[d]]
                        if d:
                            stat_mean(d - 1, False)
                stat_mean(KT - 1, False)
            q.fence()

            def write(k, hf, c, xc, r, rd):
                td = V(lambda e: e.tensor_tensor(xc, xc, r, ALU.mult), rd)

                def last_step():
                    x_parts[(k, hf)] = A(lambda e: e.activation(x[:, k, c], xc, ACT.Identity, scale=vc("ln_g", l * 8 + k),
                                                                bias=vc("ln_b", l * 8 + k)), td)
                return last_step
            x_parts = {}
            layer_norm(f"lno{l}", write)
            for k in range(KT):
                x_ready[k] = [x_parts[(k, 0)], x_parts[(k, 1)]]
            if l == 0:
                stat_all(False)

        def fourier(l):
            q.stage(f"fourier{l}")
            with ExitStack() as sc:
                cm = sb(f"fo{l}_mats", [P, 4 * P], F32, sc)
                ab = sb(f"fo{l}_ab", [P, 2, 2 * P], F32, sc)
                fu = sb(f"fo{l}_u", [P, 2, S], F32, sc)
                gf = sb(f"fo{l}_g", [P, 2, S], F32, sc)
                uh = sb(f"fo{l}_uhi", [P, 2, ST, 256], F32R, sc)
                ul = sb(f"fo{l}_ulo", [P, 2, ST, 256], F32R, sc)
                o = sb(f"fo{l}_out", [P, 2, S], F32, sc)
                s_c, s_u, s_g = q.sem(f"fo{l}_consts"), q.sem(f"fo{l}_uload"), q.sem(f"fo{l}_gload")
                for j, n in enumerate(("cosc", "sinc", f"fm{l}0", f"fm{l}1")):
                    cin = q.dma(s_c, cm[:, j * P:(j + 1) * P], ins["mats"][MAT[n]])
                for j in range(2):
                    u_in = q.dma(s_u, fu[:, j, :], proj[6 + j], spilled[("proj", 6 + j)])
                    g_in = q.dma(s_g, gf[:, j, :], proj[8 + j], spilled[("proj", 8 + j)])
                p = take()
                for g in range(2):
                    for j in range(2):
                        mm = T(lambda e, g=g, j=j, p=p: e.matmul(p.half[g][:, j * P:(j + 1) * P], cm[:, j * P:(j + 1) * P],
                                                                cm[:, (2 + g) * P:(3 + g) * P], start=True, stop=True),
                               cin, p.read)
                abd = A(lambda e, p=p: e.activation(ab[:], p.full.rearrange("p (g c) -> p g c", g=2)[:, :, 0:256],
                                                    ACT.Identity), mm)
                p.read = [abd]
                ud = []
                tf = [None, None]
                for g in range(2):
                    for t0 in (0, 4):
                        p = take()
                        for j in range(4):
                            mm = T(lambda e, g=g, j=j, p=p, t0=t0: e.matmul(
                                p.full[:, j * 256:(j + 1) * 256], fu[:, g, (t0 + j) * P:(t0 + j + 1) * P], ab[:, g, :],
                                start=True, stop=True), abd, u_in, p.read)
                        hi = uh[:, g, t0:t0 + 4, :].rearrange("p a b -> p (a b)")
                        lo = ul[:, g, t0:t0 + 4, :].rearrange("p a b -> p (a b)")
                        up = A(lambda e, p=p, hi=hi: e.activation(hi, p.full, ACT.Identity), mm)
                        dn = V(lambda e, p=p, hi=hi, lo=lo: e.tensor_tensor(lo, p.full, hi.bitcast(F32), ALU.subtract), up)
                        p.read = [dn]
                        ud.append(dn)
                for c in range(4):
                    p = None
                    for tb in range(2):
                        s, whi, wlo, wdone = get(("dft", l, c, tb))
                        if p is None:
                            p = take()
                        for g in range(2):
                            for k in range(ST):
                                for i, (a, b) in enumerate(((whi, uh), (whi, ul), (wlo, uh))):
                                    mm = T(lambda e, a=a, b=b, k=k, g=g, tb=tb, i=i, p=p: e.matmul(
                                        p.half[g][:, 0:256], b[:, g, k, tb * P:(tb + 1) * P], a[:, k * 256:(k + 1) * 256],
                                        start=(tb == 0 and k == 0 and i == 0), stop=(tb == 1 and k == ST - 1 and i == 2)),
                                        wdone, ud, p.read if tb == 0 else None)
                        W.used(s, mm)
                    res = p.full.rearrange("p (g c) -> p g c", g=2)[:, :, 0:256]
                    d = V(lambda e, res=res, c=c: e.tensor_tensor(o[:, :, c * 256:(c + 1) * 256], res,
                                                                  gf[:, :, c * 256:(c + 1) * 256], ALU.mult), mm, g_in)
                    p.read = [d]
                s_o = q.sem(f"fo{l}_stored")
                a1 = q.dma(s_o, mixd[6], o[:, 0, :], d)
                a2 = q.dma(s_o, mixd[7], o[:, 1, :])
                spilled[("mix", 6)] = spilled[("mix", 7)] = [a2]
                return [a2]

        def finish():
            s_out = q.sem("out_stored")
            for k in range(KT):
                fin = q.dma(s_out, out[:, k, :], x[:, k, :], x_ready[k], queue="sync")
            return fin

        def final_norm():
            q.stage("final1")
            q.fence()
            with ExitStack() as sc:
                parts = {}

                def write(h, r, rd):
                    c = slice(h * HALF, (h + 1) * HALF)
                    for k in range(KT):
                        parts[(k, h)] = V(lambda e, k=k: e.scalar_tensor_tensor(
                            out=x[:, k, c], in0=x[:, k, c], scalar=vc("g_final", k), in1=r, op0=ALU.mult, op1=ALU.mult), rd)

                halves(stat["pair"], "fin", eps[:, 0:1], sc, write)
                for k in range(KT):
                    x_ready[k] = [parts[(k, 0)], parts[(k, 1)]]
            stat_all(False)

        stages = [("ffn1", lambda: ffn(1, 2)), ("mixer1", mixer1), ("ffn2", lambda: ffn(2, 8)), ("final", final_norm),
                  ("b0", lambda: block2(0)), ("b1", lambda: block2(1))]
        for name, run in stages:
            run()
            if name == "ffn2":
                while W.taken < len(plan) and plan[W.taken][0] == "ada":
                    W.advance()
                    ada_finish()
            if name == stop:
                break
        q.end = finish()
        q.emit(ctx.enter_context(nc.Block()))



def tiles(w, width=256, cols=None):
    if cols is not None:
        w = np.concatenate([w, np.zeros((w.shape[0], 1), w.dtype)], 1)[:, cols]
    k, n = w.shape
    return np.ascontiguousarray(w.reshape(k // P, P, n // width, width).transpose(2, 1, 0, 3)
                                .reshape(n // width, P, -1))


def shape_constants():
    f = np.float32
    m = {}
    m["mean1024"] = np.full((P, P), 1 / 1024, f)
    blk = np.kron(np.eye(2), np.ones((64, 64)))
    m["mean64"] = (blk / 64).astype(f)
    m["mean128"] = np.full((P, P), 1 / 128, f)
    m["ones"] = np.ones((P, P), f)
    m["ident"] = np.eye(P, dtype=f)
    r1 = np.zeros((64, 64), f)
    for d in range(8):
        r1[d + 8, d] = -1.0
        r1[d, d + 8] = 1.0
    m["rot1"] = np.kron(np.eye(2), r1).astype(f)
    r2 = np.zeros((64, 64), f)
    for h in (0, 32):
        for d in range(16):
            r2[h + d + 16, h + d] = -1.0
            r2[h + d, h + d + 16] = 1.0
    m["rot2"] = np.kron(np.eye(2), r2).astype(f)
    ang = 2 * np.pi * np.outer(np.arange(64), np.arange(64)) / 64
    m["cosc"] = np.kron(np.eye(2), np.cos(ang)).astype(f)
    m["sinc"] = np.kron(np.eye(2), np.sin(ang)).astype(f)
    i = np.arange(P)
    m["causal"] = np.where(i[:, None] <= i[None, :], 0.0, NEG).astype(f)
    m["anti"] = np.where(i[:, None] >= i[None, :], 0.0, NEG).astype(f)
    t = 2 * np.pi * (np.outer(np.arange(S), np.arange(S)) % S) / S
    dft = np.stack([np.cos(t) / 256, -np.sin(t) / 256]).astype(f).reshape(2, KT, P, S)
    inv1 = (f(500000.0) ** (f(-2.0) * np.arange(8, dtype=f) / f(16))).astype(f)
    a1 = (np.arange(S, dtype=f)[:, None] * inv1[None, :]).astype(f)
    c1, s1 = np.ones((64, S), f), np.zeros((64, S), f)
    for d in range(16):
        c1[d], s1[d] = np.cos(a1[:, d % 8]), np.sin(a1[:, d % 8])
    inv2 = (f(1.0) / (f(10000.0) ** (np.arange(0, 32, 2, dtype=f) / f(32)))).astype(f)
    row = np.repeat(np.arange(S // 64, dtype=f), 64)[:, None] * inv2
    col = np.tile(np.arange(64, dtype=f), S // 64)[:, None] * inv2
    c2, s2 = np.zeros((64, S), f), np.zeros((64, S), f)
    for d in range(64):
        a = (row if d < 32 else col)[:, d % 16]
        c2[d], s2[d] = np.cos(a), np.sin(a)
    rope1 = np.stack([np.tile(c1, (2, 1)), np.tile(s1, (2, 1))])
    rope2 = np.stack([np.tile(c2, (2, 1)), np.tile(s2, (2, 1))])
    j = np.abs(np.arange(1920)[None, :] - 896 - np.arange(P)[:, None])
    count = (j <= 64).astype(int) + ((j % 4 == 0) & (j <= 256)) + (j % 16 == 0)
    band = np.where(count > 0, np.log(np.maximum(count, 1)), NEG).astype(f)
    sel = np.zeros((36, 8, P), f)
    for d in range(2):
        for h in range(4):
            sel[32 * d + h, d * 4 + h] = 1.0
    reset = np.ones((36, S), f)
    reset[:, ::P] = 0.0
    return m, dft, rope1, rope2, band, sel.reshape(36, -1), reset


def layouts(i):
    a = {k: np.asarray(v) for k, v in i.items()}
    m, dft, rope1, rope2, band, sel, reset = shape_constants()
    for l in range(2):
        for g in range(2):
            z = np.zeros((P, P), np.float32)
            z[0:64, 0:64] = a["f_mix_2"][l, 2 * g]
            z[64:, 64:] = a["f_mix_2"][l, 2 * g + 1]
            m[f"fm{l}{g}"] = z
    vec = np.zeros((P, NVEC), np.float32)

    def put(name, v):
        o, n = VEC[name]
        vec[:, o:o + n] = v

    def colsof(v):
        return v.reshape(-1, P).T

    put("c", colsof(a["c"]))
    put("b_ada", colsof(a["b_ada"]))
    for n in ("g_ffn1", "g_mix", "g_ffn2", "g_final", "g_mh"):
        put(n, colsof(a[n]))
    put("g_q", np.tile(a["g_q"][0], 2)[:, None])
    put("g_k", np.tile(a["g_k"][0], 2)[:, None])
    put("c_2", colsof(a["c_2"]))
    put("b_ada_2", colsof(a["b_ada_2"]))
    put("q_gain_2", np.tile(a["q_gain_2"], (1, 2)).T)
    put("k_gain_2", np.tile(a["k_gain_2"], (1, 2)).T)
    put("conv_w", a["conv_w_2"].reshape(-1, P).T)
    put("ln_g", colsof(a["ln_g_2"]))
    put("ln_b", colsof(a["ln_b_2"]))
    gb = a["gate_bias"][0]
    o = VEC["gate_bias"][0]
    for r0, g in ((0, 0), (32, 2), (64, 1), (96, 3)):
        vec[r0:r0 + 4, o] = gb[g]

    w = a["w_in"][0]
    R = np.arange
    mq, mk, mv, mo, mg = R(0, 256), R(256, 512), R(512, 1024), R(1024, 1536), R(1536, 1552)
    aq, ak, av = R(1552, 2064), R(2064, 2576), R(2576, 3088)
    gate_cols = np.full(P, -1)
    for r0, g in ((0, 0), (32, 2), (64, 1), (96, 3)):
        gate_cols[r0:r0 + 4] = mg[4 * g:4 * g + 4]
    sizes = (512, 128, 128, 512, 256, 256, 256, 256, 256, 256)
    st = np.cumsum((0,) + sizes)
    Q, K, V_, GA, CU, CB, CC, GC, FU, GF = (R(st[n], st[n + 1]) for n in range(10))
    h = [slice(0, P), slice(P, 256)]
    order2 = np.concatenate([Q, K, V_, FU, GF, GA] + [x_[s_] for s_ in h for x_ in (CU, CC, CB, GC)])
    gu = []
    for n in (1, 2):
        g = a[f"w_gu{n}"][0].reshape(KT, P, 2, FF_TILES, P).transpose(3, 1, 0, 2, 4)
        gu.append(np.ascontiguousarray(g).reshape(FF_TILES, P, BLK))
    return {"in_" + n: v for n, v in {
        "xT": np.ascontiguousarray(a["x"][0].T.reshape(KT, P, S).transpose(1, 0, 2)),
        "vec": vec, "mats": np.stack([m[n] for n in MATS]), "dft": dft, "rope1": rope1, "rope2": rope2,
        "band": band, "sel": sel, "reset": reset,
        "w_ada": a["w_ada"][0], "w_ada_2": a["w_ada_2"],
        "w_gu1": gu[0], "w_gu2": gu[1],
        "w_down1": a["w_down1"][0].reshape(FF_TILES, P, D), "w_down2": a["w_down2"][0].reshape(FF_TILES, P, D),
        "w_in": tiles(w, cols=np.concatenate([aq, ak, av, mv, mq, mk, mo])),
        "w_in_gate": tiles(w, P, gate_cols)[0],
        "w_out": a["w_out"][0].reshape(KT, P, D),
        "w_in_2": np.stack([tiles(a["w_in_2"][l], cols=order2) for l in range(2)]),
        "w_out_2": a["w_out_2"].reshape(2, KT, P, D),
    }.items()}


def program(nc, arrays, stop=None):
    ins = {}
    for n, v in arrays.items():
        ins[n[3:]] = nc.dram_tensor(n, list(v.shape), mybir.dt.from_np(v.dtype), kind="ExternalInput").ap()
    out = nc.dram_tensor("out", [P, KT, S], F32, kind="ExternalOutput").ap()
    build(nc, ins, out, stop)


def kernel(**inputs):
    import concourse.bacc as bacc
    from concourse.bass_utils import run_bass_kernel_spmd

    arrays = layouts(inputs)
    nc = bacc.Bacc("TRN2", target_bir_lowering=False, num_devices=1)
    program(nc, arrays)
    res = run_bass_kernel_spmd(nc, [arrays], core_ids=[0])
    y = np.asarray(res.results[0]["out"])
    return np.ascontiguousarray(y.transpose(1, 0, 2).reshape(D, S).T)[None]
```

```python
from contextlib import ExitStack

import numpy as np

import concourse.bass as bass
from concourse import mybir

F32 = mybir.dt.float32
F32R = mybir.dt.float32r
ALU = mybir.AluOpType
ACT = mybir.ActivationFunctionType
AX = mybir.AxisListType

P = 128
S = 1024
D = 1024
KT = D // P
ST = S // P
HALF = 512
EPS = 1e-6
LN_EPS = 1e-5
NEG = -1e30
FF_TILES = 22
FF_GROUPS = (5, 5, 4, 4, 4)
PROJ_ORDER = (0, 1, 2, 3, 4, 5, 12, 6, 7, 8, 9, 10, 11)
A_SLOTS = 6
RAW = 2
EARLY = 8
BLK = 2048
M_HEADS, M_QK, M_V = 4, 64, 128
A_HEADS, A_DIM = 8, 64
EXP_CAP = 88.0
ALPHA = 4.0 ** 0.25
N_ADA1, N_ADA2 = 9, 3

VEC = {}
_at = 0
for _name, _n in (("c", 8), ("b_ada", 72), ("g_ffn1", 8), ("g_mix", 8), ("g_ffn2", 8), ("g_final", 8),
                  ("g_mh", 4), ("g_q", 1), ("g_k", 1), ("c_2", 8), ("b_ada_2", 48), ("q_gain_2", 2),
                  ("k_gain_2", 2), ("conv_w", 12), ("ln_g", 16), ("ln_b", 16), ("gate_bias", 1)):
    VEC[_name] = (_at, _n)
    _at += _n
NVEC = _at
MATS = ("mean1024", "mean64", "ones", "ident", "rot1", "rot2", "cosc", "sinc", "causal", "anti",
        "fm00", "fm01", "fm10", "fm11")
MAT = {n: i for i, n in enumerate(MATS)}


class Op:

    def __init__(self, fn, after, sem):
        self.fn, self.after, self.sem, self.counted, self.value = fn, after, sem, False, 0


class Loaded:

    def __init__(self, sem, value):
        self.sem, self.value = sem, value


class Load:

    def __init__(self, fn, after, sem):
        self.fn, self.after, self.sem = fn, after, sem


class Queues:

    def __init__(self, nc, ctx):
        self.nc, self.ctx = nc, ctx
        self.q = {n: [] for n in ("tensor", "vector", "scalar", "gpsimd", "sync")}
        self.last = {}
        self.held = {n: [] for n in self.q}
        self.dma_count = {}
        self.guard = []
        self.stage("start")

    def sem(self, name):
        return self.ctx.enter_context(self.nc.semaphore(name))

    def stage(self, name):
        self.sems = {n: self.sem(f"{name}_{n}") for n in ("tensor", "vector", "scalar")}

    def put(self, engine, fn, after):
        flat = [a for a in self.held[engine]]
        self.held[engine] = []
        stack = list(after)
        while stack:
            a = stack.pop()
            if a is None:
                continue
            if isinstance(a, (list, tuple)):
                stack.extend(a)
            else:
                flat.append(a)
        for a in flat:
            if isinstance(a, Op):
                a.counted = True
        op = Op(fn, flat, self.sems[engine])
        self.q[engine].append(op)
        self.last[engine] = op
        return op

    def T(self, fn, *after):
        return self.put("tensor", fn, after)

    def V(self, fn, *after):
        return self.put("vector", fn, after)

    def A(self, fn, *after):
        return self.put("scalar", fn, after)

    def dma(self, sem, out, in_, *after, queue="gpsimd", early=None):
        if early is None:
            flat = list(self.held[queue])
            self.held[queue] = []
        else:
            flat = list(early)
        stack = list(after)
        while stack:
            a = stack.pop()
            if a is None:
                continue
            if isinstance(a, (list, tuple)):
                stack.extend(a)
            else:
                flat.append(a)
        for a in flat:
            if isinstance(a, Op):
                a.counted = True
        self.q[queue].append(Load(lambda e, out=out, in_=in_: e.dma_start(out, in_), flat, sem))
        n = self.dma_count.get(id(sem), 0) + 16
        self.dma_count[id(sem)] = n
        return Loaded(sem, n)

    def first(self, sem, out, in_, *after, early=None):
        return self.dma(sem, out, in_, self.guard if early is None else early, after, queue="sync")

    def fence(self, *more):
        done = [self.last[e] for e in ("tensor", "vector", "scalar") if e in self.last]
        extra = [x for m in more for x in (m if isinstance(m, (list, tuple)) else [m])]
        for e in ("vector", "scalar", "gpsimd"):
            self.held[e] = self.held[e] + done + extra
        self.guard = done + extra
        for op in done:
            op.counted = True

    def emit(self, block):
        counts = {}
        for ops in self.q.values():
            for op in ops:
                if isinstance(op, Op) and op.counted:
                    counts[id(op.sem)] = counts.get(id(op.sem), 0) + 1
                    op.value = counts[id(op.sem)]

        def run(name):
            def body(engine):
                seen = {}
                for op in self.q[name]:
                    need = {}
                    for a in op.after:
                        if a.value > max(seen.get(id(a.sem), 0), need.get(id(a.sem), (0, 0))[1]):
                            need[id(a.sem)] = (a.sem, a.value)
                    for key, (sem, value) in need.items():
                        engine.wait_ge(sem, value)
                        seen[key] = value
                    ins = op.fn(engine)
                    if isinstance(op, Load):
                        ins.then_inc(op.sem, 16)
                    elif op.counted:
                        ins.then_inc(op.sem, 1)
                if name == "sync":
                    engine.wait_ge(self.end.sem, self.end.value)
            return body

        block.tensor(run("tensor"))
        block.vector(run("vector"))
        block.scalar(run("scalar"))
        block.gpsimd(run("gpsimd"))
        block.sync(run("sync"))


class Pair:

    def __init__(self, tensor, i):
        self.full = tensor[:, 2 * i:2 * i + 2, :].rearrange("p a b -> p (a b)")
        self.half = [tensor[:, 2 * i + h, :] for h in range(2)]
        self.read = []
        self.kept = False


class Weights:

    def __init__(self, q, sb, plan, ada_step):
        self.q, self.plan, self.ada_step = q, plan, ada_step
        self.raw = [sb(f"w_raw{i}", [P, BLK], F32) for i in range(RAW)]
        self.hi = [sb(f"w_hi{i}", [P, BLK], F32R) for i in range(2)]
        self.lo = [sb(f"w_lo{i}", [P, BLK], F32R) for i in range(2)]
        self.sem = [q.sem(f"w_loaded{i}") for i in range(RAW)]
        self.early_sem = [q.sem(f"w_early_loaded{i}") for i in range(EARLY)]
        with ExitStack() as scope:
            self.early = [sb(f"w_early{i}", [P, BLK], F32, scope) for i in range(EARLY)]
        self.raw_read = [[] for _ in range(RAW)]
        self.landed = {}
        self.last_use = [[], []]
        self.issued = self.taken = self.split = 0
        self.ready = []
        for _ in range(EARLY + RAW):
            self.issue()

    def issue(self):
        n = self.issued
        if n >= len(self.plan):
            return
        _, src, shape, _ = self.plan[n]
        size = int(np.prod(shape))
        dst = (self.early[n] if n < EARLY else self.raw[n % RAW])[:, 0:size]
        if len(shape) == 2:
            dst = dst.rearrange("p (a b) -> p a b", a=shape[0])
        sem = self.early_sem[n] if n < EARLY else self.sem[n % RAW]
        self.landed[n] = self.q.dma(sem, dst, src, self.raw_read[n % RAW], queue="sync")
        self.issued += 1

    def advance(self):
        n = self.taken
        kind, _, shape, tag = self.plan[n]
        size = int(np.prod(shape))
        raw = (self.early[n] if n < EARLY else self.raw[n % RAW])[:, 0:size]
        if kind == "ada":
            done = self.ada_step(raw, tag, self.landed[n])
        else:
            s = self.split % 2
            hi, lo = self.hi[s][:, 0:size], self.lo[s][:, 0:size]
            up = self.q.A(lambda e: e.activation(hi, raw, ACT.Identity), self.landed[n], self.last_use[s])
            done = self.q.V(lambda e: e.tensor_tensor(lo, raw, hi.bitcast(F32), ALU.subtract), up)
            self.ready.append((s, tag, hi, lo, done))
            self.split += 1
        self.taken += 1
        if n >= EARLY:
            self.raw_read[n % RAW] = [done]
            self.issue()

    def get(self, tag):
        while not self.ready:
            self.advance()
        s, got, hi, lo, done = self.ready.pop(0)
        assert got == tag, (got, tag)
        while self.taken < len(self.plan) and not self.ready:
            self.advance()
        return s, hi, lo, done

    def prepare(self):
        while not self.ready:
            self.advance()

    def used(self, s, op):
        self.last_use[s] = [op]


def build(nc, ins, out, stop=None):
    ctx = ExitStack()
    with ctx:
        q = Queues(nc, ctx)
        T, V, A = q.T, q.V, q.A

        def sb(name, shape, dt, scope=ctx):
            return scope.enter_context(nc.sbuf_tensor(name, shape, dt))

        psum = ctx.enter_context(nc.psum_tensor("psum", [P, 8, HALF], F32))
        pairs = [Pair(psum, i) for i in range(4)]
        turn = [0]

        def take():
            while pairs[turn[0] % 4].kept:
                turn[0] += 1
            turn[0] += 1
            return pairs[(turn[0] - 1) % 4]

        x = sb("x", [P, KT, S], F32)
        vec = sb("vec", [P, NVEC], F32)
        mats = sb("mats", [P, 2 * P], F32)
        mod1 = sb("mod1", [P, N_ADA1 * KT], F32)
        mod2 = sb("mod2", [P, 2 * N_ADA2 * KT], F32)
        cs = sb("cs", [P, KT], F32)
        cols = sb("cols", [P, 64], F32)
        acc = sb("ada_acc", [P, D], F32)
        one = sb("one", [P, 1], F32)
        eps = sb("eps", [P, 2], F32)
        sqh = [sb(f"sq{h}", [P, HALF], F32) for h in range(2)]
        mean1024, ident = mats[:, 0:P], mats[:, P:2 * P]

        proj = nc.dram_tensor("proj_scratch", [24, P, S], F32).ap()
        qk_hi = nc.dram_tensor("qk_hi_scratch", [8, P, S], F32R).ap()
        qk_lo = nc.dram_tensor("qk_lo_scratch", [8, P, S], F32R).ap()
        vsp = nc.dram_tensor("v_split_scratch", [2, P, ST * 4, P], F32R).ap()
        mvs = nc.dram_tensor("mv_rows", [P, ST, 512], F32).ap()
        ml_cols = nc.dram_tensor("ml_columns", [2, P, S], F32).ap()
        ml_nm = nc.dram_tensor("ml_minus_M", [36, S], F32).ap()
        ml_dex = nc.dram_tensor("ml_decays", [36, 36 * ST], F32).ap()
        rows_out = []
        mixd = nc.dram_tensor("mix_scratch", [KT, P, S], F32).ap()

        s_const, s_x = q.sem("const_loaded"), [q.sem(f"x_loaded{i}") for i in range(2)]
        vec_in = q.dma(s_const, vec[:], ins["vec"], queue="sync")
        q.dma(s_const, mats[:, 0:P], ins["mats"][MAT["mean1024"]], vec_in, queue="sync")
        consts = q.dma(s_const, mats[:, P:2 * P], ins["mats"][MAT["ident"]], queue="sync")
        x_in = []
        for i in range(2):
            x_in += [q.dma(s_x[i], x[:, 4 * i:4 * i + 4, :], ins["xT"][:, 4 * i:4 * i + 4, :], queue="sync")] * 4
        one_set = V(lambda e: e.memset(one[:], 1.0))
        V(lambda e: e.memset(eps[:, 0:1], EPS))
        eps_set = V(lambda e: e.memset(eps[:, 1:2], LN_EPS))

        def vc(name, i=0, n=1):
            return vec[:, VEC[name][0] + i:VEC[name][0] + i + n]

        cs_set = A(lambda e: e.activation(cs[:], vc("c", 0, 8), ACT.Silu), consts)
        mod_done = {}
        ada = {"free": [], "last": None, "due": []}

        def ada_step(raw, tag, landed):
            layer, i, kp = tag
            if kp == 0:
                ada_finish()
            for j in range(2):
                k = 2 * kp + j
                w = raw[:, j * D:(j + 1) * D]
                cv = cs[:, k:k + 1] if layer == 0 else vc("c_2", k)
                if k == 0:
                    ada["last"] = V(lambda e, w=w, cv=cv: e.tensor_scalar(acc[:], w, cv, None, ALU.mult),
                                    landed, cs_set, consts, ada["free"])
                else:
                    ada["last"] = V(lambda e, w=w, cv=cv: e.scalar_tensor_tensor(
                        out=acc[:], in0=w, scalar=cv, in1=acc[:], op0=ALU.mult, op1=ALU.add), landed, ada["last"])
            if kp == KT // 2 - 1:
                ada["due"].append((layer, i, ada["last"]))
                ada["free"] = None
            return ada["last"]

        def ada_finish():
            while ada["due"]:
                layer, i, done = ada["due"].pop(0)
                p = take()
                for j in range(KT):
                    mm = T(lambda e, j=j, p=p: e.transpose(p.full[:, j * P:(j + 1) * P], acc[:, j * P:(j + 1) * P],
                                                          ident), done, p.read, consts)
                dst = mod1[:, i * KT:(i + 1) * KT] if layer == 0 else \
                    mod2[:, ((layer - 1) * N_ADA2 + i) * KT:((layer - 1) * N_ADA2 + i + 1) * KT]
                bias = vc("b_ada", i * KT, KT) if layer == 0 else vc("b_ada_2", ((layer - 1) * N_ADA2 + i) * KT, KT)
                d = V(lambda e, p=p, dst=dst: e.tensor_reduce(dst, p.full.rearrange("p (j k) -> p j k", j=KT), AX.X,
                                                              ALU.add), mm)
                p.read = [d]
                d = V(lambda e, dst=dst, bias=bias: e.tensor_tensor(dst, dst, bias, ALU.add), d)
                mod_done[(layer, i)] = d
                ada["free"] = [mm]

        plan = []
        ada_list = [(0, i, kp) for i in range(N_ADA1) for kp in range(4)] + \
                   [(l, i, kp) for l in (1, 2) for i in range(N_ADA2) for kp in range(4)]

        def plan_ada(n):
            for _ in range(min(n, len(ada_list))):
                l, i, kp = ada_list.pop(0)
                w = ins["w_ada"] if l == 0 else ins["w_ada_2"][l - 1]
                src = w[2 * kp * P:(2 * kp + 2) * P, i * D:(i + 1) * D].rearrange("(k p) n -> p k n", p=P)
                plan.append(("ada", src, (2, D), (l, i, kp)))

        def ffn_order():
            first, seq = 0, []
            starts = np.cumsum((0,) + FF_GROUPS)
            for g, n in enumerate(FF_GROUPS):
                fs = list(range(starts[g], starts[g + 1]))
                seq += [("gu", f) for f in (fs if g == 0 else fs[1:])]
                if g + 1 < len(FF_GROUPS):
                    seq.append(("gu", int(starts[g + 1])))
                seq.append(("down", g))
            return [(k, int(n)) for k, n in seq], starts

        def plan_ffn(n):
            seq, starts = ffn_order()
            for kind, i in seq:
                if kind == "gu":
                    plan.append(("w", ins[f"w_gu{n}"][i], (BLK,), ("gu", n, i)))
                    plan_ada(1)
                else:
                    for c in range(4):
                        src = ins[f"w_down{n}"][int(starts[i]):int(starts[i + 1]), :, c * 256:(c + 1) * 256]
                        plan.append(("w", src.rearrange("f p c -> p f c"), (FF_GROUPS[i], 256), ("down", n, i, c)))

        plan_ada(8)
        plan_ffn(1)
        for b in PROJ_ORDER:
            if b == 12:
                plan.append(("w", ins["w_in_gate"], (KT * P,), ("in1", b)))
            else:
                plan.append(("w", ins["w_in"][b], (BLK,), ("in1", b)))
            if b >= 4:
                plan_ada(1)
        for c in range(4):
            plan.append(("w", ins["w_out"][:, :, c * 256:(c + 1) * 256].rearrange("f p c -> p f c"), (KT, 256), ("out1", c)))
        plan_ffn(2)
        plan_ada(99)
        for l in range(2):
            for b in range(11):
                plan.append(("w", ins["w_in_2"][l, b], (BLK,), ("in2", l, b)))
            for c in range(4):
                for t in range(2):
                    plan.append(("w", ins["dft"][t][:, :, c * 256:(c + 1) * 256].rearrange("f p c -> p f c"),
                                 (KT, 256), ("dft", l, c, t)))
            for c in range(4):
                plan.append(("w", ins["w_out_2"][l][:, :, c * 256:(c + 1) * 256].rearrange("f p c -> p f c"), (KT, 256),
                             ("out2", l, c)))
        W = Weights(q, sb, plan, ada_step)

        def get(tag):
            ada_finish()
            return W.get(tag)

        def gemm(blk, m, n, hi, lo, ready, width=256, order=None):
            s, whi, wlo, wdone = blk
            p = take()
            order = order or list(range(n))
            for h in range(2):
                for k in order:
                    for i, (a, b) in enumerate(((whi, hi), (whi, lo), (wlo, hi))):
                        mm = T(lambda e, a=a, b=b(k), k=k, h=h, i=i, p=p: e.matmul(
                            p.half[h], a[:, k * width + m * P:k * width + (m + 1) * P], b[:, h * HALF:(h + 1) * HALF],
                            start=(k == order[0] and i == 0), stop=(k == order[-1] and i == 2)),
                            wdone, p.read if k == order[0] and i == 0 else None,
                            ready[k][h] if isinstance(ready[k], tuple) else ready[k])
            W.used(s, mm)
            return p, mm

        def gemm_pair(blk, hi, lo, ready):
            s, whi, wlo, wdone = blk
            ps = [take(), take()]
            mms = {}
            for h in range(2):
                for m in range(2):
                    for k in range(KT):
                        for i, (a, b) in enumerate(((whi, hi), (whi, lo), (wlo, hi))):
                            mms[m] = T(lambda e, a=a, b=b(k), k=k, h=h, m=m, i=i: e.matmul(
                                ps[m].half[h], a[:, k * 256 + m * P:k * 256 + (m + 1) * P], b[:, h * HALF:(h + 1) * HALF],
                                start=(k == 0 and i == 0), stop=(k == KT - 1 and i == 2)),
                                wdone, ps[m].read if k == 0 and i == 0 else None, ready[k][h])
            W.used(s, mms[1])
            return [(ps[m], mms[m]) for m in range(2)]

        def gemm_rows(blk, hi, lo, tt0, ready):
            s, whi, wlo, wdone = blk
            p = take()
            for j in range(4):
                for k in range(KT):
                    for i, (a, b) in enumerate(((whi, hi), (whi, lo), (wlo, hi))):
                        mm = T(lambda e, a=a, b=b(k), k=k, j=j, i=i, p=p: e.matmul(
                            p.full[:, j * 256:(j + 1) * 256], b[:, (tt0 + j) * P:(tt0 + j + 1) * P],
                            a[:, k * 256:(k + 1) * 256], start=(k == 0 and i == 0), stop=(k == KT - 1 and i == 2)),
                            wdone, p.read if j == 0 else None, list(ready[k]))
            W.used(s, mm)
            return p, mm

        stat = {"pair": None, "free": [None, None], "sq": {}}

        def stat_open():
            stat["pair"] = take()
            stat["pair"].kept = True

        def stat_square(d):
            for h in range(2):
                stat["sq"][(d, h)] = A(lambda e, h=h: e.activation(sqh[h][:], x[:, d, h * HALF:(h + 1) * HALF], ACT.Square),
                                       x_ready[d], stat["free"][h])

        def stat_mean(d):
            p = stat["pair"]
            for h in range(2):
                mm = T(lambda e, h=h: e.matmul(p.half[h], mean1024, sqh[h][:], start=(d == 0), stop=(d == KT - 1)),
                       stat["sq"][(d, h)], p.read if d == 0 else None, consts)
                stat["free"][h] = stat[("sum", h)] = mm

        def stat_add(d, acc_, squares=True, free=None):
            if squares:
                for h in range(2):
                    c = slice(h * HALF, (h + 1) * HALF)
                    dst = acc_[:, c] if d == 0 else sqh[h][:]
                    sq = A(lambda e, c=c, dst=dst: e.activation(dst, x[:, d, c], ACT.Square), x_ready[d],
                           stat["free"][h], free)
                    stat[("acc", h)] = sq if d == 0 else V(lambda e, h=h, c=c: e.tensor_tensor(
                        acc_[:, c], acc_[:, c], sqh[h][:], ALU.add), sq, stat[("acc", h)])
                    stat["free"][h] = stat[("acc", h)]
            elif d:
                a = x[:, 0, :] if d == 1 else acc_[:]
                op = V(lambda e: e.tensor_tensor(acc_[:], a, x[:, d, :], ALU.add), x_ready[0] if d == 1 else None,
                       x_ready[d], free)
                stat[("acc", 0)] = stat[("acc", 1)] = op

        def stat_total(acc_):
            stat_open()
            p = stat["pair"]
            for h in range(2):
                stat[("sum", h)] = T(lambda e, h=h: e.matmul(p.half[h], mean1024, acc_[:, h * HALF:(h + 1) * HALF],
                                                             start=True, stop=True), stat[("acc", h)], p.read, consts)
                stat["free"][h] = stat[("sum", h)]

        def stat_all(squares):
            stat_open()
            if squares:
                for d in range(KT):
                    stat_square(d)
                    stat_mean(d)
                return
            p = stat["pair"]
            for h in range(2):
                for d in range(KT):
                    stat[("sum", h)] = T(lambda e, d=d, h=h: e.matmul(
                        p.half[h], mean1024, x[:, d, h * HALF:(h + 1) * HALF], start=(d == 0), stop=(d == KT - 1)),
                        x_ready[d][h], p.read if d == 0 else None)

        def rsqrt_guess(var, epsc, r, after, free=None):
            l1 = A(lambda e: e.activation(r, var, ACT.Ln, bias=epsc), after, eps_set, free)
            return A(lambda e: e.activation(r, r, ACT.Exp, scale=-0.5), l1)

        def rsqrt_newton(var, epsc, r, u, guess, free=None):
            n1 = V(lambda e: e.scalar_tensor_tensor(out=u, in0=r, scalar=-0.5, in1=r, op0=ALU.mult, op1=ALU.mult),
                   guess, free)
            n2 = V(lambda e: e.scalar_tensor_tensor(out=u, in0=var, scalar=epsc, in1=u, op0=ALU.add, op1=ALU.mult), n1)
            return V(lambda e: e.scalar_tensor_tensor(out=r, in0=u, scalar=1.5, in1=r, op0=ALU.add, op1=ALU.mult), n2), n2

        def rsqrt(var, epsc, r, u, after, free=None):
            return rsqrt_newton(var, epsc, r, u, rsqrt_guess(var, epsc, r, after, free), free)

        x_ready = [x_in[k] for k in range(KT)]

        def scale_cols(dst, g, sc, after):
            return V(lambda e: e.scalar_tensor_tensor(out=dst, in0=sc, scalar=1.0, in1=g, op0=ALU.add, op1=ALU.mult), after)

        def halves(p, name, epsc, scope, write):
            r = [sb(f"{name}_r{h}", [P, HALF], F32, scope)[:] for h in range(2)]
            u = sb(f"{name}_u", [P, HALF], F32, scope)[:]
            g = [rsqrt_guess(p.half[h], epsc, r[h], stat[("sum", h)]) for h in range(2)]
            done, p.read = [], []
            for h in range(2):
                rd, pr = rsqrt_newton(p.half[h], epsc, r[h], u, g[h], done)
                p.read.append(pr)
                done = [rd]
                write(h, r[h], rd)
            p.kept = False

        def split_shifted(t, sh, hi, lo, after):
            up = A(lambda e: e.activation(hi, t, ACT.Identity, bias=sh), after)
            return lambda: V(lambda e: e.scalar_tensor_tensor(out=lo, in0=t, scalar=sh, in1=hi.bitcast(F32), op0=ALU.add,
                                                              op1=ALU.subtract), up)

        def modulated(name, h_, g, ish, isc):
            with ExitStack() as scope:
                t = [sb(f"{name}_t{i}", [P, HALF], F32, scope) for i in range(4)]
                ready, free = {}, [None] * 4

                def write(h, r, rd):
                    if h == 0:
                        while (0, ish) not in mod_done or (0, isc) not in mod_done:
                            W.advance()
                            ada_finish()
                        stat["cols"] = scale_cols(cols[:, 0:8], vc(g, 0, 8), mod1[:, isc * 8:isc * 8 + 8],
                                                  [mod_done[(0, isc)], mod_done[(0, ish)]])
                    c = slice(h * HALF, (h + 1) * HALF)
                    low = {}

                    def finish_tile(k):
                        ready[(k, h)] = free[(h * KT + k) % 4] = low[k]()

                    for k in range(KT):
                        i = (h * KT + k) % 4
                        td = V(lambda e, k=k, i=i: e.scalar_tensor_tensor(
                            out=t[i][:], in0=x[:, k, c], scalar=cols[:, k:k + 1], in1=r, op0=ALU.mult, op1=ALU.mult),
                            rd, stat["cols"], free[i])
                        low[k] = split_shifted(t[i][:], mod1[:, ish * 8 + k:ish * 8 + k + 1], h_[0][:, k, c],
                                               h_[1][:, k, c], td)
                        if k >= 2:
                            finish_tile(k - 2)
                    finish_tile(KT - 2)
                    finish_tile(KT - 1)

                halves(stat["pair"], name, eps[:, 0:1], scope, write)
            return [(ready[(k, 0)], ready[(k, 1)]) for k in range(KT)]

        def ffn(n, igt):
            q.stage(f"ffn{n}")
            q.fence()
            if n == 1:
                stat_all(True)
                while (0, igt - 1) not in mod_done:
                    W.advance()
                    ada_finish()
                W.prepare()
            with ExitStack() as hs:
                h = [sb(f"h{n}_hi", [P, KT, S], F32R, hs), sb(f"h{n}_lo", [P, KT, S], F32R, hs)]
                ready = modulated(f"nf{n}", h, f"g_ffn{n}", igt - 2, igt - 1)
                q.fence()
                ah = [sb(f"a{n}_hi{i}", [P, S], F32R, hs) for i in range(A_SLOTS)]
                al = [sb(f"a{n}_lo{i}", [P, S], F32R, hs) for i in range(A_SLOTS)]
                g = sb(f"gate{n}", [P, S], F32, hs)
                a_ready, a_free, g_free, gcols = {}, {}, [None], [None]
                seq, starts = ffn_order()
                for kind, i in seq:
                    if kind == "gu":
                        blk = get(("gu", n, i))
                        hi, lo = (lambda k: h[0][:, k, :]), (lambda k: h[1][:, k, :])
                        both = gemm_pair(blk, hi, lo, ready) if i == 0 else None
                        pg, m1 = both[0] if both else gemm(blk, 0, KT, hi, lo, ready)
                        gd = A(lambda e, pg=pg: e.activation(g[:], pg.full, ACT.Silu), m1, g_free[0])
                        pg.read = [gd]
                        pu, m2 = both[1] if both else gemm(blk, 1, KT, hi, lo, ready)
                        s = i % A_SLOTS
                        ad = V(lambda e, pu=pu: e.tensor_tensor(g[:], g[:], pu.full, ALU.mult), gd, m2)
                        pu.read = [ad]
                        up = A(lambda e, s=s: e.activation(ah[s][:], g[:], ACT.Identity), ad, a_free.get(i - A_SLOTS))
                        dn = V(lambda e, s=s: e.tensor_tensor(al[s][:], g[:], ah[s][:].bitcast(F32), ALU.subtract), up)
                        g_free[0] = dn
                        a_ready[i] = dn
                    else:
                        f0, nf = int(starts[i]), FF_GROUPS[i]
                        for c in range(4):
                            blk = get(("down", n, i, c))
                            if gcols[0] is None:
                                gcols[0] = V(lambda e: e.tensor_scalar(cols[:, 8:16], mod1[:, igt * 8:igt * 8 + 8], 0.5, None,
                                                                       ALU.mult), mod_done[(0, igt)])
                            last = i == len(FF_GROUPS) - 1
                            for m in range(2):
                                d = 2 * c + m
                                p, mm = gemm(blk, m, nf, lambda k: ah[(f0 + k) % A_SLOTS], lambda k: al[(f0 + k) % A_SLOTS],
                                             [a_ready[f0 + k] for k in range(nf)])
                                x_ready[d] = V(lambda e, p=p, d=d: e.scalar_tensor_tensor(
                                    out=x[:, d, :], in0=p.full, scalar=cols[:, 8 + d:9 + d], in1=x[:, d, :],
                                    op0=ALU.mult, op1=ALU.add), mm, gcols[0], x_ready[d])
                                p.read = [x_ready[d]]
                                if last:
                                    stat_add(d, g, free=g_free[0])
                        if last:
                            stat_total(g)
                        for f in range(f0, f0 + nf):
                            a_free[f] = mm

        spilled = {}

        class Store:

            def __init__(self, name, n, scope, dt=F32):
                self.t = [sb(f"{name}{i}", [P, S], dt, scope) for i in range(n)]
                self.s = [q.sem(f"{name}_stored{i}") for i in range(n)]
                self.free = [None] * n
                self.i, self.n = 0, n

            def next(self):
                i = self.i % self.n
                return self.t[i], self.free[i]

            def store(self, dst, key, *after, view=None):
                i = self.i % self.n
                self.i += 1
                for to, of in (view(self.t[i]) if view else [(dst, self.t[i][:])]):
                    self.free[i] = q.dma(self.s[i], to, of, *after)
                spilled.setdefault(key, []).append(self.free[i])

            def all(self):
                return [f for f in self.free if f is not None]

        def split_out(src, his, los, to_hi, to_lo, key, after, view=None):
            th, fh = his.next()
            tl, fl = los.next()
            up = A(lambda e: e.activation(th[:], src, ACT.Identity), after, fh)
            dn = V(lambda e: e.tensor_tensor(tl[:], src, th[:].bitcast(F32), ALU.subtract), up, fl)
            his.store(to_hi, key, dn, view=view and (lambda t: view(t, 0)))
            los.store(to_lo, key, dn, view=view and (lambda t: view(t, 1)))
            return dn

        def rope_heads(his, los, tmp, mats64, rot, cost, sint, gcol, nt, tables, p, mm):
            raw, sq, u, free = tmp
            a1 = A(lambda e: e.activation(sq, p.full, ACT.Square), mm, free)
            a2 = A(lambda e: e.activation(raw, p.full, ACT.Identity), mm, free)
            p.read = [a1, a2]
            yield
            p2 = take()
            for h in range(2):
                m2 = T(lambda e, h=h, p2=p2: e.matmul(p2.half[h], mats64, sq[:, h * HALF:(h + 1) * HALF], start=True,
                                                     stop=True), a1, p2.read, tables)
            rd, pr = rsqrt(p2.full, eps[:, 0:1], sq, u, m2)
            p2.read = [pr]
            qn = V(lambda e: e.scalar_tensor_tensor(out=raw, in0=raw, scalar=gcol, in1=sq, op0=ALU.mult, op1=ALU.mult),
                   rd, a2, tables)
            yield
            p3 = take()
            for h in range(2):
                m3 = T(lambda e, h=h, p3=p3: e.matmul(p3.half[h], rot, raw[:, h * HALF:(h + 1) * HALF], start=True,
                                                     stop=True), qn, p3.read)
            c2 = V(lambda e: e.tensor_tensor(u, p3.full, sint, ALU.mult), m3, rd)
            p3.read = [c2]
            c1 = V(lambda e: e.tensor_tensor(raw, raw, cost, ALU.mult), m3)
            c3 = V(lambda e: e.tensor_tensor(raw, raw, u, ALU.add), c1, c2)
            tmp[3] = split_out(raw, his, los, qk_hi[nt], qk_lo[nt], ("qk", nt), c3)
            yield

        def step(pending):
            for g in list(pending):
                try:
                    next(g)
                except StopIteration:
                    pending.remove(g)

        def attention(name, kv_of, kv_tile, mask, gate_tile, mixh, early, between=None):
            with ExitStack() as sc:
                qs = [sb(f"{name}_q{i}", [P, S], F32R, sc) for i in range(2)]
                kh, kl, vs = [], [], []

                def kv_tiles(i):
                    kh.append(sb(f"{name}_kh{i}", [P, S], F32R, sc))
                    kl.append(sb(f"{name}_kl{i}", [P, S], F32R, sc))
                    vs.append(sb(f"{name}_v{i}", [P, ST, P], F32R, sc))

                kv_tiles(0)
                s_q = [q.sem(f"{name}_qload{i}") for i in range(2)]
                s_k = [q.sem(f"{name}_kload{i}") for i in range(2)]
                s_v = [q.sem(f"{name}_vload{i}") for i in range(2)]
                s_c = q.sem(f"{name}_constload")
                q_free, k_free = [None, None], [None, None]
                qin, kin, vin = {}, {}, {}
                kv_list = []
                for hd in range(A_HEADS):
                    if kv_of(hd) not in kv_list:
                        kv_list.append(kv_of(hd))

                def load_q(hd, early=None):
                    i, r = hd % 2, slice(64 * (hd % 2), 64 * (hd % 2) + 64)
                    got = spilled[("qk", hd // 2)]
                    q.dma(s_q[i], qs[i][0:64, :], qk_hi[hd // 2][r, :], got, q_free[i], early=early)
                    qin[hd] = q.dma(s_q[i], qs[i][64:128, :], qk_lo[hd // 2][r, :], early=early)

                def load_kv(kv, early=None):
                    i, r, t = kv % 2, slice(64 * (kv % 2), 64 * (kv % 2) + 64), kv_tile + kv // 2
                    got = spilled[("qk", t)]
                    for d, src in ((kh, qk_hi), (kl, qk_lo)):
                        for o in (0, 64):
                            kin[kv] = q.dma(s_k[i], d[i][o:o + 64, :], src[t][r, :], got, k_free[i],
                                            early=early)
                    vin[kv] = q.dma(s_v[i], vs[i][:], vsp[kv // 4].rearrange("p (a h) d -> p a h d", h=4)[:, :, kv % 4, :],
                                    spilled[("v", kv)], k_free[i], early=early)

                def load_first():
                    load_q(0, early)
                    load_kv(kv_list[0], early)
                    load_q(1, early)

                if between is not None:
                    between(load_first)
                else:
                    load_first()
                q.stage(name)
                kv_tiles(1)
                nu = [sb(f"{name}_num{i}", [P, S], F32, sc) for i in range(2)]
                th = [sb(f"{name}_th{i}", [P, ST, 256], F32R, sc) for i in range(2)]
                tl = [sb(f"{name}_tl{i}", [P, ST, 256], F32R, sc) for i in range(2)]
                sm = [sb(f"{name}_sm{i}", [P, 4], F32, sc) for i in range(2)]
                dg = [sqh[1][:, (i + 1) * P:(i + 2) * P] for i in range(3)]
                og = sb(f"{name}_o", [P, S], F32, sc)
                onest = sqh[1][:, 0:P]
                tm = [sqh[0][0:64, i * 256:(i + 1) * 256] for i in range(2)]
                if mask is not None:
                    maskt = sb(f"{name}_mask", [P, 1920], F32, sc)
                    q.dma(s_c, maskt[:], mask)
                else:
                    gt = [sb(f"{name}_g{i}", [P, S], F32, sc) for i in range(1)]
                    s_g = q.sem(f"{name}_gload")
                    g_free = None
                c_in = q.dma(s_c, onest, ins["mats"][MAT["ones"]])
                if len(kv_list) > 1:
                    load_kv(kv_list[1])
                ps_s, ps_t, ps_o = [take(), take()], take(), take()
                ps_o_read = [list(ps_o.read), list(ps_o.read)]
                nu_free, t_free, tm_free, og_free = [None, None], [None, None], [None, None], None
                n = A_HEADS * ST
                soft, parts, o_done, sdone, maxed, turned, dgd, vdone = {}, {}, {}, {}, {}, {}, {}, {}
                dg_free, ps_t_read = [None] * 3, [list(ps_t.read), list(ps_t.read)]

                def unit(u):
                    return u // ST, u % ST

                def score_products(u):
                    hd, i = unit(u)
                    kv = kv_of(hd)
                    b, c = hd % 2, kv % 2
                    p = ps_s[u % 2]
                    for h in range(2):
                        for a, k_ in enumerate((kh, kl)):
                            mm = T(lambda e, h=h, a=a, k_=k_: e.matmul(
                                p.half[h], qs[b][:, i * P:(i + 1) * P], k_[c][:, h * HALF:(h + 1) * HALF],
                                start=(a == 0), stop=(a == 1)), qin[hd], kin[kv], p.read)
                    if i == ST - 1:
                        q_free[b] = mm
                        if hd + 2 < A_HEADS:
                            load_q(hd + 2)
                    sdone[u] = mm

                def maximum(u):
                    p, s, m, mm, i = ps_s[u % 2], nu[u % 2], sm[u % 2], sdone[u], u % ST
                    if mask is not None:
                        o = 896 - P * i
                        mx = V(lambda e: e.tensor_tensor_reduce(
                            out=s[:], in0=p.full, in1=maskt[:, o:o + S], scale=1.0, scalar=-3e38, op0=ALU.add,
                            op1=ALU.max, accum_out=m[:, 0:1]), mm, c_in, nu_free[u % 2])
                        p.read = [mx]
                        mx = V(lambda e: e.tensor_scalar(m[:, 1:2], m[:, 0:1], -1.0, None, ALU.mult), mx)
                        src = s[:]
                    else:
                        mx = V(lambda e: e.tensor_reduce(m[:, 1:2], p.full, AX.X, ALU.max, negate=True), mm,
                               nu_free[u % 2])
                        src = p.full
                    maxed[u] = (mx, src)

                def numerators(u):
                    p, s, m, (mx, src) = ps_s[u % 2], nu[u % 2], sm[u % 2], maxed[u]
                    ex = A(lambda e: e.activation(s[:], src, ACT.Exp, bias=m[:, 1:2], accum_out=m[:, 2:3]), mx,
                           nu_free[u % 2])
                    if mask is None:
                        p.read = [ex]
                    soft[u] = ex

                def reciprocal_sum(u):
                    m = sm[u % 2]
                    rc = V(lambda e: e.reciprocal(m[:, 3:4], m[:, 2:3]), soft[u])
                    dgd[u] = A(lambda e: e.activation(dg[u % 3], ident, ACT.Copy, scale=m[:, 3:4]), rc, dg_free[u % 3])

                def turn_over(u):
                    s, w = nu[u % 2], u // 2
                    c = slice((u % 2) * P, (u % 2) * P + P)
                    fr = t_free[w % 2] if u % 2 == 0 else None
                    for h in range(2):
                        for j in range(4):
                            mm = T(lambda e, h=h, j=j: e.transpose(
                                ps_t.half[h][:, j * P:(j + 1) * P], s[:, (4 * h + j) * P:(4 * h + j + 1) * P], ident),
                                soft[u], ps_t_read[h])
                        t3 = ps_t.half[h].rearrange("p (j q) -> p j q", j=4)
                        hi, lo = th[w % 2][:, 4 * h:4 * h + 4, c], tl[w % 2][:, 4 * h:4 * h + 4, c]
                        up = A(lambda e, t3=t3, hi=hi: e.activation(hi, t3, ACT.Identity), mm, fr)
                        turned[(u, h)] = (up, t3, hi, lo, fr)
                    nu_free[u % 2] = mm

                def low_parts(u):
                    for h in range(2):
                        up, t3, hi, lo, fr = turned[(u, h)]
                        dn = V(lambda e, t3=t3, hi=hi, lo=lo: e.tensor_tensor(lo, t3, hi.bitcast(F32), ALU.subtract), up, fr)
                        ps_t_read[h] = [dn]
                    parts[u] = dn

                def spread_sum(u):
                    bank = ps_o.half[(u // 2) % 2]
                    dg_free[u % 3] = T(lambda e: e.matmul(
                        bank[:, 256 + (u % 2) * P:256 + (u % 2 + 1) * P], onest, dg[u % 3], start=True, stop=True),
                        dgd[u], c_in, ps_o_read[(u // 2) % 2])

                def times_v(w, part):
                    nonlocal g_in
                    hd, i = unit(2 * w)
                    kv, pp, hh = kv_of(hd), hd // 2, hd % 2
                    if gate_tile is not None and hh == 0 and i == 0 and part == 0:
                        g_in = q.dma(s_g, gt[0][:], proj[gate_tile + pp], spilled[("proj", gate_tile + pp)], og_free)
                    bank = ps_o.half[w % 2]
                    for j in range(ST):
                        mm = T(lambda e, j=j: e.matmul(
                            bank[:, 0:256], vs[kv % 2][:, j, :], (th, tl)[part][w % 2][:, j, :],
                            start=(part == 0 and j == 0), stop=(part == 1 and j == ST - 1)), parts[2 * w + 1], vin[kv])
                    if part == 0:
                        return
                    t_free[w % 2] = mm
                    vdone[w] = mm
                    if i + 2 >= ST and (hd + 1 == A_HEADS or kv_of(hd + 1) != kv):
                        k_free[kv % 2] = mm
                        at = kv_list.index(kv)
                        if at + 2 < len(kv_list):
                            load_kv(kv_list[at + 2])

                def results(w):
                    nonlocal og_free
                    hd, i = unit(2 * w)
                    pp, hh = hd // 2, hd % 2
                    bank = ps_o.half[w % 2]
                    t = tm[w % 2]
                    a1 = A(lambda e: e.activation(t, bank[64:128, 0:256], ACT.Identity), vdone[w], tm_free[w % 2])
                    v1 = V(lambda e: e.tensor_tensor(t, bank[0:64, 0:256], t, ALU.add), a1)
                    o = og[64 * hh:64 * hh + 64, i * P:(i + 2) * P]
                    v2 = V(lambda e: e.tensor_tensor(o, t, bank[0:64, 256:512], ALU.mult), v1,
                           og_free if hh == 0 and i == 0 else None)
                    tm_free[w % 2] = v2
                    ps_o_read[w % 2] = [v2]
                    if hh == 1 and i + 2 >= ST:
                        if gate_tile is not None:
                            v2 = V(lambda e: e.tensor_tensor(og[:], og[:], gt[0][:], ALU.mult), v2, g_in)
                        up = A(lambda e: e.activation(mixh[0][:, pp, :], og[:], ACT.Identity), v2)
                        og_free = V(lambda e: e.tensor_tensor(mixh[1][:, pp, :], og[:], mixh[0][:, pp, :].bitcast(F32),
                                                              ALU.subtract), up)
                        o_done[pp] = og_free

                g_in = None
                for u in range(n + 4):
                    if u < n:
                        score_products(u)
                        maximum(u)
                    if u >= 5 and u % 2 == 1:
                        results((u - 5) // 2)
                    if 1 <= u <= n:
                        turn_over(u - 1)
                    if u < n:
                        numerators(u)
                    if 1 <= u <= n:
                        low_parts(u - 1)
                        reciprocal_sum(u - 1)
                    if u >= 3 and u % 2 == 1 and u < n + 3:
                        spread_sum(u - 3)
                        spread_sum(u - 2)
                        times_v((u - 3) // 2, 0)
                    if u >= 4 and u % 2 == 0:
                        times_v((u - 4) // 2, 1)
                ps_o.read = ps_o_read[0] + ps_o_read[1]
                ps_t.read = ps_t_read[0] + ps_t_read[1]
                return [o_done[pp] for pp in range(4)], sdone[n - 1]

        def load_mix(name, scope, first, qk_read):
            t = [sb(f"{name}_t{i}", [P, S], F32, scope) for i in range(3)]
            sm = [q.sem(f"{name}_load{i}") for i in range(3)]

            def load(k, early, free=None):
                return q.dma(sm[k % 3], t[k % 3][:], mixd[first + k], spilled[("mix", first + k)], free, early=early)

            loads = [load(k, [qk_read]) for k in range(3)]

            def split(h):
                ready = []
                for k in range(4):
                    up = A(lambda e, k=k: e.activation(h[0][:, k, :], t[k % 3][:], ACT.Identity), loads[k])
                    dn = V(lambda e, k=k: e.tensor_tensor(h[1][:, k, :], t[k % 3][:], h[0][:, k, :].bitcast(F32),
                                                          ALU.subtract), up)
                    ready.append(dn)
                    if k == 0:
                        loads.append(load(3, None, dn))
                return ready
            return split

        def mixer1():
            q.stage("proj1")
            q.fence()
            with ExitStack() as hs:
                h = [sb("hm_hi", [P, KT, S], F32R, hs), sb("hm_lo", [P, KT, S], F32R, hs)]
                ready = modulated("nm", h, "g_mix", 3, 4)
                q.fence()
                hi, lo = (lambda k: h[0][:, k, :]), (lambda k: h[1][:, k, :])
                with ExitStack() as sc:
                    cst = sb("rope_cos", [P, S], F32, sc)
                    snt = sb("rope_sin", [P, S], F32, sc)
                    m2 = sb("rope_mats", [P, 2 * P], F32, sc)
                    s_t = q.sem("rope1_loaded")
                    t1 = q.dma(s_t, cst[:], ins["rope1"][0])
                    t2 = q.dma(s_t, snt[:], ins["rope1"][1])
                    t2 = q.dma(s_t, m2[:, 0:P], ins["mats"][MAT["mean64"]])
                    tables = q.dma(s_t, m2[:, P:2 * P], ins["mats"][MAT["rot1"]])
                    gq = V(lambda e: e.tensor_scalar(cols[:, 16:17], vc("g_q"), A_DIM ** -0.5, None, ALU.mult))
                    his, los = Store("p1_hi", 2, sc, F32R), Store("p1_lo", 2, sc, F32R)
                    tmps = []
                    for i in range(2):
                        tmps.append([sb(f"p1_{n}{i}", [P, S], F32, sc)[:] for n in ("raw", "sq", "u")] + [None])
                    pending = []
                    nt = 0
                    for b in range(4):
                        blk = get(("in1", b))
                        both = gemm_pair(blk, hi, lo, ready) if b == 0 else None
                        for m in range(2):
                            p, mm = both[m] if both else gemm(blk, m, KT, hi, lo, ready)
                            step(pending)
                            gc = cols[:, 16:17] if b < 2 else vc("g_k")
                            pending.append(rope_heads(his, los, tmps[nt % 2], m2[:, 0:P], m2[:, P:2 * P], cst[:], snt[:],
                                                      gc, nt, [tables, gq], p, mm))
                            next(pending[-1])
                            nt += 1
                    for b in (4, 5):
                        blk = get(("in1", b))
                        for m in range(2):
                            p, mm = gemm_rows(blk, hi, lo, 4 * m, ready)
                            step(pending)

                            def view(t, part, b=b, m=m):
                                return [(vsp[b % 2][:, 16 * m:16 * m + 16, 64 * part:64 * part + 64],
                                         t[:].rearrange("p (r d) -> p r d", d=64))]
                            p.read = [split_out(p.full, his, los, None, None, ("vrows", b % 2), mm, view=view)]
                    for hd in range(A_HEADS):
                        spilled[("v", hd)] = spilled[("vrows", hd // 4)]
                    done = his.all() + los.all()
                q.fence(done)
                with ExitStack() as sc:
                    st = Store("p1b_o", 3, sc)
                    rows = []
                    for b in PROJ_ORDER[6:]:
                        blk = get(("in1", b))
                        for m in range(2 if b < 12 else 1):
                            if b < 8:
                                p, mm = gemm_rows(blk, hi, lo, 4 * m, ready)
                            else:
                                p, mm = gemm(blk, m, KT, hi, lo, ready, 256 if b < 12 else P)
                            step(rows)
                            t, fr = st.next()
                            fn = ACT.Sigmoid if b in (10, 11) else ACT.Identity
                            scale = M_QK ** -0.5 if b == 9 else 1.0
                            bias = vc("gate_bias") if b == 12 else 0.0
                            d = A(lambda e, p=p, t=t, fn=fn, scale=scale, bias=bias: e.activation(
                                t[:], p.full, fn, scale=scale, bias=bias), mm, fr)
                            p.read = [d]
                            if b < 8:
                                st.store(None, ("mvs", b % 2), d, view=lambda t, m=m, b=b: [
                                    (mvs[:, 4 * m:4 * m + 4, (b % 2) * 256:(b % 2 + 1) * 256],
                                     t[:].rearrange("p (a b) -> p a b", a=4))])
                                continue
                            n = 8 + 2 * (b - 8) + m
                            st.store(proj[n], ("proj", n), d)
                            if b == 12:
                                rows.append(mlstm_rows(sc, st))
                    while rows:
                        step(rows)
                    done = st.all() + rows_out
            h_read = [q.last["tensor"]]
            q.fence(done)
            done, early = mlstm(h_read)
            q.fence(done)
            with ExitStack() as ma:
                mixa = [sb("mix1a_hi", [P, 4, S], F32R, ma), sb("mix1a_lo", [P, 4, S], F32R, ma)]
                ra, qk_read = attention("attn1", lambda h: h, 4, ins["band"], None, mixa, early)
                q.stage("out1")
                mixt = load_mix("mix1", ma, 0, qk_read)
                q.fence()
                mixb = [sb("mix1b_hi", [P, 4, S], F32R, ma), sb("mix1b_lo", [P, 4, S], F32R, ma)]
                rb = mixt(mixb)
                ssum = sb("mix1_squares", [P, S], F32, ma)
                for c in range(4):
                    blk = get(("out1", c))
                    for m in range(2):
                        d = 2 * c + m
                        p, mm = gemm(blk, m, KT, lambda k: (mixb if k < 4 else mixa)[0][:, k % 4, :],
                                     lambda k: (mixb if k < 4 else mixa)[1][:, k % 4, :], rb + ra,
                                     order=[4, 5, 6, 0, 1, 2, 3, 7])
                        x_ready[d] = V(lambda e, p=p, d=d: e.scalar_tensor_tensor(
                            out=x[:, d, :], in0=p.full, scalar=mod1[:, 5 * 8 + d:5 * 8 + d + 1], in1=x[:, d, :],
                            op0=ALU.mult, op1=ALU.add), mm, x_ready[d], mod_done[(0, 5)])
                        p.read = [x_ready[d]]
                        stat_add(d, ssum)
                stat_total(ssum)

        def mlstm_rows(sc, st):
            R = 36
            li = sb("ml_li", [R, S], F32, sc)
            lf = sb("ml_lf", [R, S], F32, sc)
            t1 = sb("ml_t1", [R, S], F32, sc)
            b = sb("ml_b", [R, S], F32, sc)
            M = sb("ml_M", [R, S], F32, sc)
            nm = sb("ml_nm_rows", [R, S], F32, sc)
            mrow = sb("ml_m", [R, 16], F32, sc)
            dec = sb("ml_dec", [R, ST], F32, sc)
            dex = sb("ml_decx", [R, R, ST], F32, sc)
            QA = sb("ml_QA", [P, S], F32, sc)
            QB = sb("ml_QB", [P, S], F32, sc)
            s_g = q.sem("ml_gates_loaded")
            gate = proj[16]
            q.dma(s_g, li[0:32, :], gate[0:32, :], spilled[("proj", 16)])
            q.dma(s_g, t1[32:36, :], gate[32:36, :])
            q.dma(s_g, lf[0:32, :], gate[64:96, :])
            q.dma(s_g, b[32:36, :], gate[96:100, :])
            g_in = q.dma(s_g, nm[:], ins["reset"])
            V(lambda e: e.memset(QA[:], 0.0))
            q0 = V(lambda e: e.memset(QB[:], 0.0))
            yield
            r1 = V(lambda e: e.tensor_copy(li[32:36, :], t1[32:36, ::-1]), g_in)
            r2 = V(lambda e: e.tensor_copy(lf[32:36, :], b[32:36, ::-1]), g_in)
            a1 = A(lambda e: e.activation(t1[:], lf[:], ACT.Abs), r2, r1)
            a2 = A(lambda e: e.activation(t1[:], t1[:], ACT.Exp, scale=-1.0), a1)
            a3 = A(lambda e: e.activation(t1[:], t1[:], ACT.Ln, bias=one[0:R, 0:1]), a2, one_set)
            yield
            f1 = V(lambda e: e.scalar_tensor_tensor(out=lf[:], in0=lf[:], scalar=0.0, in1=t1[:], op0=ALU.min,
                                                    op1=ALU.subtract), a3)
            b1 = V(lambda e: e.tensor_tensor_scan(b[:], nm[:], lf[:], 0.0, ALU.mult, ALU.add), f1, r2)
            s1 = V(lambda e: e.tensor_tensor(li[:], li[:], b[:], ALU.subtract), b1)
            m0 = V(lambda e: e.memset(mrow[:, 0:1], NEG))
            yield
            prev = [s1, m0]
            for c in range(ST):
                sl = slice(c * P, (c + 1) * P)
                sc1 = V(lambda e, sl=sl, c=c: e.tensor_tensor_scan(M[:, sl], li[:, sl], li[:, sl],
                                                                 mrow[:, c:c + 1], ALU.max, ALU.max), prev)
                prev = [V(lambda e, c=c: e.tensor_tensor(mrow[:, c + 1:c + 2], b[:, c * P + P - 1:c * P + P],
                                                         M[:, c * P + P - 1:c * P + P], ALU.add), sc1)]
            yield
            a3d = li[:].rearrange("p (c t) -> p c t", c=ST)
            M3 = M[:].rearrange("p (c t) -> p c t", c=ST)
            T1 = t1[:].rearrange("p (c t) -> p c t", c=ST)
            LF3 = lf[:].rearrange("p (c t) -> p c t", c=ST)
            mp = mrow[:, 0:ST].unsqueeze(2).to_broadcast([R, ST, P])
            me = M3[:, :, P - 1:P].to_broadcast([R, ST, P])
            w1 = V(lambda e: e.tensor_tensor(T1, mp, M3, ALU.subtract), prev)
            w2 = V(lambda e: e.tensor_tensor(LF3, a3d, me, ALU.subtract), prev)
            w3 = V(lambda e: e.tensor_tensor(b[:], b[:], M[:], ALU.add), prev)
            w4 = V(lambda e: e.tensor_scalar(b[:], b[:], -1.0, EXP_CAP, ALU.mult, ALU.min), w3)
            w5 = V(lambda e: e.tensor_tensor(dec[:].unsqueeze(2), mrow[:, 0:ST].unsqueeze(2), M3[:, :, P - 1:P],
                                             ALU.subtract), prev)
            yield
            e5 = A(lambda e: e.activation(dec[:], dec[:], ACT.Exp), w5)
            outs = []
            for r0, r1_, rv in ((0, 32, 1), (32, 36, -1)):
                s_ = slice(r0, r1_)
                o_ = slice(64 + r0, 64 + r1_)

                def dirn(t, rows, rv=rv):
                    return t[rows, :] if rv == 1 else t[rows, ::-1]
                outs.append(A(lambda e, s_=s_, o_=o_, d=dirn: e.activation(d(QA, o_), t1[s_, :], ACT.Exp), w1, q0))
                outs.append(A(lambda e, s_=s_, o_=o_, d=dirn: e.activation(d(QB, o_), lf[s_, :], ACT.Exp), w2, q0))
                outs.append(A(lambda e, s_=s_, d=dirn: e.activation(d(QB, s_), b[s_, :], ACT.Exp), w4, q0))
                outs.append(V(lambda e, s_=s_, d=dirn: e.tensor_copy(d(QA, s_), li[s_, :]), q0, prev))
                nmd = V(lambda e, s_=s_, d=dirn: e.tensor_scalar(d(nm, s_), M[s_, :], -1.0, None, ALU.mult), prev)
                outs.append(nmd)
            s_r = q.sem("ml_rows_stored")
            rows_out.append(q.dma(s_r, ml_nm[:, :], nm[:], nmd))
            dx = V(lambda e: e.tensor_tensor(dex[:], ident[0:R, 0:R].unsqueeze(2).to_broadcast([R, R, ST]),
                                             dec[:].unsqueeze(1).to_broadcast([R, R, ST]), ALU.mult), e5)
            rows_out.append(q.dma(s_r, ml_dex[:, :], dex[:].rearrange("p a b -> p (a b)"), dx, rows_out[-1]))
            yield
            for n, src in enumerate((QA, QB)):
                p = take()
                for c in range(ST):
                    mm = T(lambda e, c=c, p=p, src=src: e.transpose(p.full[:, c * P:(c + 1) * P],
                                                                  src[:, c * P:(c + 1) * P], ident), outs, p.read)
                t, fr = st.next()
                d = A(lambda e, p=p, t=t: e.activation(t[:], p.full, ACT.Identity), mm, fr)
                p.read = [d]
                st.store(ml_cols[n], ("ml_cols", n), d)
                yield

        def mlstm(h_read):
            q.stage("mlstm")
            R = 36
            with ExitStack() as sc:
                colsA = sb("ml_colsA", [P, ST, P], F32, sc)
                colsB = sb("ml_colsB", [P, ST, P], F32, sc)
                nm = sb("ml_negM", [R, S], F32, sc)
                dex = sb("ml_decay_rows", [R, R * ST], F32, sc)
                decB = sb("ml_decay", [P, 2, 2, ST], F32, sc)
                sel = sb("ml_sel", [R, 8 * P], F32, sc)
                mats3 = sb("ml_mats", [P, 3 * P], F32, sc)
                qk = [sb(f"ml_{n}{i}", [P, S], F32, sc) for n in "qk" for i in range(2)]
                v1 = [sb(f"ml_v{i}", [P, 4, M_HEADS, M_V + 1], F32, sc) for i in range(2)]
                ktok = sb("ml_ktok", [P, ST, 256], F32, sc)
                E = [[sb(f"ml_E{i}{d}", [P, ST, P], F32, sc) for d in range(2)] for i in range(2)]
                kw = [sb(f"ml_kw{i}", [P, ST, M_QK], F32, sc) for i in range(2)]
                C = sb("ml_C", [P, 2, ST, M_V + 1], F32, sc)
                hs = [sb(f"ml_hs{i}", [P, ST, M_V], F32, sc) for i in range(2)]
                num = [sb(f"ml_num{i}", [P, 4, M_V + 1], F32, sc) for i in range(2)]
                dn = [sb(f"ml_den{i}", [P, 12], F32, sc) for i in range(2)]
                ss = sb("ml_ss", [P, 3, ST], F32, sc)
                mo = [sb(f"ml_mo{i}", [P, S], F32, sc) for i in range(2)]
                ones, causal, anti = mats3[:, 0:P], mats3[:, P:2 * P], mats3[:, 2 * P:3 * P]
                s_t, s_ca, s_cb = q.sem("ml_consts"), q.sem("ml_colsA_loaded"), q.sem("ml_colsB_loaded")
                s_qk = [q.sem(f"ml_qk{i}_loaded") for i in range(4)]
                s_v = [q.sem(f"ml_v{i}_loaded") for i in range(2)]
                s_mo = [q.sem(f"ml_mo_loaded{i}") for i in range(2)]
                q.first(s_t, sel[:], ins["sel"], early=h_read)
                q.first(s_t, nm[:], ml_nm[:, :], rows_out, early=h_read)
                qk_in = [None] * 4
                qk_in[0] = q.first(s_qk[0], qk[0][:], proj[8], spilled[("proj", 8)], early=h_read)
                ca_in = q.first(s_ca, colsA[:].rearrange("p a b -> p (a b)"), ml_cols[0], spilled[("ml_cols", 0)], early=h_read)
                qk_in[2] = q.first(s_qk[2], qk[2][:], proj[10], spilled[("proj", 10)], early=h_read)
                q.first(s_t, dex[:], ml_dex[:, :], early=h_read)
                for j, n in enumerate(("ones", "causal", "anti")):
                    tabs = q.first(s_t, mats3[:, j * P:(j + 1) * P], ins["mats"][MAT[n]], early=h_read)
                cb_in = q.first(s_cb, colsB[:].rearrange("p a b -> p (a b)"), ml_cols[1], spilled[("ml_cols", 1)], early=h_read)
                v_in = [None] * 2
                for g in range(2):
                    v_in[g] = q.first(s_v[g], v1[g][:].rearrange("p c h v -> p (c h) v")[:, :, 0:M_V],
                                    mvs[:, 4 * g:4 * g + 4, :].rearrange("p c (h v) -> p (c h) v", h=M_HEADS),
                                    spilled[("mvs", 0)], spilled[("mvs", 1)], early=h_read)
                for i in (1, 3):
                    qk_in[i] = q.first(s_qk[i], qk[i][:], proj[8 + i], spilled[("proj", 8 + i)], early=h_read)
                v_one = [V(lambda e, g=g: e.memset(v1[g][:, :, :, M_V:M_V + 1], 1.0)) for g in range(2)]
                zC = V(lambda e: e.memset(C[:, :, 0, :], 0.0))
                kt_done, dd = {}, []
                st = Store("ml_o", 2, sc)
                e_free = [[None, None], [None, None]]
                kw_free, c_free, mo_free, num_free, hs_free = [None] * 2, [None] * 2, [None] * 2, [None] * 2, [None] * 2
                mo_in, st_, cd, hs_done = {}, {}, {}, {}

                def prepare(h):
                    i, pr_, lo = h % 2, h // 2, 64 * (h % 2)
                    part = slice(lo, lo + 64)
                    qt, kt = qk[pr_], qk[2 + pr_]
                    if h % 2 == 0:
                        p = take()
                        for c in range(ST):
                            mm = T(lambda e, c=c, p=p: e.transpose(p.full[:, c * P:(c + 1) * P], kt[:, c * P:(c + 1) * P],
                                                                  ident), qk_in[2 + pr_], p.read)
                        d = A(lambda e, p=p: e.activation(ktok[:, :, pr_ * P:(pr_ + 1) * P],
                                                          p.full.rearrange("p (c k) -> p c k", c=ST), ACT.Identity), mm)
                        p.read = [d]
                        kt_done[pr_] = d
                        yield
                    ed = []
                    for dr in range(2):
                        row = 32 * dr + h
                        p = take()
                        hd = dr * 4 + h
                        for hf in range(2):
                            mm = T(lambda e, p=p, hf=hf, hd=hd: e.matmul(p.half[hf], sel[:, hd * P:(hd + 1) * P],
                                                                       nm[:, hf * HALF:(hf + 1) * HALF], start=True,
                                                                       stop=True), p.read, tabs)
                        Et = E[i][dr]
                        x1 = V(lambda e, p=p, Et=Et, row=row: e.tensor_tensor(
                            Et[:], p.full.rearrange("p (c t) -> p c t", c=ST),
                            colsA[:, :, row:row + 1].to_broadcast([P, ST, P]), ALU.add), mm, ca_in, e_free[i][dr])
                        p.read = [x1]
                        mk = causal if dr == 0 else anti
                        x2 = V(lambda e, Et=Et, mk=mk: e.tensor_tensor(
                            Et[:], Et[:], mk.unsqueeze(1).to_broadcast([P, ST, P]), ALU.add), x1, tabs)
                        ed.append(A(lambda e, Et=Et: e.activation(Et[:], Et[:], ACT.Exp), x2))
                        yield
                    if not dd:
                        p = take()
                        mm = T(lambda e, p=p: e.matmul(p.full[:, 0:R * ST], ones[0:R, :], dex[:], start=True, stop=True),
                               tabs, p.read)
                        for hh in range(M_HEADS):
                            for dr in range(2):
                                row = 32 * dr + hh
                                hp = slice(64 * (hh % 2), 64 * (hh % 2) + 64)
                                dd.append(V(lambda e, hh=hh, dr=dr, row=row, hp=hp, p=p: e.tensor_copy(
                                    decB[hp, hh // 2, dr, :], p.full[hp, row * ST:(row + 1) * ST]), mm))
                        p.read = [dd[-1]]
                    kds = []
                    for dr in range(2):
                        row = 32 * dr + h
                        kds.append(V(lambda e, dr=dr, row=row: e.tensor_tensor(
                            kw[dr][:], ktok[:, :, h * 64:(h + 1) * 64],
                            colsB[:, :, 64 + row:64 + row + 1].to_broadcast([P, ST, M_QK]), ALU.mult),
                            kt_done[pr_], kw_free[dr], cb_in))
                    last = [zC, zC]
                    for j0 in (0, 4):
                        for dr in range(2):
                            p = take()
                            for j in range(j0, min(j0 + 4, ST - 1)):
                                c = j if dr == 0 else ST - 1 - j
                                mm = T(lambda e, p=p, j=j, c=c, dr=dr: e.matmul(
                                    p.full[part, (j % 4) * 256:(j % 4) * 256 + M_V + 1], kw[dr][:, c, :],
                                    v1[c // 4][:, c % 4, h, :], start=True, stop=True),
                                    kds[dr], v_in, v_one, p.read)
                            kw_free[dr] = mm
                            for j in range(j0, min(j0 + 4, ST - 1)):
                                last[dr] = V(lambda e, p=p, j=j, dr=dr: e.scalar_tensor_tensor(
                                    out=C[part, dr, j + 1, :], in0=C[part, dr, j, :],
                                    scalar=decB[part, pr_, dr, j:j + 1],
                                    in1=p.full[part, (j % 4) * 256:(j % 4) * 256 + M_V + 1],
                                    op0=ALU.mult, op1=ALU.add), mm, last[dr], c_free[i], dd)
                            p.read = [last[dr]]
                            yield
                    cd[h] = last
                    p = take()
                    for c in range(ST):
                        mm = T(lambda e, p=p, c=c: e.matmul(p.full[:, c * P:(c + 1) * P], kt[part, c * P:(c + 1) * P],
                                                            qt[part, c * P:(c + 1) * P], start=True, stop=True),
                               p.read, qk_in[pr_], qk_in[2 + pr_])
                    st_[h] = []
                    for dr in range(2):
                        Et = E[i][dr]
                        st_[h].append(V(lambda e, p=p, Et=Et: e.tensor_tensor(
                            Et[:], Et[:], p.full.rearrange("p (c t) -> p c t", c=ST), ALU.mult), ed[dr], mm))
                    p.read = [st_[h][1]]
                    yield

                def outputs(h):
                    i, pr_, lo = h % 2, h // 2, 64 * (h % 2)
                    part = slice(lo, lo + 64)
                    qt, n = qk[pr_], 0
                    for dr in range(2):
                        row = 32 * dr + h
                        for c0 in (0, 4):
                            pl = take()
                            for c in range(c0, c0 + 4):
                                ml = T(lambda e, pl=pl, c=c, dr=dr: e.matmul(
                                    pl.full[:, (c % 4) * 256:(c % 4) * 256 + M_V + 1], E[i][dr][:, c, :],
                                    v1[c // 4][:, c % 4, h, :], start=True, stop=True), st_[h][dr], pl.read)
                            pi = take()
                            for c in range(c0, c0 + 4):
                                j = c if dr == 0 else ST - 1 - c
                                mi = T(lambda e, pi=pi, c=c, dr=dr, j=j: e.matmul(
                                    pi.full[:, (c % 4) * 256:(c % 4) * 256 + M_V + 1], qt[part, c * P:(c + 1) * P],
                                    C[part, dr, j, :], start=True, stop=True), cd[h][dr], pi.read)
                            pi3 = pi.full.rearrange("p (c v) -> p c v", c=4)[:, :, 0:M_V + 1]
                            pl3 = pl.full.rearrange("p (c v) -> p c v", c=4)[:, :, 0:M_V + 1]
                            nu, de = num[n % 2], dn[n % 2]
                            n1 = V(lambda e, pi3=pi3, c0=c0, row=row, nu=nu: e.tensor_tensor(
                                nu[:], pi3, colsA[:, c0:c0 + 4, 64 + row:64 + row + 1].to_broadcast([P, 4, M_V + 1]),
                                ALU.mult), mi, num_free[n % 2])
                            pi.read = [n1]
                            n2 = V(lambda e, pl3=pl3, nu=nu: e.tensor_tensor(nu[:], nu[:], pl3, ALU.add), n1, ml)
                            pl.read = [n2]
                            n3 = A(lambda e, nu=nu, de=de: e.activation(de[:, 0:4].unsqueeze(2), nu[:, :, M_V:M_V + 1],
                                                                        ACT.Abs), n2)
                            if dr == 1 and c0 == 4:
                                c_free[i] = mi
                            e_free[i][dr] = ml
                            yield
                            n4 = V(lambda e, c0=c0, row=row, de=de: e.tensor_tensor(
                                de[:, 4:8].unsqueeze(2), de[:, 0:4].unsqueeze(2), colsB[:, c0:c0 + 4, row:row + 1],
                                ALU.max), n3)
                            n5 = V(lambda e, de=de: e.reciprocal(de[:, 8:12], de[:, 4:8]), n4)
                            rb = de[:, 8:12].unsqueeze(2).to_broadcast([P, 4, M_V])
                            dst = hs[i][:, c0:c0 + 4, :]
                            if dr == 0:
                                n6 = V(lambda e, dst=dst, rb=rb, nu=nu: e.tensor_tensor(dst, nu[:, :, 0:M_V], rb, ALU.mult),
                                       n5, hs_free[i])
                            else:
                                n5 = V(lambda e, rb=rb, nu=nu: e.tensor_tensor(nu[:, :, 0:M_V], nu[:, :, 0:M_V], rb,
                                                                               ALU.mult), n5)
                                n6 = V(lambda e, dst=dst, nu=nu: e.tensor_tensor(dst, dst, nu[:, :, 0:M_V], ALU.add), n5)
                            num_free[n % 2] = n6
                            n += 1
                    hs_done[h] = n6

                def norm(h):
                    i = h % 2
                    mo_in[h] = q.dma(s_mo[i], mo[i][:], proj[12 + h], spilled[("proj", 12 + h)], mo_free[i])
                    for f in range(2):
                        s1 = A(lambda e, f=f: e.activation(sqh[f][:].rearrange("p (c v) -> p c v", c=4),
                                                           hs[i][:, 4 * f:4 * f + 4, :], ACT.Square), hs_done[h], sq_free[f])
                        sq_free[f] = V(lambda e, f=f: e.tensor_reduce(
                            ss[:, 0, 4 * f:4 * f + 4], sqh[f][:].rearrange("p (c v) -> p c v", c=4), AX.X, ALU.add), s1)
                    s3 = V(lambda e: e.tensor_scalar(ss[:, 0, :], ss[:, 0, :], 1.0 / M_V, None, ALU.mult), sq_free)
                    guess = rsqrt_guess(ss[:, 0, :], eps[:, 0:1], ss[:, 1, :], s3)
                    yield
                    rd, _ = rsqrt_newton(ss[:, 0, :], eps[:, 0:1], ss[:, 1, :], ss[:, 2, :], guess)
                    hn = V(lambda e: e.tensor_tensor(hs[i][:], hs[i][:], ss[:, 1, :].unsqueeze(2).to_broadcast([P, ST, M_V]),
                                                     ALU.mult), rd)
                    p = take()
                    p.kept = True
                    for c in range(ST):
                        mm = T(lambda e, p=p, c=c: e.transpose(p.full[:, c * P:(c + 1) * P], hs[i][:, c, :], ident),
                               hn, p.read)
                    hs_free[i] = mm
                    yield
                    t, fr = st.next()
                    d = V(lambda e, p=p, t=t: e.scalar_tensor_tensor(out=t[:], in0=p.full, scalar=vc("g_mh", h),
                                                                   in1=mo[i][:], op0=ALU.mult, op1=ALU.mult),
                          mm, mo_in[h], fr)
                    p.read = [d]
                    p.kept = False
                    mo_free[i] = d
                    if h + 1 < M_HEADS:
                        st.store(mixd[h], ("mix", h), d)
                    else:
                        spilled[("mix", h)] = [q.dma(q.sem("ml_last_stored"), mixd[h], t[:], d, queue="sync")]
                    yield

                sq_free = [None, None]
                for _ in prepare(0):
                    pass
                for h in range(M_HEADS):
                    prep = [prepare(h + 1)] if h + 1 < M_HEADS else []
                    rest = [outputs(h)] + ([norm(h - 1)] if h else [])
                    while prep or rest:
                        step(prep)
                        step(prep)
                        step(rest)
                early = [q.last[e] for e in ("tensor", "vector", "scalar")]
                for _ in norm(M_HEADS - 1):
                    pass
                return st.all() + spilled[("mix", M_HEADS - 1)], early

        def layer_norm(name, write):
            with ExitStack() as sc:
                xc = sb(f"{name}_xc", [P, KT, S], F32, sc)
                sq = [sb(f"{name}_sq{i}", [P, HALF], F32, sc) for i in range(4)]
                pm = stat["pair"]
                pm.kept = False
                pv = take()
                sf, n, pm.read = [None] * 4, 0, []
                mean_done = [stat[("sum", 0)], stat[("sum", 1)]]
                for h in range(2):
                    c = slice(h * HALF, (h + 1) * HALF)
                    for k in range(KT):
                        xd = V(lambda e, k=k, h=h, c=c: e.tensor_tensor(xc[:, k, c], x[:, k, c], pm.half[h], ALU.subtract),
                               mean_done[h], x_ready[k])
                        i = n % 4
                        n += 1
                        sd = A(lambda e, k=k, i=i, c=c: e.activation(sq[i][:], xc[:, k, c], ACT.Square), xd, sf[i])
                        sf[i] = T(lambda e, k=k, h=h, i=i: e.matmul(pv.half[h], mean1024, sq[i][:], start=(k == 0),
                                                                   stop=(k == KT - 1)), sd, pv.read)
                    pm.read.append(xd)
                    stat[("sum", h)] = sf[i]

                def put(h, r, rd):
                    c = slice(h * HALF, (h + 1) * HALF)
                    later = []
                    for k in range(KT):
                        later.append(write(k, h, c, xc[:, k, c], r, rd))
                        if len(later) > 2:
                            later.pop(0)()
                    for f in later:
                        f()

                halves(pv, name, eps[:, 1:2], sc, put)

        def block2(l):
            q.stage(f"proj2_{l}")
            q.fence()
            mo = l * N_ADA2 * KT
            c1 = V(lambda e: e.tensor_scalar(cols[:, 24:32], mod2[:, mo + 8:mo + 16], 1.0, None, ALU.add),
                   [mod_done[(l + 1, i)] for i in range(3)])
            c2 = V(lambda e: e.tensor_scalar(cols[:, 32:40], mod2[:, mo + 16:mo + 24], 1.0, None, ALU.add))
            c3 = V(lambda e: e.tensor_scalar(cols[:, 16:17], vc("q_gain_2", l), A_DIM ** -0.5, None, ALU.mult))
            with ExitStack() as hs:
                h = [sb(f"h2{l}_hi", [P, KT, S], F32R, hs), sb(f"h2{l}_lo", [P, KT, S], F32R, hs)]

                rr = {}

                def write(k, hf, c, xc, r, rd):
                    td = V(lambda e: e.scalar_tensor_tensor(out=xc, in0=xc, scalar=cols[:, 24 + k:25 + k], in1=r,
                                                            op0=ALU.mult, op1=ALU.mult), rd, c1)
                    low = split_shifted(xc, mod2[:, mo + k:mo + k + 1], h[0][:, k, c], h[1][:, k, c], td)

                    def last_step():
                        rr[(k, hf)] = low()
                    return last_step

                layer_norm(f"ln{l}", write)
                ready = [(rr[(k, 0)], rr[(k, 1)]) for k in range(KT)]
                q.fence()
                hi, lo = (lambda k: h[0][:, k, :]), (lambda k: h[1][:, k, :])
                with ExitStack() as sc:
                    cst = sb(f"r2cos{l}", [P, S], F32, sc)
                    snt = sb(f"r2sin{l}", [P, S], F32, sc)
                    m2 = sb(f"r2mats{l}", [P, 2 * P], F32, sc)
                    s_t = q.sem(f"rope2_loaded{l}")
                    q.dma(s_t, cst[:], ins["rope2"][0])
                    q.dma(s_t, snt[:], ins["rope2"][1])
                    q.dma(s_t, m2[:, 0:P], ins["mats"][MAT["mean64"]])
                    tables = q.dma(s_t, m2[:, P:2 * P], ins["mats"][MAT["rot2"]])
                    his, los = Store(f"p2{l}_hi", 2, sc, F32R), Store(f"p2{l}_lo", 2, sc, F32R)
                    tmps = [[sb(f"p2{l}_{n}{i}", [P, S], F32, sc)[:] for n in ("raw", "sq", "u")] + [None]
                            for i in range(2)]
                    pending = []
                    for b in range(3):
                        blk = get(("in2", l, b))
                        both = gemm_pair(blk, hi, lo, ready) if b == 0 else None
                        for m in range(2):
                            nt = 2 * b + m
                            p, mm = both[m] if both else gemm(blk, m, KT, hi, lo, ready)
                            step(pending)
                            if nt < 5:
                                gc = cols[:, 16:17] if nt < 4 else vc("k_gain_2", l)
                                pending.append(rope_heads(his, los, tmps[nt % 2], m2[:, 0:P], m2[:, P:2 * P], cst[:], snt[:],
                                                          gc, nt, [tables, c3], p, mm))
                                next(pending[-1])
                            else:
                                raw = tmps[nt % 2][0]
                                d = A(lambda e, p=p, raw=raw: e.activation(raw, p.full, ACT.Identity), mm, tmps[nt % 2][3])
                                p.read = [d]
                                pv = take()
                                for j in range(ST):
                                    mt = T(lambda e, j=j, pv=pv, raw=raw: e.transpose(
                                        pv.full[:, j * P:(j + 1) * P], raw[:, j * P:(j + 1) * P], ident), d, pv.read)

                                def view(t, part):
                                    t4 = t[:].rearrange("p (a h d) -> p a h d", a=ST, h=2)
                                    v4 = vsp[0].rearrange("p (a h) d -> p a h d", h=4)
                                    return [(v4[:, :, hd, 64 * part:64 * part + 64], t4[:, :, hd, :]) for hd in range(2)]
                                pv.read = [split_out(pv.full, his, los, None, None, ("v2", l), mt, view=view)]
                    while pending:
                        step(pending)
                    done = his.all() + los.all()
                    spilled[("v", 0)] = spilled[("v", 1)] = spilled[("v2", l)]
                q.fence(done)
                with ExitStack() as sc:
                    st = Store(f"p2b{l}_o", 4, sc)
                    cu = sb(f"cu{l}", [P, S], F32, sc)
                    uu = sb(f"cuu{l}", [P, S], F32, sc)
                    ac = sb(f"cac{l}", [P, S], F32, sc)
                    conv_free = None
                    table = fourier_table(l)
                    next(table)
                    for b in range(3, 11):
                        blk = get(("in2", l, b))
                        for m in range(2):
                            nt = 2 * b + m
                            p, mm = gemm(blk, m, KT, hi, lo, ready)
                            if nt < 14:
                                t, fr = st.next()
                                fn = ACT.Identity if nt < 8 else ACT.Silu
                                d = A(lambda e, p=p, t=t, fn=fn: e.activation(t[:], p.full, fn), mm, fr)
                                p.read = [d]
                                st.store(proj[nt], ("proj", nt), d)
                                if nt == 8:
                                    ab = next(table)
                                continue
                            what, tile = (nt - 14) % 4, (nt - 14) // 4

                            def w(j, tile=tile):
                                return vc("conv_w", (l * 3 + j) * 2 + tile)
                            if what == 0:
                                v0 = A(lambda e, p=p: e.activation(cu[:], p.full, ACT.Identity), mm, conv_free)
                                p.read = [v0]
                            elif what == 1:
                                v1_ = V(lambda e, p=p: e.tensor_tensor(uu[:], cu[:], p.full, ALU.mult), v0, mm)
                                p.read = [v1_]
                                v2 = V(lambda e, w=w: e.tensor_scalar(ac[:], uu[:], w(1), None, ALU.mult), v1_)
                                v3 = V(lambda e, w=w: e.scalar_tensor_tensor(out=ac[:, 1:S], in0=uu[:, 0:S - 1], scalar=w(0),
                                                                             in1=ac[:, 1:S], op0=ALU.mult, op1=ALU.add), v2)
                                v4 = V(lambda e, w=w: e.scalar_tensor_tensor(out=ac[:, 0:S - 1], in0=uu[:, 1:S], scalar=w(2),
                                                                             in1=ac[:, 0:S - 1], op0=ALU.mult, op1=ALU.add),
                                       v3)
                            elif what == 2:
                                v5 = V(lambda e, p=p: e.tensor_tensor(ac[:], ac[:], p.full, ALU.mult), v4, mm)
                                p.read = [v5]
                            else:
                                v6 = A(lambda e, p=p: e.activation(cu[:], p.full, ACT.Silu), mm, v1_)
                                p.read = [v6]
                                t, fr = st.next()
                                conv_free = V(lambda e, t=t: e.tensor_tensor(t[:], ac[:], cu[:], ALU.mult), v5, v6, fr)
                                st.store(mixd[4 + tile], ("mix", 4 + tile), conv_free)
                    done = st.all()
            h_read = [q.last["tensor"]]
            q.fence(done)
            with ExitStack() as ma:
                mixa = [sb(f"mix2a{l}_hi", [P, 4, S], F32R, ma), sb(f"mix2a{l}_lo", [P, 4, S], F32R, ma)]
                ra, qk_read = attention(f"attn2_{l}", lambda hq: hq // 4, 4, None, 10, mixa, h_read,
                                        lambda load_next: q.fence(fourier(l, ab, load_next, h_read)))
                q.stage(f"out2_{l}")
                mixt = load_mix(f"mix2{l}", ma, 4, qk_read)
                q.fence()
                mixb = [sb(f"mix2b{l}_hi", [P, 4, S], F32R, ma), sb(f"mix2b{l}_lo", [P, 4, S], F32R, ma)]
                rb = mixt(mixb)
                ssum = sb(f"mix2{l}_sum", [P, S], F32, ma)
                xa = [V(lambda e, k=k: e.tensor_scalar(x[:, k, :], x[:, k, :], ALPHA, None, ALU.mult)) for k in range(KT)]
                for c in range(4):
                    blk = get(("out2", l, c))
                    for m in range(2):
                        d = 2 * c + m
                        p, mm = gemm(blk, m, KT, lambda k: (mixa if k < 4 else mixb)[0][:, k % 4, :],
                                     lambda k: (mixa if k < 4 else mixb)[1][:, k % 4, :], ra + rb,
                                     order=[0, 1, 2, 4, 5, 6, 7, 3])
                        x_ready[d] = V(lambda e, p=p, d=d: e.scalar_tensor_tensor(
                            out=x[:, d, :], in0=p.full, scalar=cols[:, 32 + d:33 + d], in1=x[:, d, :],
                            op0=ALU.mult, op1=ALU.add), mm, xa[d], c2)
                        p.read = [x_ready[d]]
                        stat_add(d, ssum, False)
                stat_total(ssum)
            q.fence()

            def write(k, hf, c, xc, r, rd):
                td = V(lambda e: e.tensor_tensor(xc, xc, r, ALU.mult), rd)

                def last_step():
                    x_parts[(k, hf)] = A(lambda e: e.activation(x[:, k, c], xc, ACT.Identity, scale=vc("ln_g", l * 8 + k),
                                                                bias=vc("ln_b", l * 8 + k)), td)
                return last_step
            x_parts = {}
            layer_norm(f"lno{l}", write)
            for k in range(KT):
                x_ready[k] = [x_parts[(k, 0)], x_parts[(k, 1)]]
            if l == 0:
                stat_all(False)

        def fourier_table(l):
            cm, ab = sqh[0], sqh[1]
            s_c = q.sem(f"fo{l}_consts")
            for j, n in enumerate(("cosc", "sinc", f"fm{l}0", f"fm{l}1")):
                cin = q.dma(s_c, cm[:, j * P:(j + 1) * P], ins["mats"][MAT[n]])
            yield
            p = take()
            for g in range(2):
                for j in range(2):
                    mm = T(lambda e, g=g, j=j, p=p: e.matmul(p.half[g][:, j * P:(j + 1) * P], cm[:, j * P:(j + 1) * P],
                                                            cm[:, (2 + g) * P:(3 + g) * P], start=True, stop=True),
                           cin, p.read)
            d = A(lambda e, p=p: e.activation(ab[:].rearrange("p (g c) -> p g c", g=2),
                                              p.full.rearrange("p (g c) -> p g c", g=2)[:, :, 0:256], ACT.Identity), mm)
            p.read = [d]
            yield ab[:].rearrange("p (g c) -> p g c", g=2), d

        def fourier(l, table, load_next, h_read):
            q.stage(f"fourier{l}")
            with ExitStack() as sc:
                ab, abd = table
                fu = sb(f"fo{l}_u", [P, 2, S], F32, sc)
                gf = sb(f"fo{l}_g", [P, 2, S], F32, sc)
                uh = sb(f"fo{l}_uhi", [P, 2, ST, 256], F32R, sc)
                ul = sb(f"fo{l}_ulo", [P, 2, ST, 256], F32R, sc)
                o = fu
                s_u, s_g = [q.sem(f"fo{l}_uload{j}") for j in range(2)], q.sem(f"fo{l}_gload")
                u_in = [q.first(s_u[j], fu[:, j, :], proj[6 + j], spilled[("proj", 6 + j)], early=h_read)
                        for j in range(2)]
                for j in range(2):
                    g_in = q.first(s_g, gf[:, j, :], proj[8 + j], spilled[("proj", 8 + j)])
                load_next()
                ud = []
                for g in range(2):
                    for t0 in (0, 4):
                        p = take()
                        for j in range(4):
                            mm = T(lambda e, g=g, j=j, p=p, t0=t0: e.matmul(
                                p.full[:, j * 256:(j + 1) * 256], fu[:, g, (t0 + j) * P:(t0 + j + 1) * P], ab[:, g, :],
                                start=True, stop=True), abd, u_in[g], p.read)
                        hi = uh[:, g, t0:t0 + 4, :].rearrange("p a b -> p (a b)")
                        lo = ul[:, g, t0:t0 + 4, :].rearrange("p a b -> p (a b)")
                        up = A(lambda e, p=p, hi=hi: e.activation(hi, p.full, ACT.Identity), mm)
                        dn = V(lambda e, p=p, hi=hi, lo=lo: e.tensor_tensor(lo, p.full, hi.bitcast(F32), ALU.subtract), up)
                        p.read = [dn]
                        ud.append(dn)
                for c in range(4):
                    p = None
                    for tb in range(2):
                        s, whi, wlo, wdone = get(("dft", l, c, tb))
                        if p is None:
                            p = take()
                        for g in range(2):
                            for k in range(ST):
                                for i, (a, b) in enumerate(((whi, uh), (whi, ul), (wlo, uh))):
                                    mm = T(lambda e, a=a, b=b, k=k, g=g, tb=tb, i=i, p=p: e.matmul(
                                        p.half[g][:, 0:256], b[:, g, k, tb * P:(tb + 1) * P], a[:, k * 256:(k + 1) * 256],
                                        start=(tb == 0 and k == 0 and i == 0), stop=(tb == 1 and k == ST - 1 and i == 2)),
                                        wdone, ud, p.read if tb == 0 else None)
                        W.used(s, mm)
                    res = p.full.rearrange("p (g c) -> p g c", g=2)[:, :, 0:256]
                    d = V(lambda e, res=res, c=c: e.tensor_tensor(o[:, :, c * 256:(c + 1) * 256], res,
                                                                  gf[:, :, c * 256:(c + 1) * 256], ALU.mult), mm, g_in)
                    p.read = [d]
                s_o = q.sem(f"fo{l}_stored")
                a1 = q.dma(s_o, mixd[6], o[:, 0, :], d)
                a2 = q.dma(s_o, mixd[7], o[:, 1, :])
                spilled[("mix", 6)] = spilled[("mix", 7)] = [a2]
                return [a2]

        def finish():
            s_out = q.sem("out_stored")
            for k in range(KT):
                fin = q.dma(s_out, out[:, k, :], x[:, k, :], x_ready[k], queue="sync")
            return fin

        def final_norm():
            q.stage("final1")
            q.fence()
            with ExitStack() as sc:
                parts = {}

                def write(h, r, rd):
                    c = slice(h * HALF, (h + 1) * HALF)
                    for k in range(KT):
                        parts[(k, h)] = V(lambda e, k=k: e.scalar_tensor_tensor(
                            out=x[:, k, c], in0=x[:, k, c], scalar=vc("g_final", k), in1=r, op0=ALU.mult, op1=ALU.mult), rd)

                halves(stat["pair"], "fin", eps[:, 0:1], sc, write)
                for k in range(KT):
                    x_ready[k] = [parts[(k, 0)], parts[(k, 1)]]
            stat_all(False)

        stages = [("ffn1", lambda: ffn(1, 2)), ("mixer1", mixer1), ("ffn2", lambda: ffn(2, 8)), ("final", final_norm),
                  ("b0", lambda: block2(0)), ("b1", lambda: block2(1))]
        for name, run in stages:
            run()
            if name == "ffn2":
                while W.taken < len(plan) and plan[W.taken][0] == "ada":
                    W.advance()
                    ada_finish()
            if name == stop:
                break
        q.end = finish()
        q.emit(ctx.enter_context(nc.Block()))



def tiles(w, width=256, cols=None):
    if cols is not None:
        w = np.concatenate([w, np.zeros((w.shape[0], 1), w.dtype)], 1)[:, cols]
    k, n = w.shape
    return np.ascontiguousarray(w.reshape(k // P, P, n // width, width).transpose(2, 1, 0, 3)
                                .reshape(n // width, P, -1))


def shape_constants():
    f = np.float32
    m = {}
    m["mean1024"] = np.full((P, P), 1 / 1024, f)
    blk = np.kron(np.eye(2), np.ones((64, 64)))
    m["mean64"] = (blk / 64).astype(f)
    m["ones"] = np.ones((P, P), f)
    m["ident"] = np.eye(P, dtype=f)
    r1 = np.zeros((64, 64), f)
    for d in range(8):
        r1[d + 8, d] = -1.0
        r1[d, d + 8] = 1.0
    m["rot1"] = np.kron(np.eye(2), r1).astype(f)
    r2 = np.zeros((64, 64), f)
    for h in (0, 32):
        for d in range(16):
            r2[h + d + 16, h + d] = -1.0
            r2[h + d, h + d + 16] = 1.0
    m["rot2"] = np.kron(np.eye(2), r2).astype(f)
    ang = 2 * np.pi * np.outer(np.arange(64), np.arange(64)) / 64
    m["cosc"] = np.kron(np.eye(2), np.cos(ang)).astype(f)
    m["sinc"] = np.kron(np.eye(2), np.sin(ang)).astype(f)
    i = np.arange(P)
    m["causal"] = np.where(i[:, None] <= i[None, :], 0.0, NEG).astype(f)
    m["anti"] = np.where(i[:, None] >= i[None, :], 0.0, NEG).astype(f)
    t = 2 * np.pi * (np.outer(np.arange(S), np.arange(S)) % S) / S
    dft = np.stack([np.cos(t) / 256, -np.sin(t) / 256]).astype(f).reshape(2, KT, P, S)
    inv1 = (f(500000.0) ** (f(-2.0) * np.arange(8, dtype=f) / f(16))).astype(f)
    a1 = (np.arange(S, dtype=f)[:, None] * inv1[None, :]).astype(f)
    c1, s1 = np.ones((64, S), f), np.zeros((64, S), f)
    for d in range(16):
        c1[d], s1[d] = np.cos(a1[:, d % 8]), np.sin(a1[:, d % 8])
    inv2 = (f(1.0) / (f(10000.0) ** (np.arange(0, 32, 2, dtype=f) / f(32)))).astype(f)
    row = np.repeat(np.arange(S // 64, dtype=f), 64)[:, None] * inv2
    col = np.tile(np.arange(64, dtype=f), S // 64)[:, None] * inv2
    c2, s2 = np.zeros((64, S), f), np.zeros((64, S), f)
    for d in range(64):
        a = (row if d < 32 else col)[:, d % 16]
        c2[d], s2[d] = np.cos(a), np.sin(a)
    rope1 = np.stack([np.tile(c1, (2, 1)), np.tile(s1, (2, 1))])
    rope2 = np.stack([np.tile(c2, (2, 1)), np.tile(s2, (2, 1))])
    j = np.abs(np.arange(1920)[None, :] - 896 - np.arange(P)[:, None])
    count = (j <= 64).astype(int) + ((j % 4 == 0) & (j <= 256)) + (j % 16 == 0)
    band = np.where(count > 0, np.log(np.maximum(count, 1)), NEG).astype(f)
    sel = np.zeros((36, 8, P), f)
    for d in range(2):
        for h in range(4):
            sel[32 * d + h, d * 4 + h] = 1.0
    reset = np.ones((36, S), f)
    reset[:, ::P] = 0.0
    return m, dft, rope1, rope2, band, sel.reshape(36, -1), reset


def layouts(i):
    a = {k: np.asarray(v) for k, v in i.items()}
    m, dft, rope1, rope2, band, sel, reset = shape_constants()
    for l in range(2):
        for g in range(2):
            z = np.zeros((P, P), np.float32)
            z[0:64, 0:64] = a["f_mix_2"][l, 2 * g]
            z[64:, 64:] = a["f_mix_2"][l, 2 * g + 1]
            m[f"fm{l}{g}"] = z
    vec = np.zeros((P, NVEC), np.float32)

    def put(name, v):
        o, n = VEC[name]
        vec[:, o:o + n] = v

    def colsof(v):
        return v.reshape(-1, P).T

    put("c", colsof(a["c"]))
    put("b_ada", colsof(a["b_ada"]))
    for n in ("g_ffn1", "g_mix", "g_ffn2", "g_final", "g_mh"):
        put(n, colsof(a[n]))
    put("g_q", np.tile(a["g_q"][0], 2)[:, None])
    put("g_k", np.tile(a["g_k"][0], 2)[:, None])
    put("c_2", colsof(a["c_2"]))
    put("b_ada_2", colsof(a["b_ada_2"]))
    put("q_gain_2", np.tile(a["q_gain_2"], (1, 2)).T)
    put("k_gain_2", np.tile(a["k_gain_2"], (1, 2)).T)
    put("conv_w", a["conv_w_2"].reshape(-1, P).T)
    put("ln_g", colsof(a["ln_g_2"]))
    put("ln_b", colsof(a["ln_b_2"]))
    gb = a["gate_bias"][0]
    o = VEC["gate_bias"][0]
    for r0, g in ((0, 0), (32, 2), (64, 1), (96, 3)):
        vec[r0:r0 + 4, o] = gb[g]

    w = a["w_in"][0]
    R = np.arange
    mq, mk, mv, mo, mg = R(0, 256), R(256, 512), R(512, 1024), R(1024, 1536), R(1536, 1552)
    aq, ak, av = R(1552, 2064), R(2064, 2576), R(2576, 3088)
    gate_cols = np.full(P, -1)
    for r0, g in ((0, 0), (32, 2), (64, 1), (96, 3)):
        gate_cols[r0:r0 + 4] = mg[4 * g:4 * g + 4]
    sizes = (512, 128, 128, 512, 256, 256, 256, 256, 256, 256)
    st = np.cumsum((0,) + sizes)
    Q, K, V_, GA, CU, CB, CC, GC, FU, GF = (R(st[n], st[n + 1]) for n in range(10))
    h = [slice(0, P), slice(P, 256)]
    order2 = np.concatenate([Q, K, V_, FU, GF, GA] + [x_[s_] for s_ in h for x_ in (CU, CC, CB, GC)])
    gu = []
    for n in (1, 2):
        g = a[f"w_gu{n}"][0].reshape(KT, P, 2, FF_TILES, P).transpose(3, 1, 0, 2, 4)
        gu.append(np.ascontiguousarray(g).reshape(FF_TILES, P, BLK))
    return {"in_" + n: v for n, v in {
        "xT": np.ascontiguousarray(a["x"][0].T.reshape(KT, P, S).transpose(1, 0, 2)),
        "vec": vec, "mats": np.stack([m[n] for n in MATS]), "dft": dft, "rope1": rope1, "rope2": rope2,
        "band": band, "sel": sel, "reset": reset,
        "w_ada": a["w_ada"][0], "w_ada_2": a["w_ada_2"],
        "w_gu1": gu[0], "w_gu2": gu[1],
        "w_down1": a["w_down1"][0].reshape(FF_TILES, P, D), "w_down2": a["w_down2"][0].reshape(FF_TILES, P, D),
        "w_in": tiles(w, cols=np.concatenate([aq, ak, av, mv, mq, mk, mo])),
        "w_in_gate": tiles(w, P, gate_cols)[0],
        "w_out": a["w_out"][0].reshape(KT, P, D),
        "w_in_2": np.stack([tiles(a["w_in_2"][l], cols=order2) for l in range(2)]),
        "w_out_2": a["w_out_2"].reshape(2, KT, P, D),
    }.items()}


def program(nc, arrays, stop=None):
    ins = {}
    for n, v in arrays.items():
        ins[n[3:]] = nc.dram_tensor(n, list(v.shape), mybir.dt.from_np(v.dtype), kind="ExternalInput").ap()
    out = nc.dram_tensor("out", [P, KT, S], F32, kind="ExternalOutput").ap()
    build(nc, ins, out, stop)


def kernel(**inputs):
    import concourse.bacc as bacc
    from concourse.bass_utils import run_bass_kernel_spmd

    arrays = layouts(inputs)
    nc = bacc.Bacc("TRN2", target_bir_lowering=False, num_devices=1)
    program(nc, arrays)
    res = run_bass_kernel_spmd(nc, [arrays], core_ids=[0])
    y = np.asarray(res.results[0]["out"])
    return np.ascontiguousarray(y.transpose(1, 0, 2).reshape(D, S).T)[None]
```
